# Optimizing a Trainium2 kernel written in Bass

```python
import jax, jax.numpy as jnp
from jax import lax
import numpy as np

D_MODEL = 1024
BATCH = 1
SEQ = 128
DEPTH = 2
DEC_BATCH = 1
DEC_SEQ = 512
PAST_LEN = 128

GRID_W = 64
N_MIXERS = 3
N_A = len(range(0, DEPTH, N_MIXERS))
N_B = len(range(1, DEPTH, N_MIXERS))
N_C = len(range(2, DEPTH, N_MIXERS))
N_MOD = 6
EPS = 1e-6
D_RNN = D_MODEL
RNN_BLOCKS = 16
RNN_BLOCK = D_RNN // RNN_BLOCKS
CONV_W = 4
CONV_LEFT = 2
LRU_C = 8.0
N_HEADS = 16
N_KV = 4
HEAD_DIM = 64
GQA_G = N_HEADS // N_KV
WINDOW = 128
BLOCK = 128
ROPE_BASE = 10000.0
FOURIER_GROUPS = 4
FOURIER_GW = D_MODEL // FOURIER_GROUPS
N_EXPERTS = 16
EXPERT_FF = 1024
EC_FACTOR = 2
F32 = jnp.float32

kernel_name = 'hybrid_flow_rglru_swa_fnet_ecmoe_step'

def _rmsnorm(x, g):
    x32 = x.astype(F32)
    y = x32 * lax.rsqrt(jnp.mean(x32 * x32, axis=-1, keepdims=True) + EPS)
    return (y * g.astype(F32)).astype(x.dtype)

def _modulate(x, g, shift, scale):
    return _rmsnorm(x, g) * (1.0 + scale[:, None, :]) + shift[:, None, :]

def _centred_dwconv(u, w, b):
    S = u.shape[1]
    up = jnp.pad(u, ((0, 0), (CONV_LEFT, CONV_W - 1 - CONV_LEFT), (0, 0)))
    return sum(up[:, k:k + S] * w[k] for k in range(CONV_W)) + b

def _linear_scan(a, b, h0):
    def comb(x, y):
        return (x[0] * y[0], y[0] * x[1] + y[1])
    a_cum, b_cum = lax.associative_scan(comb, (a, b), axis=1)
    return a_cum * h0[:, None, :] + b_cum

def _rglru_coeffs(u, w_a, b_a, w_x, b_x, lam):
    B, S, _ = u.shape
    ub = u.reshape(B, S, RNN_BLOCKS, RNN_BLOCK)
    r = jax.nn.sigmoid(jnp.einsum('bshi,hij->bshj', ub, w_a.astype(F32)).reshape(B, S, D_RNN) + b_a.astype(F32))
    i = jax.nn.sigmoid(jnp.einsum('bshi,hij->bshj', ub, w_x.astype(F32)).reshape(B, S, D_RNN) + b_x.astype(F32))
    log_a = -LRU_C * r * jax.nn.softplus(-lam.astype(F32))
    return jnp.exp(log_a), jnp.sqrt(-jnp.expm1(2.0 * log_a)) * (i * u)

def _recurrent_mixer(xn, w_in, conv_w, conv_b, w_a, b_a, w_x, b_x, lam, w_out, h0_f, h0_b):
    gate, u = jnp.split(xn @ w_in, 2, axis=-1)
    u = _centred_dwconv(u, conv_w, conv_b).astype(F32)
    a_f, b_f = _rglru_coeffs(u, w_a[0], b_a[0], w_x[0], b_x[0], lam[0])
    h_f = _linear_scan(a_f, b_f, h0_f.astype(F32))
    a_b, b_b = _rglru_coeffs(jnp.flip(u, 1), w_a[1], b_a[1], w_x[1], b_x[1], lam[1])
    h_b = _linear_scan(a_b, b_b, h0_b.astype(F32))
    h = h_f + jnp.flip(h_b, 1)
    y = (h * jax.nn.gelu(gate.astype(F32))).astype(xn.dtype) @ w_out
    final = jnp.stack([h_f[:, -1], h_b[:, -1]], axis=1)
    return y, final

def _qkv(xn, w_qkv, q_g, k_g):
    B, S, _ = xn.shape
    nq, nk = N_HEADS * HEAD_DIM, N_KV * HEAD_DIM
    qkv = xn @ w_qkv
    q = qkv[..., :nq].reshape(B, S, N_HEADS, HEAD_DIM)
    k = qkv[..., nq:nq + nk].reshape(B, S, N_KV, HEAD_DIM)
    v = qkv[..., nq + nk:].reshape(B, S, N_KV, HEAD_DIM)
    return _rmsnorm(q, q_g), _rmsnorm(k, k_g), v

def _rope2d(x):
    S = x.shape[1]
    n_rows = S // GRID_W
    row = jnp.repeat(jnp.arange(n_rows), GRID_W).astype(F32)
    col = jnp.tile(jnp.arange(GRID_W), n_rows).astype(F32)
    n_freq = HEAD_DIM // 4
    inv = ROPE_BASE ** (-jnp.arange(n_freq, dtype=F32) / n_freq)
    ar, ac = row[:, None] * inv, col[:, None] * inv
    ang = jnp.concatenate([ar, ar, ac, ac], axis=-1)[None, :, None, :]
    x32 = x.astype(F32)
    x1, x2, x3, x4 = jnp.split(x32, 4, axis=-1)
    rot = jnp.concatenate([-x2, x1, -x4, x3], axis=-1)
    return (x32 * jnp.cos(ang) + rot * jnp.sin(ang)).astype(x.dtype)

def _attend(q, ks, vs, masks, sink):
    logits = []
    for k, m in zip(ks, masks):
        l = jnp.einsum('bqkgd,bskd->bkgqs', q, k, preferred_element_type=F32)
        if m is not None:
            l = jnp.where(m, l, -jnp.inf)
        logits.append(l)
    s = sink[None, :, :, None, None]
    mx = s
    for l in logits:
        mx = jnp.maximum(mx, jnp.max(l, axis=-1, keepdims=True))
    den = jnp.exp(s - mx)
    out = 0.0
    for l, v in zip(logits, vs):
        p = jnp.exp(l - mx)
        den = den + jnp.sum(p, axis=-1, keepdims=True)
        out = out + jnp.einsum('bkgqs,bskd->bqkgd', p.astype(v.dtype), v, preferred_element_type=F32)
    den = jnp.transpose(den, (0, 3, 1, 2, 4))
    return (out / den).astype(q.dtype)

def _context_attention(q, k, v, sink):
    B, L = q.shape[:2]
    nb = L // BLOCK
    qb = jnp.moveaxis(q.reshape(B, nb, BLOCK, N_KV, GQA_G, HEAD_DIM), 1, 0)
    ob = lax.map(lambda qq: _attend(qq, [k], [v], [None], sink), qb)
    return jnp.moveaxis(ob, 0, 1).reshape(B, L, N_HEADS * HEAD_DIM)

def _latent_attention(q, k, v, k_ctx, v_ctx, sink):
    B, S = q.shape[:2]
    nb = S // BLOCK
    span = BLOCK + 2 * WINDOW
    kp = jnp.pad(k, ((0, 0), (WINDOW, WINDOW), (0, 0), (0, 0)))
    vp = jnp.pad(v, ((0, 0), (WINDOW, WINDOW), (0, 0), (0, 0)))
    qb = jnp.moveaxis(q.reshape(B, nb, BLOCK, N_KV, GQA_G, HEAD_DIM), 1, 0)

    def blk(args):
        j, qq = args
        start = j * BLOCK
        kk = lax.dynamic_slice_in_dim(kp, start, span, axis=1)
        vv = lax.dynamic_slice_in_dim(vp, start, span, axis=1)
        qpos = start + jnp.arange(BLOCK)
        kpos = start - WINDOW + jnp.arange(span)
        mask = (kpos[None, :] >= 0) & (kpos[None, :] < S) & (jnp.abs(qpos[:, None] - kpos[None, :]) <= WINDOW)
        return _attend(qq, [kk, k_ctx], [vv, v_ctx], [mask, None], sink)

    ob = lax.map(blk, (jnp.arange(nb), qb))
    return jnp.moveaxis(ob, 0, 1).reshape(B, S, N_HEADS * HEAD_DIM)

def _fourier_mixer(xn, w_f):
    B, S, D = xn.shape
    xg = xn.astype(F32).reshape(B, S, FOURIER_GROUPS, FOURIER_GW)
    f = jnp.fft.fft2(xg, axes=(1, 3), norm='ortho').real
    return f.reshape(B, S, D).astype(xn.dtype) @ w_f

def _expert_choice_moe(xn, w_router, w_gate, w_up, w_down):
    B, S, D = xn.shape
    n_tok = B * S
    cap = EC_FACTOR * n_tok // N_EXPERTS
    xt = xn.reshape(n_tok, D)
    aff = jax.nn.softmax(jnp.dot(xt, w_router, preferred_element_type=F32), axis=-1)
    g, idx = lax.top_k(aff.T, cap)
    xe = xt[idx]
    h = jax.nn.silu(jnp.einsum('ecd,edf->ecf', xe, w_gate)) * jnp.einsum('ecd,edf->ecf', xe, w_up)
    ye = jnp.einsum('ecf,efd->ecd', h, w_down) * g[..., None].astype(xn.dtype)
    out = jnp.zeros_like(xt).at[idx.reshape(-1)].add(ye.reshape(-1, D))
    return out.reshape(B, S, D)

def setup_inputs(seed: int = 0) -> dict:
    key = jax.random.key(seed)
    keys = iter(jax.random.split(key, 40))

    def nrm(shape, scale):
        return jax.random.normal(next(keys), shape, F32) * scale

    D = D_MODEL
    u = jax.random.uniform(next(keys), (N_A, 2, D_RNN), F32, 0.9, 0.999)
    a_base = u ** (1.0 / LRU_C)
    return {
        'x_prompt': nrm((BATCH, SEQ, D), 1.0),
        'x_sample': nrm((DEC_BATCH, DEC_SEQ, D), 1.0),
        'state_rglru': nrm((DEC_BATCH, N_A, 2, D_RNN), 0.5),
        'cache_k': nrm((DEC_BATCH, N_B, PAST_LEN, N_KV, HEAD_DIM), 1.0),
        'cache_v': nrm((DEC_BATCH, N_B, PAST_LEN, N_KV, HEAD_DIM), 1.0),
        'c': nrm((DEC_BATCH, D), 1.0),
        'c_ctx': nrm((D,), 1.0),
        'mod_w': nrm((DEPTH, D, N_MOD * D), 0.5 * D ** -0.5),
        'mod_b': nrm((DEPTH, N_MOD * D), 0.01),
        'norm1_g': 1.0 + nrm((DEPTH, D), 0.05),
        'norm2_g': 1.0 + nrm((DEPTH, D), 0.05),
        'rg_w_in': nrm((N_A, D, 2 * D_RNN), D ** -0.5),
        'rg_conv_w': nrm((N_A, CONV_W, D_RNN), CONV_W ** -0.5),
        'rg_conv_b': nrm((N_A, D_RNN), 0.01),
        'rg_w_a': nrm((N_A, 2, RNN_BLOCKS, RNN_BLOCK, RNN_BLOCK), RNN_BLOCK ** -0.5),
        'rg_b_a': nrm((N_A, 2, D_RNN), 0.01),
        'rg_w_x': nrm((N_A, 2, RNN_BLOCKS, RNN_BLOCK, RNN_BLOCK), RNN_BLOCK ** -0.5),
        'rg_b_x': nrm((N_A, 2, D_RNN), 0.01),
        'rg_lambda': jnp.log(a_base) - jnp.log1p(-a_base),
        'rg_w_out': nrm((N_A, D_RNN, D), D_RNN ** -0.5),
        'at_w_qkv': nrm((N_B, D, (N_HEADS + 2 * N_KV) * HEAD_DIM), D ** -0.5),
        'at_q_norm': 1.0 + nrm((N_B, HEAD_DIM), 0.05),
        'at_k_norm': 1.0 + nrm((N_B, HEAD_DIM), 0.05),
        'at_sink': nrm((N_B, N_HEADS), 0.5),
        'at_w_o': nrm((N_B, N_HEADS * HEAD_DIM, D), (N_HEADS * HEAD_DIM) ** -0.5),
        'ft_w': nrm((N_C, D, D), D ** -0.5),
        'moe_router': nrm((DEPTH, D, N_EXPERTS), D ** -0.5),
        'moe_w_gate': nrm((DEPTH, N_EXPERTS, D, EXPERT_FF), D ** -0.5),
        'moe_w_up': nrm((DEPTH, N_EXPERTS, D, EXPERT_FF), D ** -0.5),
        'moe_w_down': nrm((DEPTH, N_EXPERTS, EXPERT_FF, D), EXPERT_FF ** -0.5),
    }

def reference(x_prompt, x_sample, state_rglru, cache_k, cache_v, c, c_ctx,
              mod_w, mod_b, norm1_g, norm2_g,
              rg_w_in, rg_conv_w, rg_conv_b, rg_w_a, rg_b_a, rg_w_x, rg_b_x, rg_lambda, rg_w_out,
              at_w_qkv, at_q_norm, at_k_norm, at_sink, at_w_o,
              ft_w, moe_router, moe_w_gate, moe_w_up, moe_w_down):
    q_scale = HEAD_DIM ** -0.5
    cond_ctx = jax.nn.silu(c_ctx)[None, :]
    cond_lat = jax.nn.silu(c)
    xp, xs = x_prompt, x_sample
    new_rg, new_k, new_v = [], [], []
    for layer in range(DEPTH):
        kind, j = layer % N_MIXERS, layer // N_MIXERS
        mp = jnp.split(cond_ctx @ mod_w[layer] + mod_b[layer], N_MOD, axis=-1)
        ms = jnp.split(cond_lat @ mod_w[layer] + mod_b[layer], N_MOD, axis=-1)
        hp = _modulate(xp, norm1_g[layer], mp[0], mp[1])
        hs = _modulate(xs, norm1_g[layer], ms[0], ms[1])
        if kind == 0:
            rg = (rg_w_in[j], rg_conv_w[j], rg_conv_b[j], rg_w_a[j], rg_b_a[j],
                  rg_w_x[j], rg_b_x[j], rg_lambda[j], rg_w_out[j])
            h0 = jnp.zeros((xp.shape[0], D_RNN), F32)
            yp, st = _recurrent_mixer(hp, *rg, h0, h0)
            ys, _ = _recurrent_mixer(hs, *rg, state_rglru[:, j, 0], state_rglru[:, j, 1])
            new_rg.append(st)
        elif kind == 1:
            sink = at_sink[j].astype(F32).reshape(N_KV, GQA_G)
            qp, kp, vp = _qkv(hp, at_w_qkv[j], at_q_norm[j], at_k_norm[j])
            yp = _context_attention(qp * q_scale, kp, vp, sink) @ at_w_o[j]
            qs, ks, vs = _qkv(hs, at_w_qkv[j], at_q_norm[j], at_k_norm[j])
            ys = _latent_attention(_rope2d(qs) * q_scale, _rope2d(ks), vs,
                                   cache_k[:, j], cache_v[:, j], sink) @ at_w_o[j]
            new_k.append(kp)
            new_v.append(vp)
        else:
            yp = _fourier_mixer(hp, ft_w[j])
            ys = _fourier_mixer(hs, ft_w[j])
        xp = xp + mp[2][:, None, :] * yp
        xs = xs + ms[2][:, None, :] * ys
        moe = (moe_router[layer], moe_w_gate[layer], moe_w_up[layer], moe_w_down[layer])
        xp = xp + mp[5][:, None, :] * _expert_choice_moe(_modulate(xp, norm2_g[layer], mp[3], mp[4]), *moe)
        xs = xs + ms[5][:, None, :] * _expert_choice_moe(_modulate(xs, norm2_g[layer], ms[3], ms[4]), *moe)
    return (xp, xs, jnp.stack(new_rg, axis=1), jnp.stack(new_k, axis=1), jnp.stack(new_v, axis=1))


_drawn_inputs = setup_inputs


def setup_inputs(seed=0):
    import zlib

    import numpy as np

    out = dict(_drawn_inputs(seed))
    spreads = {}
    factors = {'cache_k': 4.786,
     'cache_v': 3.702,
     'norm2_g': 4.346,
     'rg_b_a': 8.0,
     'rg_b_x': 8.0,
     'at_q_norm': 8.0,
     'at_sink': 64.0}
    for name, (base, spread) in spreads.items():
        noise = np.random.default_rng([zlib.crc32(name.encode()), seed]).standard_normal(out[name].shape)
        drawn = base * np.exp(spread * noise) if base else spread * noise
        out[name] = __import__('jax').numpy.asarray(drawn.astype(out[name].dtype))
    for name, factor in factors.items():
        out[name] = (out[name] * factor).astype(out[name].dtype)
    return out
```

```python
from contextlib import ExitStack

import numpy as np

import concourse.bass as bass
from concourse import mybir

F32 = mybir.dt.float32
U32 = mybir.dt.uint32
ALU = mybir.AluOpType
ACT = mybir.ActivationFunctionType
AX = mybir.AxisListType

P = 128
D = 1024
KB = D // P
NLAT, NCTX = 512, 128
NTOK = NLAT + NCTX
TL = NLAT // P
NT = NTOK // P
NMOD = 6
EPS = 1e-6
NB = 16
RB = D // NB
NH, NKV, HD = 16, 4, 64
NQK = NH + NKV
QKV = (NH + 2 * NKV) * HD
NE = 16
CL, CC = 2 * NLAT // NE, 2 * NCTX // NE
CE = CL + CC
NEG = -1e30

SLOTS = 12
ROUND_MOD0A, ROUND_RG, ROUND_MOD, ROUND_MOE0 = 0, 1, 2, 5
ROUND_AT, ROUND_MOE1 = ROUND_MOE0 + NE, ROUND_MOE0 + NE + 1
MOD_BANKS = (6, 7, 2)
MOE_ROUND = (ROUND_MOE0, ROUND_MOE1)

R_C, R_CCTX, R_G1, R_G2, R_CW, R_CB, R_BA, R_BX, R_LAM, R_H0, R_MODB = 0, 1, 2, 4, 6, 10, 11, 13, 15, 17, 19
NROWS = R_MODB + 2 * NMOD
UPAD = 2 + NLAT + 2 + NCTX + 1
UC = NLAT + 2 + NCTX
C0 = NLAT + 2


def build(nc, x_all, state, cache_k, cache_v, c, c_ctx, mod_w, mod_b, norm1_g, norm2_g,
          rg_w_in, rg_conv_w, rg_conv_b, rg_w_a, rg_b_a, rg_w_x, rg_b_x, rg_lambda, rg_w_out,
          at_w_qkv, at_q_norm, at_k_norm, at_sink, at_w_o, moe_router, moe_w_gate, moe_w_up,
          moe_w_down, rope, y_all, new_state, new_k, new_v):
    with ExitStack() as ctx:
        def sb(name, shape, dt=F32):
            return ctx.enter_context(nc.sbuf_tensor(name, shape, dt))

        def sem(name):
            return ctx.enter_context(nc.semaphore(name))

        x_mid = nc.dram_tensor("x_mid", (NTOK, D), F32, kind="Internal").ap()
        x_hat = [nc.dram_tensor(f"x_hat{l}", (NTOK, D), F32, kind="Internal").ap() for l in range(2)]
        x_res = (x_mid, y_all)

        ps = ctx.enter_context(nc.psum_tensor("ps", [P, 8, 512], F32))
        ring = sb("ring", [P, SLOTS, 2 * D])
        r1 = sb("r1", [P, 5 * D])
        r2 = sb("r2", [P, 5 * D])
        gb = sb("gb", [P, 2, D])
        W = sb("W", [P, 14592])
        ident = sb("ident", [P, P])
        vec = sb("vec", [P, KB, 32])
        mod = sb("mod", [P, 2, NMOD, KB, 2])
        cond = sb("cond", [P, KB, 2])
        amod = sb("amod", [P, 4, KB, 2])
        router = sb("router", [P, 2, KB, NE])
        sp4 = sb("sp4", [P, KB, 2])
        stv = sb("stv", [P, 2, KB])
        st_row = sb("st_row", [16, P])
        sm = sb("sm", [P, 4, 3, 8])
        modraw = sb("modraw", [P, 2, KB, 2])
        mx5 = sb("mx5", [P, 2, 8])
        spt = sb("spt", [P, 6, KB, 2])
        sinks = sb("sinks", [P, 2, NH])
        stat = sb("stat", [P, 4, 8, 2])
        ss20 = sb("ss20", [P, 2, NQK])
        idx_t = sb("idx_t", [CE, NE], U32)
        g_t = sb("g_t", [CE, NE])
        gi = sb("gi", [CE, 1], U32)
        si = sb("si", [CE, 1], U32)
        sg = sb("sg", [CE, 1])

        def tok(t):
            return t[:, :].rearrange("p (t d) -> p t d", t=NT)

        w_tmp = W[:, 6144:7168].rearrange("p (a n) -> p a n", a=2)

        def feat(t):
            return t[:, 0:KB * NTOK].rearrange("p (k n) -> p k n", k=KB)

        off = [0]

        def work(n, at=None):
            if at is not None:
                off[0] = at
            off[0] += n
            assert off[0] <= 14592
            return W[:, off[0] - n:off[0]]

        w_xhat = work(5 * D, 0)
        w_junk = work(D)
        rows = work(D)
        ones = work(P)
        diag = work(2 * D).rearrange("p (s b d) -> p s b d", s=2, b=KB)
        w_junk2 = W[:, 8320:8320 + D]
        upad = work(UPAD + 3, 0)
        ucs = [work(UC) for _ in range(2)]
        rt = work(2 * NTOK).rearrange("p (a n) -> p a n", a=2)
        ig = work(2 * NTOK).rearrange("p (a n) -> p a n", a=2)
        sq = work(2 * NTOK).rearrange("p (a n) -> p a n", a=2)
        qq = work(2 * NTOK).rearrange("p (a n) -> p a n", a=2)
        aa = work(2 * NTOK).rearrange("p (a n) -> p a n", a=2)
        hh = work(2 * NTOK).rearrange("p (a n) -> p a n", a=2)
        gel = work(NTOK)
        bd = work(4 * KB * P).rearrange("p (m c j) -> p m c j", m=4, c=KB)
        q_t = work(KB * NTOK, 0).rearrange("p (h n) -> p h n", h=KB)
        KEYS = NTOK + P
        k_t = work(NKV * KEYS).rearrange("p (g n) -> p g n", g=NKV)
        v_s = work(6 * NKV * HD).rearrange("p (t n) -> p t n", t=6)
        T1 = off[0]
        qn = work(NQK * HD)
        qs = work(NQK * HD)
        gains = work(NQK * HD)
        tab = work(2 * TL * HD).rearrange("p (s t n) -> p s t n", s=2, t=TL)
        kdup = work(NKV * P).rearrange("p (g a n) -> p g a n", g=NKV, a=2)
        pm = work(2 * 2 * 512, T1).rearrange("p (u i n) -> p u i n", u=2, i=2)
        pt = work(2 * 2 * 512).rearrange("p (u i n) -> p u i n", u=2, i=2)
        mask = work(5 * P)
        kc = qn[:, 0:NKV * HD]
        gb1 = work(2 * D, 0).rearrange("p (s d) -> p s d", s=2)
        diag1 = work(2 * D).rearrange("p (s b d) -> p s b d", s=2, b=KB)
        ones1 = work(P)
        xn2 = work(5 * D, 0)
        xg = work(D)
        xt = work(KB * CE).rearrange("p (k n) -> p k n", k=KB)
        sil = work(KB * CE).rearrange("p (k n) -> p k n", k=KB)
        ht = work(KB * CE).rearrange("p (k n) -> p k n", k=KB)
        yt = work(KB * CE).rearrange("p (k n) -> p k n", k=KB)
        ob = work(D)
        ex = [work(KB * CE).rearrange("p (k n) -> p k n", k=KB) for _ in range(3)]
        tk = work(512)
        tv = work(CL)
        ti = W[:, off[0]:off[0] + CL].bitcast(U32)
        work(CL)
        comb = work(2 * CE).rearrange("p (a n) -> p a n", a=2)
        lg = work(NT * NE).rearrange("p (t n) -> p t n", t=NT)
        assert off[0] <= 14592

        waits_passed = sem("waits_passed")
        slot_ready = [sem(f"slot_ready{s}") for s in range(SLOTS)]
        ring_used, rows_in, x_in, bd_in = sem("ring_used"), sem("rows_in"), sem("x_in"), sem("bd_in")
        small_in, router_in, consts, dve = sem("small_in"), sem("router_in"), sem("consts"), sem("dve")
        pool_s, rows_t, vec_ok, sig_c = sem("pool_s"), sem("rows_t"), sem("vec_ok"), sem("sig_c")
        cond_ok, lam_abs, lam_exp, sp_ok = sem("cond_ok"), sem("lam_abs"), sem("lam_exp"), sem("sp_ok")
        mod_read, mod_ok, diag_ok, gate_mm = sem("mod_read"), sem("mod_ok"), sem("diag_ok"), sem("gate_mm")
        gate_ok, ssq_act, ssq_ok, var_ok = sem("gate_ok"), sem("ssq_act"), sem("ssq_ok"), sem("var_ok")
        std_ok, xhat_ok, tr_mm, tr_act = sem("std_ok"), sem("xhat_ok"), sem("tr_mm"), sem("tr_act")
        tr_dve, amod_ok, u_mm, u_ok = sem("tr_dve"), sem("amod_ok"), sem("u_mm"), sem("u_ok")
        conv_ok, g_mm, z_mm, sig_ok = sem("conv_ok"), sem("g_mm"), sem("z_mm"), sem("sig_ok")
        tanh_ok, sqrt_ok, gel_ok, iu_ok = sem("tanh_ok"), sem("sqrt_ok"), sem("gel_ok"), sem("iu_ok")
        q_read, scan_ok, hg_ok, st_ok = sem("q_read"), sem("scan_ok"), sem("hg_ok"), sem("st_ok")
        st_mm, st_row_ok, out_mm, out_mul = sem("st_mm"), sem("st_row_ok"), sem("out_mm"), sem("out_mul")
        x1_ok, x1_stored, xh_stored, stored = sem("x1_ok"), sem("x1_stored"), sem("xh_stored"), sem("stored")
        kv_stored, lg_mm, lg_sub, lg_exp = sem("kv_stored"), sem("lg_mm"), sem("lg_sub"), sem("lg_exp")
        aff_ok, aff_mm, tk_set, comb_ok = sem("aff_ok"), sem("aff_mm"), sem("tk_set"), sem("comb_ok")
        comb_mm, route_ok, ex_ok, cols_ok = sem("comb_mm"), sem("route_ok"), sem("ex_ok"), sem("cols_ok")
        gathered, scattered, xtr_mm, xt_mul = sem("gathered"), sem("scattered"), sem("xtr_mm"), sem("xt_mul")
        xt_ok, sil_ok, h_ok, yt_ok = sem("xt_ok"), sem("sil_ok"), sem("h_ok"), sem("yt_ok")
        otr_mm, ob_ok, kdup_ok, rot_ok = sem("otr_mm"), sem("ob_ok"), sem("kdup_ok"), sem("rot_ok")
        qkv_mm, qsq_ok, qvar_ok, qstd_ok = sem("qkv_mm"), sem("qsq_ok"), sem("qvar_ok"), sem("qstd_ok")
        v_ok, qn_read, qn_ok, q_mm = sem("v_ok"), sem("qn_read"), sem("qn_ok"), sem("q_mm")
        q_act, q_dve, k_mm, k_ok = sem("q_act"), sem("q_dve"), sem("k_mm"), sem("k_ok")
        sink_ok, s_mm, s_max, nm_ok = sem("sink_ok"), sem("s_mm"), sem("s_max"), sem("nm_ok")
        p_ok, pt_mm, pt_act, pt_dve = sem("p_ok"), sem("pt_mm"), sem("pt_act"), sem("pt_dve")
        pv_mm, o_ok, ot_mm, ot_act = sem("pv_mm"), sem("o_ok"), sem("ot_mm"), sem("ot_act")
        ot_dve, gains_ok = sem("ot_dve"), sem("gains_ok")

        KEYB = {0: ([0, 1, 5], 2 * P), 1: ([0, 1, 2, 5], P), 2: ([1, 2, 3, 5], P), 3: ([5, 2, 3], 0), 4: ([4], 0)}
        units = [(j, hp) for j in range(NT) for hp in range(KB)]
        NU = len(units)

        def last_of_tile(i):
            return 0 <= i < NU and i % KB == KB - 1

        def runs(blocks):
            out = []
            for n, b in enumerate(blocks):
                if out and b == out[-1][1] + out[-1][2]:
                    out[-1][2] += 1
                else:
                    out.append([n, b, 1])
            return out

        def used(rnd, s, e=0):
            return e * SLOTS + (rnd * SLOTS + s + 1)

        x_tiles = x_all.rearrange("(t p) d -> p t d", p=P)
        XF = KB * NTOK
        NORMS = ((r2, w_xhat, r1), (r1, r2, xn2), (r2, w_xhat, r1), (r2, r1, xn2))

        block = ctx.enter_context(nc.Block())

        @block.sync
        def _(sp):
            def load(rnd, s, dst, src, e=0):
                if not (isinstance(rnd, int) and rnd == 0):
                    sp.wait_ge(ring_used, used(rnd - 1, s, e))
                sp.dma_start(dst, src).then_inc(slot_ready[s], 16)

            def pair(s):
                return ring[:, s, :].rearrange("p (k n) -> p k n", k=2)

            def rows2(w, k2, c0=0):
                return w[k2 * 2 * P:(k2 + 1) * 2 * P, c0:c0 + D].rearrange("(k p) n -> p k n", p=P)

            def load_mod(rnd, layer, half):
                for s in range(SLOTS):
                    load(rnd, s, pair(s), rows2(mod_w[layer], s % 4, (3 * half + s // 4) * D))

            def load_moe(layer):
                with sp.Fori(0, NE) as e:
                    for s in range(SLOTS):
                        w = (moe_w_gate, moe_w_up, moe_w_down)[s // 4]
                        src = w[layer].rearrange("e (k p) n -> p (e k) n", p=P)[:, bass.ds(e * KB + (s % 4) * 2, 2), :]
                        load(MOE_ROUND[layer], s, pair(s), src, e)

            def store_x(layer, x1):
                sp.wait_ge(x1_ok, 2 * NT * (layer + 1))
                sp.dma_start(x_res[layer].rearrange("(t p) d -> p t d", p=P), tok(x1)).then_inc(x1_stored, 16)

            load_mod(ROUND_MOD0A, 0, 0)
            for s in range(KB):
                load(ROUND_RG, s, ring[:, s, :], rg_w_in[s * P:(s + 1) * P, :])
            for s in range(4):
                load(ROUND_RG, KB + s, pair(KB + s), rows2(rg_w_out, s))
            sp.wait_ge(g_mm, KB)
            sp.dma_start(tok(r1), x_tiles).then_inc(x_in, 16)
            load_mod(ROUND_MOD, 0, 1)
            store_x(0, r1)
            load_mod(ROUND_MOD + 1, 1, 0)
            load_mod(ROUND_MOD + 2, 1, 1)
            load_moe(0)
            for s in range(KB):
                load(ROUND_AT, s, ring[:, s, 0:QKV], at_w_qkv[s * P:(s + 1) * P, :])
            for s in range(4):
                load(ROUND_AT, KB + s, pair(KB + s), rows2(at_w_o, s))
            sp.wait_ge(qn_ok, NT)
            sp.dma_start(new_k, qn[:, NH * HD:NQK * HD]).then_inc(kv_stored, 16)
            sp.wait_ge(v_ok, NT)
            sp.dma_start(new_v, v_s[:, TL, :]).then_inc(kv_stored, 16)
            store_x(1, r2)
            load_moe(1)
            sp.wait_ge(st_row_ok, 1)
            sp.dma_start(new_state.rearrange("s (b p) -> (s b) p", p=P), st_row[:, :]).then_inc(stored, 16)
            sp.wait_ge(stored, 16)
            sp.wait_ge(kv_stored, 32)
            sp.wait_ge(x1_stored, 32)
            sp.wait_ge(xh_stored, 32)
            sp.wait_ge(scattered, 16 * 2 * NE)

        @block.gpsimd
        def _(pool):
            n = [0]

            def step(ins):
                n[0] += 1
                ins.then_inc(pool_s, 1)
                pool.wait_ge(pool_s, n[0])

            step(nc.gpsimd.memset(ident[:, :], 0.0))
            nc.gpsimd.affine_select(out=ident[:, :], in_=ident[:, :], compare_op=ALU.not_equal, fill=1.0,
                                    base=0, pattern=[[-1, P]], channel_multiplier=1).then_inc(consts, 1)
            nc.gpsimd.memset(bd, 0.0).then_inc(consts, 1)
            nc.gpsimd.memset(ones, 1.0).then_inc(consts, 1)

            def mod_bias(v):
                pool.wait_ge(mod_read, v + 1)
                nc.gpsimd.tensor_tensor(mod[:, v // NMOD, v % NMOD], modraw[:, v % 2],
                                        vec[:, :, R_MODB + v:R_MODB + v + 1].to_broadcast([P, KB, 2]),
                                        ALU.add).then_inc(mod_ok, 1)

            pool.wait_ge(vec_ok, 1)
            for v in range(3):
                mod_bias(v)
            pool.wait_ge(tr_mm, 2 * KB)
            nc.gpsimd.memset(upad, 0.0).then_inc(consts, 1)
            for b in range(KB):
                uc = ucs[b % 2]
                pool.wait_ge(sig_ok, 8 * (b + 1))
                pool.wait_ge(conv_ok, b + 1)
                nc.gpsimd.tensor_tensor(ig[:, :, 0:NLAT], ig[:, :, 0:NLAT],
                                        uc[:, 0:NLAT].unsqueeze(1).to_broadcast([P, 2, NLAT]), ALU.mult).then_inc(iu_ok, 1)
                nc.gpsimd.tensor_tensor(ig[:, :, NLAT:], ig[:, :, NLAT:],
                                        uc[:, C0:].unsqueeze(1).to_broadcast([P, 2, NCTX]), ALU.mult).then_inc(iu_ok, 1)
                pool.wait_ge(scan_ok, 4 * (b + 1))
                nc.gpsimd.tensor_copy(stv[:, 0, b:b + 1], hh[:, 0, NTOK - 1:NTOK]).then_inc(st_ok, 1)
                nc.gpsimd.tensor_copy(stv[:, 1, b:b + 1], hh[:, 1, NLAT:NLAT + 1]).then_inc(st_ok, 1)
            for v in range(3, 6):
                mod_bias(v)

            def experts(layer):
                base = layer * NE
                pool.wait_ge(x1_ok, 2 * NT * (layer + 1))
                nc.gpsimd.memset(tk[0:48, :], -1.0).then_inc(tk_set, 1)
                pool.wait_ge(amod_ok, 2 * layer + 2)
                pool.wait_ge(mod_ok, NMOD * (layer + 1))
                for m, src in enumerate((amod[:, 2 * layer + 1], mod[:, layer, 3], mod[:, layer, 5])):
                    nc.gpsimd.tensor_copy(ex[m][:, :, 0:CL], src[:, :, 0:1].to_broadcast([P, KB, CL])).then_inc(ex_ok, 1)
                    nc.gpsimd.tensor_copy(ex[m][:, :, CL:CE], src[:, :, 1:2].to_broadcast([P, KB, CC])).then_inc(ex_ok, 1)
                if layer == 0:
                    for v in range(6, 12):
                        mod_bias(v)
                pool.wait_ge(route_ok, 2 * (layer + 1))
                pool.wait_ge(xh_stored, 16 * (layer + 1))
                pool.wait_ge(x1_stored, 16 * (layer + 1))

                def gather():
                    nc.gpsimd.indirect_dma_start(xg[0:CE, :], None, x_hat[layer],
                                                 bass.IndirectOffsetOnAxis(ap=gi[:, 0:1], axis=0)).then_inc(gathered, 16)

                def passed():
                    pool.sem_inc(waits_passed, 1)

                def scatter():
                    nc.gpsimd.indirect_dma_start(x_res[layer], bass.IndirectOffsetOnAxis(ap=si[:, 0:1], axis=0), ob[0:CE, :],
                                                 None, compute_op=ALU.add).then_inc(scattered, 16)

                nc.gpsimd.tensor_copy(gi[:, :], idx_t[:, 0:1]).then_inc(cols_ok, 1)
                pool.wait_ge(cols_ok, 3 * base + 1)
                gather()
                with pool.Fori(0, NE - 1) as e:
                    nc.gpsimd.tensor_copy(sg[:, :], g_t[:, bass.ds(e, 1)]).then_inc(cols_ok, 1)
                    pool.wait_ge(gathered, e * 16 + 16 * (base + 1))
                    pool.wait_ge(xtr_mm, e + (base + 1))
                    nc.gpsimd.tensor_copy(gi[:, :], idx_t[:, bass.ds(e + 1, 1)]).then_inc(cols_ok, 1)
                    pool.wait_ge(cols_ok, e * 3 + (3 * base + 3))
                    passed()
                    gather()
                    nc.gpsimd.tensor_copy(si[:, :], idx_t[:, bass.ds(e, 1)]).then_inc(cols_ok, 1)
                    pool.wait_ge(cols_ok, e * 3 + (3 * base + 4))
                    pool.wait_ge(ob_ok, e * 2 + ((2 * NE + 2) * layer + 4))
                    passed()
                    scatter()
                    pool.wait_ge(scattered, e * 16 + 16 * (base + 1))
                nc.gpsimd.tensor_copy(sg[:, :], g_t[:, NE - 1:NE]).then_inc(cols_ok, 1)
                nc.gpsimd.tensor_copy(si[:, :], idx_t[:, NE - 1:NE]).then_inc(cols_ok, 1)
                pool.wait_ge(cols_ok, 3 * (base + NE))
                pool.wait_ge(ob_ok, (2 * NE + 2) * (layer + 1))
                scatter()
                pool.wait_ge(scattered, 16 * (base + NE))

            experts(0)
            pool.wait_ge(small_in, 16 * 7)
            for a in range(2):
                nc.gpsimd.tensor_copy(kdup[:, :, a, :], kc.rearrange("p (g n) -> p g n", g=NKV)).then_inc(kdup_ok, 1)
            nc.gpsimd.tensor_scalar(gains[:, 0:NH * HD], gains[:, 0:NH * HD], float(HD) ** -0.5, None, ALU.mult).then_inc(gains_ok, 1)
            nc.gpsimd.tensor_scalar(sinks[:, 1, :], sinks[:, 0, :], -1.0, None, ALU.mult).then_inc(sink_ok, 1)
            for t in range(NT):
                pool.wait_ge(qn_ok, t + 1)
                pool.wait_ge(k_mm, t + 1)
                for a in range(2):
                    nc.gpsimd.tensor_copy(kdup[:, :, a, :], qn[:, NH * HD:].rearrange("p (g n) -> p g n", g=NKV)).then_inc(kdup_ok, 1)
            pool.wait_ge(k_mm, NT + 1)
            pool.wait_ge(q_mm, NT)
            step(nc.gpsimd.memset(mask, 0.0))
            nc.gpsimd.affine_select(out=mask[:, P:2 * P], in_=mask[:, P:2 * P], compare_op=ALU.is_ge, fill=NEG,
                                    base=0, pattern=[[1, P]], channel_multiplier=-1).then_inc(consts, 1)
            nc.gpsimd.affine_select(out=mask[:, 3 * P:4 * P], in_=mask[:, 3 * P:4 * P], compare_op=ALU.is_ge, fill=NEG,
                                    base=0, pattern=[[-1, P]], channel_multiplier=1).then_inc(consts, 1)
            pool.wait_ge(s_mm, NU)
            nc.gpsimd.memset(ones1, 1.0).then_inc(consts, 1)
            experts(1)

        @block.tensor
        def _(pe):
            def wait_slot(rnd, s, e=0):
                pe.wait_ge(slot_ready[s], e * 16 + 16 * (rnd + 1))

            def modulation(rnd, n0, e=0):
                for v, bank in enumerate(MOD_BANKS):
                    if n0:
                        pe.wait_ge(mod_read, e * 3 + (n0 + v - 2))
                    for s in range(4):
                        wait_slot(rnd, 4 * v + s, e)
                        for k in range(2):
                            for m in range(KB):
                                mm = nc.tensor.matmul(ps[:, bank, 2 * m:2 * m + 2],
                                                      ring[:, 4 * v + s, k * D + m * P:k * D + (m + 1) * P],
                                                      cond[:, 2 * s + k, :], start=(s + k + m == 0),
                                                      stop=(s == 3 and k == 1), skip_group_check=True)
                        mm.then_inc(ring_used, 1)

            def gate_rows(layer, src_ones, src_diag):
                for s in range(2):
                    pe.wait_ge(diag_ok, 2 * layer + s + 1)
                    for n in range(2):
                        mm = nc.tensor.matmul(ps[:, 4 + 2 * s + n, :], src_ones, src_diag[:, s, 4 * n:4 * n + 4, :],
                                              start=True, stop=True)
                    mm.then_inc(gate_mm, 1)

            def turn(phase, route=None):
                xh, n0 = tok(NORMS[phase][1]), KB * phase
                pe.wait_ge(xhat_ok, NT * (phase + 1))
                pe.wait_ge(router_in, 32)
                for b in range(KB + 1):
                    if b < KB:
                        if b >= 2:
                            pe.wait_ge(tr_act, n0 + b - 1)
                            pe.wait_ge(tr_dve, n0 + b - 1)
                        for t in range(TL):
                            mm = nc.tensor.transpose(ps[:, b % 2, t * P:(t + 1) * P], xh[:, t, b * P:(b + 1) * P], ident[:, :])
                        mm.then_inc(tr_mm, 1)
                        nc.tensor.transpose(ps[:, 2 + b % 2, 0:P], xh[:, TL, b * P:(b + 1) * P], ident[:, :]).then_inc(tr_mm, 1)
                    if route is not None and b >= 1:
                        k = b - 1
                        pe.wait_ge(tr_act, n0 + k + 1)
                        pe.wait_ge(tr_dve, n0 + k + 1)
                        for t in range(NT):
                            mm = nc.tensor.matmul(ps[:, 4, t * NE:(t + 1) * NE], feat(xn2)[:, k, t * P:(t + 1) * P],
                                                  router[:, route, k, :], start=(k == 0 and t == 0),
                                                  stop=(k == KB - 1), skip_group_check=True)
                if route is not None:
                    mm.then_inc(lg_mm, 1)

            def mixer_out(layer, rnd, src):
                for t in range(NT):
                    if t >= 2:
                        pe.wait_ge(out_mul, 2 * (NT * layer + t - 1))
                    for n in range(2):
                        for k in range(KB):
                            if t == 0 and n == 0 and k % 2 == 0:
                                wait_slot(rnd, KB + k // 2)
                            mm = nc.tensor.matmul(ps[:, 2 * (t % 2) + n, :], feat(src)[:, k, t * P:(t + 1) * P],
                                                  ring[:, KB + k // 2, (k % 2) * D + n * 512:(k % 2) * D + (n + 1) * 512],
                                                  start=(k == 0), stop=(k == KB - 1))
                        if t == NT - 1 and n == 1:
                            mm.then_inc(ring_used, 4)
                        else:
                            mm.then_inc(out_mm, 1)

            def routes(layer):
                pe.wait_ge(aff_ok, layer + 1)
                for t in range(TL):
                    nc.tensor.transpose(ps[0:NE, 5, t * P:(t + 1) * P], lg[:, t, :], ident[:, :])
                nc.tensor.transpose(ps[0:NE, 3, 0:P], lg[:, TL, :], ident[:, :]).then_inc(aff_mm, 1)

            def chosen(layer):
                pe.wait_ge(comb_ok, 4 * (layer + 1))
                nc.tensor.transpose(ps[0:CE, 4, 0:NE], comb[0:NE, 0, :], ident[0:NE, 0:NE])
                nc.tensor.transpose(ps[0:CE, 4, NE:2 * NE], comb[0:NE, 1, :], ident[0:NE, 0:NE]).then_inc(comb_mm, 1)

            def experts(layer):
                rnd, base = MOE_ROUND[layer], layer * NE

                def product(e, bank, s0, rhs, first, last):
                    for s in range(s0 + first, s0 + last):
                        wait_slot(rnd, s, e)
                        for kk in range(2):
                            k = 2 * (s - s0) + kk
                            if s0 == 8 and k in (0, KB // 2):
                                pe.wait_ge(h_ok, e * 2 + (2 * base + 1 + k // 4))
                            for m in range(KB):
                                mm = nc.tensor.matmul(ps[:, bank + m // 4, (m % 4) * CE:(m % 4 + 1) * CE],
                                                      ring[:, s, kk * D + m * P:kk * D + (m + 1) * P], rhs[:, k, :],
                                                      start=(k == 0 and m % 4 == 0), stop=(k == KB - 1), skip_group_check=True)
                        mm.then_inc(ring_used, 1)

                def x_turn(e):
                    pe.wait_ge(gathered, e * 16 + 16 * (base + 1))
                    pe.wait_ge(ob_ok, (2 * NE + 2) * layer + 2 if isinstance(e, int) else e * 2 + (2 * NE + 2) * layer)
                    for b in range(KB):
                        mm = nc.tensor.transpose(ps[:, 6 + b // 4, (b % 4) * CE:(b % 4 + 1) * CE], xg[0:CE, b * P:(b + 1) * P],
                                                 ident[0:CE, 0:CE])
                    mm.then_inc(xtr_mm, 1)

                def gate_first(e):
                    pe.wait_ge(xt_ok, e * 2 + 2 * (base + 1))
                    product(e, 0, 0, xt, 0, 2)

                def y_turn(e):
                    pe.wait_ge(yt_ok, e * 2 + 2 * (base + 1))
                    for b in range(KB):
                        mm = nc.tensor.transpose(ps[0:CE, 6 + b // 4, (b % 4) * P:(b % 4 + 1) * P], yt[:, b, :], ident[:, :])
                    mm.then_inc(otr_mm, 1)

                x_turn(0)
                gate_first(0)
                with pe.Fori(0, NE - 1) as e:
                    product(e, 0, 0, xt, 2, 4)
                    product(e, 2, 4, xt, 0, 4)
                    x_turn(e + 1)
                    product(e, 4, 8, ht, 0, 4)
                    gate_first(e + 1)
                    y_turn(e)
                product(NE - 1, 0, 0, xt, 2, 4)
                product(NE - 1, 2, 4, xt, 0, 4)
                product(NE - 1, 4, 8, ht, 0, 4)
                y_turn(NE - 1)

            pe.wait_ge(consts, 1)
            pe.wait_ge(rows_in, 16 * 11)
            for b in range(KB):
                mm = nc.tensor.transpose(ps[:, 0, b * 32:b * 32 + NROWS], rows[0:NROWS, b * P:(b + 1) * P],
                                         ident[0:NROWS, 0:NROWS])
            mm.then_inc(rows_t, 1)
            pe.wait_ge(cond_ok, 1)
            modulation(ROUND_MOD0A, 0)
            pe.wait_ge(mod_read, 3)
            turn(0)
            pe.wait_ge(consts, 3)
            pe.wait_ge(mod_read, 3)
            gate_rows(0, ones, diag)
            pe.wait_ge(tr_act, KB)
            pe.wait_ge(tr_dve, KB)
            pe.wait_ge(gate_ok, 4)
            xf = feat(r1)

            def project(cols, lat, con, gates_read, done):
                for k in range(KB):
                    nc.tensor.matmul(ps[:, lat, :], ring[:, k, cols:cols + P], xf[:, k, 0:NLAT], start=(k == 0), stop=(k == KB - 1))
                if gates_read:
                    pe.wait_ge(sig_ok, gates_read)
                for k in range(KB):
                    mm = nc.tensor.matmul(ps[:, con, 0:P], ring[:, k, cols:cols + P], xf[:, k, NLAT:], start=(k == 0), stop=(k == KB - 1))
                mm.then_inc(done, 1)

            for b in range(KB + 1):
                if b < KB:
                    if b == 0:
                        for s in range(KB):
                            wait_slot(ROUND_RG, s)
                    if b >= 1:
                        pe.wait_ge(u_ok, 2 * b)
                    project(D + b * P, 0, 1, 0, u_mm)
                if b >= 1:
                    pe.wait_ge(conv_ok, b)
                    pe.wait_ge(bd_in, 16 * 8)
                    pe.wait_ge(gel_ok, 2 * b)
                    if b >= 2:
                        pe.wait_ge(sig_ok, 8 * (b - 1))
                    for m in range(4):
                        nc.tensor.matmul(ps[:, 4 + m, :], bd[:, m, b - 1, :], ucs[(b - 1) % 2][:, 0:NLAT], start=True, stop=True)
                        mm = nc.tensor.matmul(ps[:, 3, m * P:(m + 1) * P], bd[:, m, b - 1, :], ucs[(b - 1) % 2][:, C0:],
                                              start=True, stop=True)
                        if b == KB and m == 0:
                            mm.then_inc(ring_used, KB)
                    mm.then_inc(z_mm, 1)
                if b < KB:
                    if b >= 1:
                        pe.wait_ge(gel_ok, 2 * b)
                    project(b * P, 2, 3, 8 * b - 4 if b else 0, g_mm)
            pe.wait_ge(hg_ok, KB)
            mixer_out(0, ROUND_RG, r2)
            pe.wait_ge(st_ok, 2 * KB)
            nc.tensor.transpose(ps[0:16, 4, 0:P], stv[:, :, :].rearrange("p s b -> p (s b)"), ident[:, :]).then_inc(st_mm, 1)
            pe.wait_ge(out_mul, 8)
            modulation(ROUND_MOD, 3)
            pe.wait_ge(st_row_ok, 1)
            pe.wait_ge(mod_read, 6)
            turn(1, 0)
            routes(0)
            with pe.Fori(0, 2) as h:
                modulation(ROUND_MOD + 1, 6, h)
            chosen(0)
            experts(0)

            def turn_k(n, bank):
                pe.wait_ge(kdup_ok, 2 * (n + 1))
                for g in range(NKV):
                    mm = nc.tensor.transpose(ps[:, bank, g * P:(g + 1) * P], kdup[:, g].rearrange("p a n -> p (a n)"), ident[:, :])
                mm.then_inc(k_mm, 1)

            turn(2)
            pe.wait_ge(tr_act, 3 * KB)
            pe.wait_ge(tr_dve, 3 * KB)
            turn_k(0, 6)

            def turn_q(t):
                pe.wait_ge(qn_ok, t + 1)
                pe.wait_ge(k_ok, t + 1)
                if t >= 1:
                    pe.wait_ge(q_dve, t)
                for h in range(KB):
                    mm = nc.tensor.transpose(ps[:, 6 + h // 4, (h % 4) * P:(h % 4 + 1) * P], qn[:, h * P:(h + 1) * P], ident[:, :])
                mm.then_inc(q_mm, 1)
                pe.wait_ge(q_act, t + 1)
                turn_k(t + 1, 6)

            for t in range(NT):
                if t >= 2:
                    pe.wait_ge(qn_read, t - 1)
                    pe.wait_ge(v_ok, t - 1)
                for k in range(KB):
                    if t == 0:
                        wait_slot(ROUND_AT, k)
                    for n in range(3):
                        mm = nc.tensor.matmul(ps[:, 3 * (t % 2) + n, :], xf[:, k, t * P:(t + 1) * P],
                                              ring[:, k, n * 512:(n + 1) * 512], start=(k == 0), stop=(k == KB - 1))
                if t == NT - 1:
                    mm.then_inc(ring_used, KB)
                else:
                    mm.then_inc(qkv_mm, 1)
                if t >= 1:
                    turn_q(t - 1)
            turn_q(NT - 1)
            pe.wait_ge(k_ok, NT + 1)
            pe.wait_ge(q_dve, NT)
            pe.wait_ge(qn_read, NT)
            pe.wait_ge(v_ok, NT)
            for i in range(NU + 3):
                if i < NU:
                    j, hp = units[i]
                    if i >= 2:
                        pe.wait_ge(s_max, 2 * (i - 1))
                    for a in range(2):
                        for n, b0, m in runs(KEYB[j][0]):
                            mm = nc.tensor.matmul(ps[:, 2 * (i % 2) + a, n * P:(n + m) * P],
                                                  q_t[a * HD:(a + 1) * HD, hp, j * P:(j + 1) * P],
                                                  k_t[a * HD:(a + 1) * HD, hp // 2, b0 * P:(b0 + m) * P], start=True, stop=True)
                    mm.then_inc(s_mm, 1)
                if 1 <= i <= NU:
                    j, hp = units[i - 1]
                    pe.wait_ge(p_ok, 3 * i)
                    if i >= 2:
                        pe.wait_ge(pt_act, i - 1)
                        pe.wait_ge(pt_dve, i - 1)
                    if last_of_tile(i - 4):
                        pe.wait_ge(ot_act, (i - 4) // KB + 1)
                        pe.wait_ge(ot_dve, (i - 4) // KB + 1)
                    for a in range(2):
                        for n in range(len(KEYB[j][0])):
                            mm = nc.tensor.transpose(ps[:, 4 + a, n * P:(n + 1) * P], pm[:, (i - 1) % 2, a, n * P:(n + 1) * P], ident[:, :])
                    mm.then_inc(pt_mm, 1)
                if 2 <= i < NU + 2:
                    j, hp = units[i - 2]
                    pe.wait_ge(pt_act, i - 1)
                    pe.wait_ge(pt_dve, i - 1)
                    if i >= 4:
                        pe.wait_ge(o_ok, i - 3)
                    for a in range(2):
                        for n, b in enumerate(KEYB[j][0]):
                            mm = nc.tensor.matmul(ps[:, 6 + i % 2, a * HD:(a + 1) * HD], pt[:, i % 2, a, n * P:(n + 1) * P],
                                                  v_s[:, b, (hp // 2) * HD:(hp // 2 + 1) * HD], start=(n == 0),
                                                  stop=(n == len(KEYB[j][0]) - 1))
                    mm.then_inc(pv_mm, 1)
                if last_of_tile(i - 3):
                    j = (i - 3) // KB
                    pe.wait_ge(o_ok, KB * (j + 1))
                    if i <= NU:
                        pe.wait_ge(pt_act, i)
                        pe.wait_ge(pt_dve, i)
                    for b in range(KB):
                        mm = nc.tensor.transpose(ps[:, 4 + b // 4, (b % 4) * P:(b % 4 + 1) * P], gb[:, j % 2, b * P:(b + 1) * P], ident[:, :])
                    mm.then_inc(ot_mm, 1)
            pe.wait_ge(ot_act, NT)
            pe.wait_ge(ot_dve, NT)
            pe.wait_ge(consts, 7)
            gate_rows(1, ones1, diag1)
            mixer_out(1, ROUND_AT, r1)
            turn(3, 1)
            routes(1)
            chosen(1)
            experts(1)

        @block.scalar
        def _(act):
            def copy(out, in_, done, n=1):
                nc.scalar.activation(out, in_, ACT.Copy).then_inc(done, n)

            def squares(phase, x_ready):
                for t in range(3):
                    if x_ready is not None:
                        act.wait_ge(x1_ok, x_ready + 2 * (t + 1))
                    nc.scalar.activation(w_junk, tok(NORMS[phase][0])[:, t, :], ACT.Square,
                                         accum_out=sm[:, phase, 0, t:t + 1]).then_inc(ssq_act, 1)
                    act.wait_ge(ssq_act, 3 * phase + t + 1)
                act.wait_ge(var_ok, phase + 1)
                nc.scalar.activation(sm[:, phase, 1, 0:NT], sm[:, phase, 0, 0:NT], ACT.Sqrt).then_inc(std_ok, 1)

            def turned(phase, layer):
                out = feat(NORMS[phase][2])
                act.wait_ge(amod_ok, phase + 1)
                for b in range(KB):
                    act.wait_ge(tr_mm, 2 * (KB * phase + b) + 2 - (b + 1) % 2)
                    src, cols, st = ((ps[:, b % 2, :], slice(0, NLAT), 0) if b % 2 == 0
                                     else (ps[:, 2 + b % 2, 0:P], slice(NLAT, NTOK), 1))
                    nc.scalar.activation(out[:, b, cols], src, ACT.Identity, scale=amod[:, phase, b, st:st + 1],
                                         bias=mod[:, layer, 3 * (phase % 2), b, st:st + 1]).then_inc(tr_act, 1)

            def mod_reads(vs):
                for v in vs:
                    act.wait_ge(ring_used, used((ROUND_MOD0A, ROUND_MOD, ROUND_MOD + 1, ROUND_MOD + 2)[v // 3], 4 * (v % 3) + 3))
                    if v >= 2:
                        act.wait_ge(mod_ok, v - 1)
                    copy(modraw[:, v % 2].rearrange("p b s -> p (b s)"), ps[:, MOD_BANKS[v % 3], 0:2 * KB], mod_read)

            def gate_copy(layer, out):
                for s in range(2):
                    act.wait_ge(gate_mm, 2 * layer + s + 1)
                    for n in range(2):
                        copy(out[:, s, n * 512:(n + 1) * 512], ps[:, 4 + 2 * s + n, :], gate_ok)

            def softmax(layer):
                act.wait_ge(lg_sub, layer + 1)
                nc.scalar.activation(lg, lg, ACT.Exp).then_inc(lg_exp, 1)

            def store_xhat(layer):
                act.wait_ge(xhat_ok, NT * (2 * layer + 2))
                act.dma_start(x_hat[layer].rearrange("(t p) d -> p t d", p=P), tok(NORMS[2 * layer + 1][1])).then_inc(xh_stored, 16)

            def experts(layer):
                rnd, base = MOE_ROUND[layer], layer * NE
                act.wait_ge(mod_read, 2 * NMOD)
                act.wait_ge(gate_ok, 4 * (layer + 1))
                act.sem_inc(ob_ok, 2)

                def body(e):
                    act.wait_ge(ring_used, used(rnd, 3, e))
                    for n in range(2):
                        nc.scalar.activation(sil[:, 4 * n:4 * n + 4, :], ps[:, n, 0:4 * CE], ACT.Silu).then_inc(sil_ok, 1)
                    act.wait_ge(cols_ok, e * 3 + (3 * base + 2))
                    act.wait_ge(otr_mm, e + (base + 1))
                    for n in range(2):
                        nc.scalar.activation(ob[0:CE, n * 512:(n + 1) * 512], ps[0:CE, 6 + n, :], ACT.Copy,
                                             scale=sg[:, 0:1]).then_inc(ob_ok, 1)
                with act.Fori(0, NE) as e:
                    body(e)

            vecs = ((R_C, c), (R_CCTX, c_ctx), (R_G1, norm1_g), (R_G2, norm2_g), (R_CW, rg_conv_w), (R_CB, rg_conv_b),
                    (R_BA, rg_b_a), (R_BX, rg_b_x), (R_LAM, rg_lambda), (R_H0, state), (R_MODB, mod_b))
            for r, v in vecs:
                act.dma_start(rows[r:r + v.shape[0], :], v).then_inc(rows_in, 16)
            act.dma_start(tok(r2), x_tiles).then_inc(x_in, 16)
            for l in range(2):
                act.dma_start(router[:, l], moe_router[l].rearrange("(k p) e -> p k e", p=P)).then_inc(router_in, 16)
            act.wait_ge(consts, 2)
            for m, w in enumerate((rg_w_a[0], rg_w_a[1], rg_w_x[0], rg_w_x[1])):
                for h in range(2):
                    act.dma_start(bd[h * RB:(h + 1) * RB, m, :, h * RB:(h + 1) * RB],
                                  w.rearrange("(c h) i j -> h i c j", h=2)[h]).then_inc(bd_in, 16)
            act.wait_ge(vec_ok, 1)
            nc.scalar.activation(cond[:, :, :], vec[:, :, R_C:R_C + 2], ACT.Sigmoid).then_inc(sig_c, 1)
            act.wait_ge(lam_abs, 1)
            nc.scalar.activation(spt[:, 3], spt[:, 1], ACT.Exp, scale=-1.0).then_inc(lam_exp, 1)
            act.wait_ge(x_in, 16)
            squares(0, None)
            mod_reads(range(3))
            turned(0, 0)
            gate_copy(0, gb)

            act.wait_ge(consts, 4)
            for b in range(KB + 1):
                if b < KB:
                    act.wait_ge(u_mm, b + 1)
                    if b >= 1:
                        act.wait_ge(conv_ok, b)
                    copy(upad[:, 2:2 + NLAT], ps[:, 0, :], u_ok)
                    copy(upad[:, 4 + NLAT:4 + NLAT + NCTX], ps[:, 1, 0:P], u_ok)
                if b >= 1:
                    c1 = b - 1
                    act.wait_ge(z_mm, b)
                    if b >= 2:
                        act.wait_ge(q_read, c1)
                        act.wait_ge(hg_ok, c1)
                    for cols in (slice(NLAT, NTOK), slice(0, NLAT)):
                        for m, row in enumerate((R_BA, R_BA + 1, R_BX, R_BX + 1)):
                            nc.scalar.activation((rt, ig)[m // 2][:, m % 2, cols],
                                                 ps[:, 3, m * P:(m + 1) * P] if cols.start else ps[:, 4 + m, :],
                                                 ACT.Sigmoid, bias=vec[:, c1, row:row + 1]).then_inc(sig_ok, 1)
                    act.wait_ge(sig_ok, 8 * b)
                    act.wait_ge(sp_ok, 1)
                    for s in range(2):
                        nc.scalar.activation(rt[:, s], rt[:, s], ACT.Tanh, scale=sp4[:, c1, s:s + 1]).then_inc(tanh_ok, 1)
                    act.wait_ge(tanh_ok, 2 * b)
                    nc.scalar.activation(sq, rt, ACT.Sqrt, scale=4.0).then_inc(sqrt_ok, 1)
                if b < KB:
                    act.wait_ge(g_mm, b + 1)
                    if b >= 1:
                        act.wait_ge(hg_ok, b)
                    nc.scalar.activation(gel[:, 0:NLAT], ps[:, 2, :], ACT.Gelu_apprx_tanh).then_inc(gel_ok, 1)
                    nc.scalar.activation(gel[:, NLAT:], ps[:, 3, 0:P], ACT.Gelu_apprx_tanh).then_inc(gel_ok, 1)
            squares(1, 0)
            mod_reads(range(3, 6))
            store_xhat(0)
            turned(1, 0)
            softmax(0)
            mod_reads(range(6, 12))
            experts(0)

            act.wait_ge(scattered, 16 * NE)
            act.dma_start(tok(r2), x_mid.rearrange("(t p) d -> p t d", p=P)).then_inc(x_in, 16)
            act.dma_start(kc, cache_k).then_inc(small_in, 16)
            act.dma_start(v_s[:, 5, :], cache_v).then_inc(small_in, 16)
            act.dma_start(gains[:, 0:NH * HD].rearrange("p (h n) -> p h n", n=HD),
                          at_q_norm.unsqueeze(1).to_broadcast([P, NH, HD])).then_inc(small_in, 16)
            act.dma_start(gains[:, NH * HD:].rearrange("p (h n) -> p h n", n=HD),
                          at_k_norm.unsqueeze(1).to_broadcast([P, NKV, HD])).then_inc(small_in, 16)
            for s in range(2):
                act.dma_start(tab[:, s], rope[s].rearrange("(t p) n -> p t n", p=P)).then_inc(small_in, 16)
            act.dma_start(sinks[:, 0, :], at_sink.to_broadcast([P, NH])).then_inc(small_in, 16)
            act.wait_ge(x_in, 48)
            squares(2, None)
            turned(2, 1)
            act.wait_ge(k_mm, 1)
            copy(k_t[:, :, NTOK:KEYS], ps[:, 6, :], k_ok)

            def turned_q(t):
                act.wait_ge(q_mm, t + 1)
                copy(q_t[:, 0:4, t * P:(t + 1) * P], ps[:, 6, :], q_act)
                act.wait_ge(k_mm, t + 2)
                copy(k_t[:, :, t * P:(t + 1) * P], ps[:, 6, :], k_ok)

            for t in range(NT):
                if t < NT - 1:
                    act.wait_ge(qkv_mm, t + 1)
                else:
                    act.wait_ge(ring_used, used(ROUND_AT, KB - 1))
                z = 3 * (t % 2)
                if t >= 1:
                    act.wait_ge(qn_ok, t)
                for n, w in ((0, 512), (1, 512), (2, 256)):
                    nc.scalar.activation(qs[:, n * 512:n * 512 + w], ps[:, z + n, 0:w], ACT.Square).then_inc(qsq_ok, 1)
                copy(v_s[:, t, :], ps[:, z + 2, 256:512], v_ok)
                act.wait_ge(qvar_ok, t + 1)
                nc.scalar.activation(ss20[:, 1], ss20[:, 0], ACT.Sqrt).then_inc(qstd_ok, 1)
                if t >= 1:
                    turned_q(t - 1)
            turned_q(NT - 1)
            for i in range(NU + 3):
                if i < NU:
                    j, hp = units[i]
                    act.wait_ge(nm_ok, i + 1)
                    w = len(KEYB[j][0]) * P
                    for a in range(2):
                        nc.scalar.activation(pm[:, i % 2, a, 0:w], pm[:, i % 2, a, 0:w], ACT.Exp, bias=stat[:, i % 4, 1, a:a + 1],
                                             accum_out=stat[:, i % 4, 3, a:a + 1]).then_inc(p_ok, 1)
                    nc.scalar.activation(stat[:, i % 4, 4, :], stat[:, i % 4, 2, :], ACT.Exp).then_inc(p_ok, 1)
                if 1 <= i <= NU:
                    w = len(KEYB[units[i - 1][0]][0]) * P
                    act.wait_ge(pt_mm, i)
                    if i >= 3:
                        act.wait_ge(pv_mm, i - 2)
                    copy(pt[:, (i - 1) % 2, 0, 0:w], ps[:, 4, 0:w], pt_act)
                if last_of_tile(i - 3):
                    j = (i - 3) // KB
                    act.wait_ge(ot_mm, j + 1)
                    copy(feat(r1)[:, 0:4, j * P:(j + 1) * P], ps[:, 4, :], ot_act)
            gate_copy(1, gb1)
            squares(3, 2 * NT)
            store_xhat(1)
            turned(3, 1)
            softmax(1)
            experts(1)

        @block.vector
        def _(eng):
            n = [0]

            def step(ins):
                n[0] += 1
                ins.then_inc(dve, 1)
                eng.wait_ge(dve, n[0])

            v = nc.vector

            def norm(phase, x_ready):
                x, xh = tok(NORMS[phase][0]), tok(NORMS[phase][1])
                for t in range(3, NT):
                    if x_ready is not None:
                        eng.wait_ge(x1_ok, x_ready + 2 * (t + 1))
                    v.tensor_tensor_reduce(out=w_junk2, in0=x[:, t, :], in1=x[:, t, :], scale=1.0, scalar=0.0,
                                           op0=ALU.mult, op1=ALU.add, accum_out=sm[:, phase, 0, t:t + 1]).then_inc(ssq_ok, 1)
                    eng.wait_ge(ssq_ok, 2 * phase + t - 2)
                eng.wait_ge(ssq_act, 3 * (phase + 1))
                eng.wait_ge(ssq_ok, 2 * (phase + 1))
                v.tensor_scalar(sm[:, phase, 0, 0:NT], sm[:, phase, 0, 0:NT], 1.0 / D, EPS, ALU.mult, ALU.add).then_inc(var_ok, 1)
                eng.wait_ge(std_ok, phase + 1)
                step(v.reciprocal(sm[:, phase, 2, 0:NT], sm[:, phase, 1, 0:NT]))
                for t in range(NT):
                    v.tensor_scalar(xh[:, t, :], x[:, t, :], sm[:, phase, 2, t:t + 1], None, ALU.mult).then_inc(xhat_ok, 1)

            def turned(phase, layer):
                eng.wait_ge(mod_ok, NMOD * layer + 3 * (phase % 2) + 2)
                row = (R_G1, R_G2)[phase % 2] + layer
                v.scalar_tensor_tensor(out=amod[:, phase], in0=mod[:, layer, 3 * (phase % 2) + 1], scalar=1.0,
                                       in1=vec[:, :, row:row + 1].to_broadcast([P, KB, 2]), op0=ALU.add,
                                       op1=ALU.mult).then_inc(amod_ok, 1)
                eng.wait_ge(amod_ok, phase + 1)
                out = feat(NORMS[phase][2])
                for b in range(KB):
                    eng.wait_ge(tr_mm, 2 * (KB * phase + b) + 1 + (b + 1) % 2)
                    src, cols, st = ((ps[:, b % 2, :], slice(0, NLAT), 0) if b % 2 == 1
                                     else (ps[:, 2 + b % 2, 0:P], slice(NLAT, NTOK), 1))
                    v.tensor_scalar(out[:, b, cols], src, amod[:, phase, b, st:st + 1],
                                    mod[:, layer, 3 * (phase % 2), b, st:st + 1], ALU.mult, ALU.add).then_inc(tr_dve, 1)

            def diagonals(layer, out):
                eng.wait_ge(mod_ok, NMOD * layer + 3)
                for s in range(2):
                    v.tensor_tensor(out[:, s], ident[:, :].unsqueeze(1).to_broadcast([P, KB, P]),
                                    mod[:, layer, 2, :, s:s + 1].to_broadcast([P, KB, P]), ALU.mult).then_inc(diag_ok, 1)

            def residual(layer, x1, g, rnd):
                x = tok(x1)
                eng.wait_ge(gate_ok, 4 * (layer + 1))
                for t in range(NT):
                    for h in range(2):
                        m = 2 * t + h
                        if m < 2 * NT - 1:
                            eng.wait_ge(out_mm, (2 * NT - 1) * layer + m + 1)
                        else:
                            eng.wait_ge(ring_used, used(rnd, SLOTS - 1))
                        v.tensor_tensor(w_tmp[:, m % 2], ps[:, 2 * (t % 2) + h, :], g[:, t // TL, h * 512:(h + 1) * 512],
                                        ALU.mult).then_inc(out_mul, 1)
                        eng.wait_ge(out_mul, 2 * NT * layer + m + 1)
                        xs = x[:, t, h * 512:(h + 1) * 512]
                        v.tensor_tensor(xs, xs, w_tmp[:, m % 2], ALU.add).then_inc(x1_ok, 1)

            def route(layer):
                lgp = ps[:, 4, 0:NT * NE].rearrange("p (t n) -> p t n", t=NT)
                eng.wait_ge(lg_mm, layer + 1)
                step(v.tensor_reduce(mx5[:, 0, 0:NT], lgp, AX.X, ALU.max))
                v.tensor_tensor(lg, lgp, mx5[:, 0, 0:NT].unsqueeze(2).to_broadcast([P, NT, NE]), ALU.subtract).then_inc(lg_sub, 1)
                eng.wait_ge(lg_exp, layer + 1)
                step(v.tensor_reduce(mx5[:, 1, 0:NT], lg, AX.X, ALU.add))
                step(v.reciprocal(mx5[:, 1, 0:NT], mx5[:, 1, 0:NT]))
                v.tensor_tensor(lg, lg, mx5[:, 1, 0:NT].unsqueeze(2).to_broadcast([P, NT, NE]), ALU.mult).then_inc(aff_ok, 1)
                eng.wait_ge(tk_set, layer + 1)
                eng.wait_ge(aff_mm, layer + 1)
                step(v.tensor_copy(tk[0:NE, :], ps[0:NE, 5, :]))
                step(v.tensor_copy(tk[32:32 + NE, 0:NCTX], ps[0:NE, 3, 0:P]))
                for r in range(CL // 8):
                    k8 = slice(8 * r, 8 * r + 8)
                    step(v.max(tv[0:48, k8], tk[0:48, :]))
                    step(v.max_index(ti[0:48, k8], tv[0:48, k8], tk[0:48, :]))
                    if r < CL // 8 - 1:
                        step(v.match_replace(tk[0:48, :], tv[0:48, k8], tk[0:48, :], -1.0))
                v.tensor_copy(comb[0:NE, 0, 0:CL], tv[0:NE, :]).then_inc(comb_ok, 1)
                v.tensor_copy(comb[0:NE, 0, CL:CE], tv[32:32 + NE, 0:CC]).then_inc(comb_ok, 1)
                v.tensor_copy(comb[0:NE, 1, 0:CL], ti[0:NE, :]).then_inc(comb_ok, 1)
                v.tensor_scalar(comb[0:NE, 1, CL:CE], ti[32:32 + NE, 0:CC], float(NLAT), None, ALU.add).then_inc(comb_ok, 1)
                eng.wait_ge(comb_mm, layer + 1)
                v.tensor_copy(g_t[:, :], ps[0:CE, 4, 0:NE]).then_inc(route_ok, 1)
                v.tensor_copy(idx_t[:, :], ps[0:CE, 4, NE:2 * NE]).then_inc(route_ok, 1)

            def experts(layer):
                rnd, base = MOE_ROUND[layer], layer * NE
                eng.wait_ge(ex_ok, 6 * (layer + 1))

                def x_mod(e):
                    eng.wait_ge(xtr_mm, e + (base + 1))
                    for h in range(2):
                        v.tensor_tensor(xt[:, 4 * h:4 * h + 4, :], ps[:, 6 + h, 0:4 * CE], ex[0][:, 4 * h:4 * h + 4, :],
                                        ALU.mult).then_inc(xt_mul, 1)
                    eng.wait_ge(xt_mul, e * 2 + 2 * (base + 1))
                    for h in range(2):
                        v.tensor_tensor(xt[:, 4 * h:4 * h + 4, :], xt[:, 4 * h:4 * h + 4, :], ex[1][:, 4 * h:4 * h + 4, :],
                                        ALU.add).then_inc(xt_ok, 1)

                def hidden(e):
                    eng.wait_ge(ring_used, used(rnd, 7, e))
                    for h in range(2):
                        eng.wait_ge(sil_ok, e * 2 + (2 * base + 1 + h))
                        v.tensor_tensor(ht[:, 4 * h:4 * h + 4, :], ps[:, 2 + h, 0:4 * CE], sil[:, 4 * h:4 * h + 4, :],
                                        ALU.mult).then_inc(h_ok, 1)

                def output(e):
                    eng.wait_ge(ring_used, used(rnd, 11, e))
                    for h in range(2):
                        v.tensor_tensor(yt[:, 4 * h:4 * h + 4, :], ps[:, 4 + h, 0:4 * CE], ex[2][:, 4 * h:4 * h + 4, :],
                                        ALU.mult).then_inc(yt_ok, 1)

                x_mod(0)
                with eng.Fori(0, NE - 1) as e:
                    hidden(e)
                    x_mod(e + 1)
                    output(e)
                hidden(NE - 1)
                output(NE - 1)

            eng.wait_ge(rows_t, 1)
            v.tensor_copy(vec[:, :, 0:NROWS], ps[:, 0, 0:KB * 32].rearrange("p (b r) -> p b r", b=KB)[:, :, 0:NROWS]).then_inc(vec_ok, 1)
            eng.wait_ge(vec_ok, 1)
            eng.wait_ge(sig_c, 1)
            v.tensor_tensor(cond[:, :, :], cond[:, :, :], vec[:, :, R_C:R_C + 2], ALU.mult).then_inc(cond_ok, 1)
            lam = vec[:, :, R_LAM:R_LAM + 2]
            step(v.tensor_scalar(spt[:, 0], lam, -1.0, None, ALU.mult))
            v.tensor_tensor(spt[:, 1], spt[:, 0], lam, ALU.max).then_inc(lam_abs, 1)
            step(v.tensor_scalar(spt[:, 2], spt[:, 0], 0.0, 4.0, ALU.max, ALU.mult))
            eng.wait_ge(lam_exp, 1)
            step(v.tensor_scalar(spt[:, 4], spt[:, 3], 2.0, None, ALU.add))
            step(v.reciprocal(spt[:, 4], spt[:, 4]))
            step(v.tensor_tensor(spt[:, 3], spt[:, 3], spt[:, 4], ALU.mult))
            step(v.tensor_tensor(spt[:, 4], spt[:, 3], spt[:, 3], ALU.mult))
            step(v.tensor_scalar(spt[:, 5], spt[:, 4], 1.0 / 17, None, ALU.mult))
            for m in (15, 13, 11, 9, 7, 5, 3):
                step(v.scalar_tensor_tensor(out=spt[:, 5], in0=spt[:, 5], scalar=1.0 / m, in1=spt[:, 4], op0=ALU.add, op1=ALU.mult))
            step(v.scalar_tensor_tensor(out=spt[:, 5], in0=spt[:, 5], scalar=1.0, in1=spt[:, 3], op0=ALU.add, op1=ALU.mult))
            v.scalar_tensor_tensor(out=sp4[:, :, :], in0=spt[:, 5], scalar=8.0, in1=spt[:, 2], op0=ALU.mult, op1=ALU.add).then_inc(sp_ok, 1)
            eng.wait_ge(x_in, 16)
            norm(0, None)
            turned(0, 0)
            diagonals(0, diag)

            hg = feat(r2)
            eng.wait_ge(consts, 4)
            for b in range(KB + 1):
                if b < KB:
                    uc = ucs[b % 2]
                    eng.wait_ge(u_ok, 2 * (b + 1))
                    if b >= 2:
                        eng.wait_ge(z_mm, b - 1)
                        eng.wait_ge(iu_ok, 2 * (b - 1))
                    step(v.tensor_scalar(uc, upad[:, 0:UC], vec[:, b, R_CW:R_CW + 1], vec[:, b, R_CB:R_CB + 1], ALU.mult, ALU.add))
                    for k in range(1, 4):
                        ins = v.scalar_tensor_tensor(out=uc, in0=upad[:, k:k + UC], scalar=vec[:, b, R_CW + k:R_CW + k + 1],
                                                     in1=uc, op0=ALU.mult, op1=ALU.add)
                        if k < 3:
                            step(ins)
                    ins.then_inc(conv_ok, 1)
                if b >= 1:
                    c1 = b - 1
                    eng.wait_ge(tanh_ok, 2 * b)
                    v.tensor_scalar(qq, rt, 1.0, None, ALU.add).then_inc(q_read, 1)
                    eng.wait_ge(q_read, b)
                    step(v.reciprocal(qq, qq))
                    v.tensor_scalar(aa, qq, 2.0, -1.0, ALU.mult, ALU.add)
                    eng.wait_ge(sqrt_ok, b)
                    step(v.tensor_tensor(sq, sq, qq, ALU.mult))
                    eng.wait_ge(iu_ok, 2 * b)
                    step(v.tensor_tensor(sq, sq, ig, ALU.mult))
                    if b >= 2:
                        eng.wait_ge(st_ok, 2 * c1)
                    v.tensor_tensor_scan(hh[:, 0, 0:NLAT], aa[:, 0, 0:NLAT], sq[:, 0, 0:NLAT],
                                         vec[:, c1, R_H0:R_H0 + 1], ALU.mult, ALU.add).then_inc(scan_ok, 1)
                    v.tensor_tensor_scan(hh[:, 0, NLAT:], aa[:, 0, NLAT:], sq[:, 0, NLAT:], 0.0, ALU.mult, ALU.add).then_inc(scan_ok, 1)
                    v.tensor_tensor_scan(hh[:, 1, 0:NLAT][:, ::-1], aa[:, 1, 0:NLAT][:, ::-1], sq[:, 1, 0:NLAT][:, ::-1],
                                         vec[:, c1, R_H0 + 1:R_H0 + 2], ALU.mult, ALU.add).then_inc(scan_ok, 1)
                    v.tensor_tensor_scan(hh[:, 1, NLAT:][:, ::-1], aa[:, 1, NLAT:][:, ::-1], sq[:, 1, NLAT:][:, ::-1],
                                         0.0, ALU.mult, ALU.add).then_inc(scan_ok, 1)
                    eng.wait_ge(scan_ok, 4 * b)
                    step(v.tensor_tensor(aa[:, 0], hh[:, 0], hh[:, 1], ALU.add))
                    eng.wait_ge(gel_ok, 2 * b)
                    v.tensor_tensor(hg[:, c1, :], aa[:, 0], gel, ALU.mult).then_inc(hg_ok, 1)
            eng.wait_ge(x_in, 32)
            residual(0, r1, gb, ROUND_RG)
            eng.wait_ge(st_mm, 1)
            v.tensor_copy(st_row[:, :], ps[0:16, 4, 0:P]).then_inc(st_row_ok, 1)
            norm(1, 0)
            turned(1, 0)
            route(0)
            experts(0)

            eng.wait_ge(x_in, 48)
            norm(2, None)
            turned(2, 1)

            def turned_q(t):
                eng.wait_ge(q_mm, t + 1)
                v.tensor_copy(q_t[:, 4:8, t * P:(t + 1) * P], ps[:, 7, :].rearrange("p (h n) -> p h n", h=4)).then_inc(q_dve, 1)

            qn3, qs3, gn3 = (a.rearrange("p (h n) -> p h n", h=NQK) for a in (qn, qs, gains))
            qn4, qs4 = (a.rearrange("p (h f q n) -> p h f q n", h=NQK, f=2, q=2) for a in (qn, qs))
            eng.wait_ge(gains_ok, 1)
            eng.wait_ge(small_in, 16 * 7)
            for t in range(NT):
                z = 3 * (t % 2)
                eng.wait_ge(qsq_ok, 3 * (t + 1))
                step(v.tensor_reduce(ss20[:, 0], qs3, AX.X, ALU.add))
                v.tensor_scalar(ss20[:, 0], ss20[:, 0], 1.0 / HD, EPS, ALU.mult, ALU.add).then_inc(qvar_ok, 1)
                eng.wait_ge(qstd_ok, t + 1)
                step(v.reciprocal(ss20[:, 1], ss20[:, 1]))
                eng.wait_ge(kdup_ok, 2 * (t + 1))
                if t >= 1:
                    turned_q(t - 1)
                for lo, hi, src in ((0, 8, ps[:, z, :]), (8, 16, ps[:, z + 1, :]), (16, 20, ps[:, z + 2, 0:256])):
                    ins = v.tensor_tensor(qn3[:, lo:hi], src.rearrange("p (h n) -> p h n", n=HD),
                                          ss20[:, 1, lo:hi].unsqueeze(2).to_broadcast([P, hi - lo, HD]), ALU.mult)
                    if hi < NQK:
                        step(ins)
                ins.then_inc(qn_read, 1)
                eng.wait_ge(qn_read, t + 1)
                ins = v.tensor_tensor(qn, qn, gains, ALU.mult)
                if t < TL:
                    step(ins)
                    for q in range(2):
                        v.tensor_tensor(qs4[:, :, :, q, :], qn4[:, :, :, 1 - q, :],
                                        tab[:, 1, t].rearrange("p (f q n) -> p f q n", f=2, q=2)[:, :, q, :].unsqueeze(1)
                                        .to_broadcast([P, NQK, 2, HD // 4]), ALU.mult).then_inc(rot_ok, 1)
                    eng.wait_ge(rot_ok, 2 * (t + 1))
                    step(v.tensor_tensor(qn3, qn3, tab[:, 0, t].unsqueeze(1).to_broadcast([P, NQK, HD]), ALU.mult))
                    ins = v.tensor_tensor(qn, qn, qs, ALU.add)
                ins.then_inc(qn_ok, 1)
            turned_q(NT - 1)
            eng.wait_ge(consts, 6)
            eng.wait_ge(sink_ok, 1)
            eng.wait_ge(kv_stored, 32)
            for i in range(NU + 3):
                if i < NU:
                    j, hp = units[i]
                    w, m0 = len(KEYB[j][0]) * P, KEYB[j][1]
                    st = stat[:, i % 4]
                    eng.wait_ge(s_mm, i + 1)
                    if i >= 2:
                        eng.wait_ge(pt_mm, i - 1)
                    for a in range(2):
                        v.tensor_tensor_reduce(out=pm[:, i % 2, a, 0:w], in0=ps[:, 2 * (i % 2) + a, 0:w],
                                               in1=mask[:, m0:m0 + w], scale=1.0, scalar=NEG, op0=ALU.add, op1=ALU.max,
                                               accum_out=st[:, 0, a:a + 1]).then_inc(s_max, 1)
                    eng.wait_ge(s_max, 2 * (i + 1))
                    step(v.scalar_tensor_tensor(out=st[:, 1, :], in0=st[:, 0, :], scalar=-1.0, in1=sinks[:, 1, 2 * hp:2 * hp + 2],
                                                op0=ALU.mult, op1=ALU.min))
                    v.tensor_tensor(st[:, 2, :], sinks[:, 0, 2 * hp:2 * hp + 2], st[:, 1, :], ALU.add).then_inc(nm_ok, 1)
                if 1 <= i <= NU:
                    w = len(KEYB[units[i - 1][0]][0]) * P
                    eng.wait_ge(pt_mm, i)
                    if i >= 3:
                        eng.wait_ge(pv_mm, i - 2)
                    v.tensor_copy(pt[:, (i - 1) % 2, 1, 0:w], ps[:, 5, 0:w]).then_inc(pt_dve, 1)
                if 2 <= i < NU + 2:
                    j, hp = units[i - 2]
                    st = stat[:, (i - 2) % 4]
                    eng.wait_ge(p_ok, 3 * (i - 1))
                    step(v.tensor_tensor(st[:, 5, :], st[:, 3, :], st[:, 4, :], ALU.add))
                    step(v.reciprocal(st[:, 6, :], st[:, 5, :]))
                    eng.wait_ge(pv_mm, i - 1)
                    if j >= 2:
                        eng.wait_ge(ot_mm, j - 1)
                    v.tensor_tensor(gb[:, j % 2, hp * P:(hp + 1) * P].rearrange("p (a n) -> p a n", a=2),
                                    ps[:, 6 + i % 2, 0:P].rearrange("p (a n) -> p a n", a=2),
                                    st[:, 6, :].unsqueeze(2).to_broadcast([P, 2, HD]), ALU.mult).then_inc(o_ok, 1)
                if last_of_tile(i - 3):
                    j = (i - 3) // KB
                    eng.wait_ge(ot_mm, j + 1)
                    v.tensor_copy(feat(r1)[:, 4:8, j * P:(j + 1) * P], ps[:, 5, :].rearrange("p (h n) -> p h n", h=4)).then_inc(ot_dve, 1)
            diagonals(1, diag1)
            residual(1, r2, gb1, ROUND_AT)
            norm(3, 2 * NT)
            turned(3, 1)
            route(1)
            experts(1)


def rope_table():
    t = np.arange(NLAT)
    inv = (np.float32(10000.0) ** (-np.arange(HD // 4, dtype=np.float32) / (HD // 4))).astype(np.float32)
    ar = (t // 64).astype(np.float32)[:, None] * inv
    ac = (t % 64).astype(np.float32)[:, None] * inv
    ang = np.concatenate([ar, ar, ac, ac], axis=1)
    sign = np.repeat(np.array([-1, 1, -1, 1], np.float32), HD // 4)
    return np.stack([np.cos(ang), np.sin(ang) * sign]).astype(np.float32)


def kernel(x_prompt, x_sample, state_rglru, cache_k, cache_v, c, c_ctx, mod_w, mod_b, norm1_g, norm2_g,
           rg_w_in, rg_conv_w, rg_conv_b, rg_w_a, rg_b_a, rg_w_x, rg_b_x, rg_lambda, rg_w_out,
           at_w_qkv, at_q_norm, at_k_norm, at_sink, at_w_o, ft_w, moe_router, moe_w_gate, moe_w_up, moe_w_down):
    import concourse.bacc as bacc
    from concourse.bass_utils import run_bass_kernel_spmd

    ins = {
        "x_all": np.concatenate([np.asarray(x_sample)[0], np.asarray(x_prompt)[0]]),
        "state": np.asarray(state_rglru).reshape(2, D),
        "cache_k": np.asarray(cache_k).reshape(P, NKV * HD), "cache_v": np.asarray(cache_v).reshape(P, NKV * HD),
        "c": np.asarray(c).reshape(1, D), "c_ctx": np.asarray(c_ctx).reshape(1, D),
        "mod_w": np.asarray(mod_w), "mod_b": np.asarray(mod_b).reshape(2 * NMOD, D),
        "norm1_g": np.asarray(norm1_g), "norm2_g": np.asarray(norm2_g),
        "rg_w_in": np.asarray(rg_w_in)[0], "rg_conv_w": np.asarray(rg_conv_w)[0], "rg_conv_b": np.asarray(rg_conv_b),
        "rg_w_a": np.asarray(rg_w_a)[0], "rg_b_a": np.asarray(rg_b_a)[0],
        "rg_w_x": np.asarray(rg_w_x)[0], "rg_b_x": np.asarray(rg_b_x)[0],
        "rg_lambda": np.asarray(rg_lambda)[0], "rg_w_out": np.asarray(rg_w_out)[0],
        "at_w_qkv": np.asarray(at_w_qkv)[0], "at_q_norm": np.asarray(at_q_norm), "at_k_norm": np.asarray(at_k_norm),
        "at_sink": np.asarray(at_sink), "at_w_o": np.asarray(at_w_o)[0], "moe_router": np.asarray(moe_router),
        "moe_w_gate": np.asarray(moe_w_gate), "moe_w_up": np.asarray(moe_w_up), "moe_w_down": np.asarray(moe_w_down),
        "rope": rope_table(),
    }
    outs = {"y_all": (NTOK, D), "new_state": (2, D), "new_k": (NCTX, NKV * HD), "new_v": (NCTX, NKV * HD)}
    nc = bacc.Bacc("TRN2", target_bir_lowering=False, num_devices=1)
    aps = {k: nc.dram_tensor(f"in_{k}", a.shape, F32, kind="ExternalInput").ap() for k, a in ins.items()}
    aps.update({k: nc.dram_tensor(f"out_{k}", s, F32, kind="ExternalOutput").ap() for k, s in outs.items()})
    build(nc, **aps)
    r = run_bass_kernel_spmd(nc, [{f"in_{k}": np.ascontiguousarray(a) for k, a in ins.items()}], core_ids=[0]).results[0]
    y = r["out_y_all"]
    return (y[NLAT:].reshape(1, NCTX, D), y[:NLAT].reshape(1, NLAT, D), r["out_new_state"].reshape(1, 1, 2, D),
            r["out_new_k"].reshape(1, 1, NCTX, NKV, HD), r["out_new_v"].reshape(1, 1, NCTX, NKV, HD))
```

```python
from contextlib import ExitStack

import numpy as np

import concourse.bass as bass
from concourse import mybir

F32 = mybir.dt.float32
F32R = mybir.dt.float32r
U32 = mybir.dt.uint32
ALU = mybir.AluOpType
ACT = mybir.ActivationFunctionType
AX = mybir.AxisListType

P = 128
D = 1024
KB = D // P
NLAT, NCTX = 512, 128
NTOK = NLAT + NCTX
TL = NLAT // P
NT = NTOK // P
NMOD = 6
EPS = 1e-6
NB = 16
RB = D // NB
NH, NKV, HD = 16, 4, 64
NQK = NH + NKV
QKV = (NH + 2 * NKV) * HD
NE = 16
CL, CC = 2 * NLAT // NE, 2 * NCTX // NE
CE = CL + CC
NEG = -1e30

SLOTS, MSLOTS = 12, 8
ROUND_RG, ROUND_AT = 1, 5
MOD_ROUNDS = (0, 2, 3, 4)
ROUNDS = (4, 6)
USES = 12
ESLOTS = NE * USES
HL = 4
EQ = 2 * ESLOTS

R_C, R_CCTX, R_G1, R_G2, R_CW, R_CB, R_BA, R_BX, R_LAM, R_H0, R_MODB = 0, 1, 2, 4, 6, 10, 11, 13, 15, 17, 19
NROWS = R_MODB + 2 * NMOD
UPAD = 2 + NLAT + 2 + NCTX + 1
UC = NLAT + 2 + NCTX
C0 = NLAT + 2


def build(nc, x_all, state, cache_k, cache_v, c, c_ctx, mod_w, mod_b, norm1_g, norm2_g,
          rg_w_in, rg_conv_w, rg_conv_b, rg_w_a, rg_b_a, rg_w_x, rg_b_x, rg_lambda, rg_w_out,
          at_w_qkv, at_q_norm, at_k_norm, at_sink, at_w_o, moe_router, moe_w_gate, moe_w_up,
          moe_w_down, rope, y_all, new_state, new_k, new_v):
    with ExitStack() as ctx:
        def sb(name, shape, dt=F32):
            return ctx.enter_context(nc.sbuf_tensor(name, shape, dt))

        def sem(name):
            return ctx.enter_context(nc.semaphore(name))

        x_mid = nc.dram_tensor("x_mid", (NTOK, D), F32, kind="Internal").ap()
        x_hat = [nc.dram_tensor(f"x_hat{l}", (NTOK, D), F32, kind="Internal").ap() for l in range(2)]
        x_res = (x_mid, y_all)

        ps = ctx.enter_context(nc.psum_tensor("ps", [P, 8, 512], F32))
        ring_at = -(-nc.sbuf_base // 32) * 32
        ring = sb("ring", [P, SLOTS, 2 * D])
        whl = nc.alloc_sbuf_tensor_at("whl", [P, HL, 2, D], F32R, offset=ring_at + 4 * MSLOTS * 2 * D)
        r1_at = ring_at + 4 * SLOTS * 2 * D
        assert nc.sbuf_base == r1_at
        r1 = sb("r1", [P, 5 * D])
        r2 = sb("r2", [P, 5 * D])
        xs_hl = nc.alloc_sbuf_tensor_at("xs_hl", [P, 2, 2, KB, CE], F32R, offset=r1_at)
        hs_hl = nc.alloc_sbuf_tensor_at("hs_hl", [P, 2, KB, CE], F32R, offset=r1_at + 4 * 4 * KB * CE)
        gb = sb("gb", [P, 2, D])
        W = sb("W", [P, 14592])
        ident = sb("ident", [P, P])
        vec = sb("vec", [P, KB, 32])
        mod = sb("mod", [P, 2, NMOD, KB, 2])
        cond = sb("cond", [P, KB, 2])
        amod = sb("amod", [P, 4, KB, 2])
        router = sb("router", [P, 2, KB, NE])
        sp4 = sb("sp4", [P, KB, 2])
        stv = sb("stv", [P, 2, KB])
        st_row = sb("st_row", [16, P])
        sm = sb("sm", [P, 4, 3, 8])
        modraw = sb("modraw", [P, 2, KB, 2])
        mx5 = sb("mx5", [P, 2, 8])
        spt = sb("spt", [P, 6, KB, 2])
        sinks = sb("sinks", [P, 2, NH])
        stat = sb("stat", [P, 4, 8, 2])
        ss20 = sb("ss20", [P, 2, NQK])
        idx_t = sb("idx_t", [CE, NE], U32)
        g_t = sb("g_t", [CE, NE])
        gi = sb("gi", [CE, 1], U32)
        si = sb("si", [CE, 1], U32)
        sg = sb("sg", [CE, 1])

        def tok(t):
            return t[:, :].rearrange("p (t d) -> p t d", t=NT)

        w_tmp = W[:, 6144:7168].rearrange("p (a n) -> p a n", a=2)

        def mod_rows(v):
            src = r1[:, 3 * D:] if v < 5 else W[:, 6144:]
            return src[:, (v % 2) * D:(v % 2 + 1) * D]

        def feat(t):
            return t[:, 0:KB * NTOK].rearrange("p (k n) -> p k n", k=KB)

        off = [0]

        def work(n, at=None):
            if at is not None:
                off[0] = at
            off[0] += n
            assert off[0] <= 14592
            return W[:, off[0] - n:off[0]]

        w_xhat = work(5 * D, 0)
        w_junk = work(D)
        rows = work(D)
        ones = work(P)
        diag = work(2 * D).rearrange("p (s b d) -> p s b d", s=2, b=KB)
        w_junk2 = W[:, 8320:8320 + D]
        upad = work(UPAD + 3, 0)
        ucs = [work(UC) for _ in range(2)]
        rt = work(2 * NTOK).rearrange("p (a n) -> p a n", a=2)
        ig = work(2 * NTOK).rearrange("p (a n) -> p a n", a=2)
        sq = work(2 * NTOK).rearrange("p (a n) -> p a n", a=2)
        qq = work(2 * NTOK).rearrange("p (a n) -> p a n", a=2)
        aa = work(2 * NTOK).rearrange("p (a n) -> p a n", a=2)
        hh = work(2 * NTOK).rearrange("p (a n) -> p a n", a=2)
        gel = work(NTOK)
        bd = work(4 * KB * P).rearrange("p (m c j) -> p m c j", m=4, c=KB)
        q_t = work(KB * NTOK, 0).rearrange("p (h n) -> p h n", h=KB)
        KEYS = NTOK + P
        k_t = work(NKV * KEYS).rearrange("p (g n) -> p g n", g=NKV)
        v_s = work(6 * NKV * HD).rearrange("p (t n) -> p t n", t=6)
        T1 = off[0]
        qn = work(NQK * HD)
        qs = work(NQK * HD)
        gains = work(NQK * HD)
        tab = work(2 * TL * HD).rearrange("p (s t n) -> p s t n", s=2, t=TL)
        kdup = work(NKV * P).rearrange("p (g a n) -> p g a n", g=NKV, a=2)
        pm = work(2 * 2 * 512, T1).rearrange("p (u i n) -> p u i n", u=2, i=2)
        pt = work(2 * 2 * 512).rearrange("p (u i n) -> p u i n", u=2, i=2)
        mask = work(5 * P)
        kc = qn[:, 0:NKV * HD]
        gb1 = work(2 * D, 0).rearrange("p (s d) -> p s d", s=2)
        diag1 = work(2 * D).rearrange("p (s b d) -> p s b d", s=2, b=KB)
        ones1 = work(P)
        xn2 = work(5 * D, 0)
        xg = work(D)
        sil = work(D)
        hid = work(D)
        ob = work(D)
        gg = work(D)
        ex = [work(KB * CE) for _ in range(2)]
        xt = work(KB * CE)
        tk = work(512)
        tv = work(CL)
        ti = W[:, off[0]:off[0] + CL].bitcast(U32)
        work(CL)
        sel = work(2 * CE).rearrange("p (s n) -> p s n", s=2)
        diag2 = W[:, 0:2 * D].rearrange("p (s b d) -> p s b d", s=2, b=KB)
        comb = work(2 * CE).rearrange("p (a n) -> p a n", a=2)
        lg = work(NT * NE).rearrange("p (t n) -> p t n", t=NT)
        assert off[0] <= 14592

        waits_passed = sem("waits_passed")
        slot_ready = [sem(f"slot_ready{s}") for s in range(SLOTS)]
        ring_used, rows_in, x_in, bd_in = sem("ring_used"), sem("rows_in"), sem("x_in"), sem("bd_in")
        small_in, router_in, consts, dve = sem("small_in"), sem("router_in"), sem("consts"), sem("dve")
        pool_s, rows_t, vec_ok, sig_c = sem("pool_s"), sem("rows_t"), sem("vec_ok"), sem("sig_c")
        cond_ok, lam_abs, lam_exp, sp_ok = sem("cond_ok"), sem("lam_abs"), sem("lam_exp"), sem("sp_ok")
        mod_row, mod_tr = sem("mod_row"), sem("mod_tr")
        ig_used = sem("ig_used")
        mod_read, mod_ok, diag_ok, gate_mm = sem("mod_read"), sem("mod_ok"), sem("diag_ok"), sem("gate_mm")
        gate_ok, ssq_act, ssq_ok, var_ok = sem("gate_ok"), sem("ssq_act"), sem("ssq_ok"), sem("var_ok")
        std_ok, xhat_ok, tr_mm, tr_act = sem("std_ok"), sem("xhat_ok"), sem("tr_mm"), sem("tr_act")
        tr_dve, amod_ok, u_mm, u_ok = sem("tr_dve"), sem("amod_ok"), sem("u_mm"), sem("u_ok")
        conv_ok, g_mm, z_mm, sig_ok = sem("conv_ok"), sem("g_mm"), sem("z_mm"), sem("sig_ok")
        tanh_ok, sqrt_ok, gel_ok, iu_ok = sem("tanh_ok"), sem("sqrt_ok"), sem("gel_ok"), sem("iu_ok")
        q_read, scan_ok, hg_ok, st_ok = sem("q_read"), sem("scan_ok"), sem("hg_ok"), sem("st_ok")
        st_mm, st_row_ok, out_mm, out_mul = sem("st_mm"), sem("st_row_ok"), sem("out_mm"), sem("out_mul")
        x1_ok, x1_stored, xh_stored, stored = sem("x1_ok"), sem("x1_stored"), sem("xh_stored"), sem("stored")
        kv_stored, lg_mm, lg_sub, lg_exp = sem("kv_stored"), sem("lg_mm"), sem("lg_sub"), sem("lg_exp")
        aff_ok, aff_mm, tk_set, comb_ok = sem("aff_ok"), sem("aff_mm"), sem("tk_set"), sem("comb_ok")
        comb_mm, route_ok, ex_ok = sem("comb_mm"), sem("route_ok"), sem("ex_ok")
        gathered, scattered, xtr_mm, xt_mul = sem("gathered"), sem("scattered"), sem("xtr_mm"), sem("xt_mul")
        xt_ok, xh_ok, xl_ok, sil_ok = sem("xt_ok"), sem("xh_ok"), sem("xl_ok"), sem("sil_ok")
        h_ok, htr_mm, hh_ok, hl_ok = sem("h_ok"), sem("htr_mm"), sem("hh_ok"), sem("hl_ok")
        whi_ok, wlo_ok, whl_used, y_act = sem("whi_ok"), sem("wlo_ok"), sem("whl_used"), sem("y_act")
        ob_ok, sg_ok, gi_ok, si_ok = sem("ob_ok"), sem("sg_ok"), sem("gi_ok"), sem("si_ok")
        sel_ok, diag2_ok, gg_mm, gg_ok = sem("sel_ok"), sem("diag2_ok"), sem("gg_mm"), sem("gg_ok")
        kdup_ok, rot_ok = sem("kdup_ok"), sem("rot_ok")
        qkv_mm, qsq_ok, qvar_ok, qstd_ok = sem("qkv_mm"), sem("qsq_ok"), sem("qvar_ok"), sem("qstd_ok")
        v_ok, qn_read, qn_ok, q_mm = sem("v_ok"), sem("qn_read"), sem("qn_ok"), sem("q_mm")
        q_act, q_dve, k_mm, k_ok = sem("q_act"), sem("q_dve"), sem("k_mm"), sem("k_ok")
        sink_ok, s_mm, s_max, nm_ok = sem("sink_ok"), sem("s_mm"), sem("s_max"), sem("nm_ok")
        p_ok, pt_mm, pt_act, pt_dve = sem("p_ok"), sem("pt_mm"), sem("pt_act"), sem("pt_dve")
        pv_mm, o_ok, ot_mm, ot_act = sem("pv_mm"), sem("o_ok"), sem("ot_mm"), sem("ot_act")
        ot_dve, gains_ok = sem("ot_dve"), sem("gains_ok")

        KEYB = {0: ([0, 1, 5], 2 * P), 1: ([0, 1, 2, 5], P), 2: ([1, 2, 3, 5], P), 3: ([5, 2, 3], 0), 4: ([4], 0)}
        units = [(j, hp) for j in range(NT) for hp in range(KB)]
        NU = len(units)

        def last_of_tile(i):
            return 0 <= i < NU and i % KB == KB - 1

        def runs(blocks):
            out = []
            for n, b in enumerate(blocks):
                if out and b == out[-1][1] + out[-1][2]:
                    out[-1][2] += 1
                else:
                    out.append([n, b, 1])
            return out

        order = [(rnd, s) for rnd in range(ROUNDS[1]) for s in range(SLOTS) if rnd not in (ROUND_RG, MOD_ROUNDS[1])]
        order[SLOTS:SLOTS] = [(rnd, s) for part in (range(MSLOTS), range(MSLOTS, SLOTS))
                              for rnd in (ROUND_RG, MOD_ROUNDS[1]) for s in part]

        def used(rnd, s):
            return order.index((rnd, s)) + 1

        def ready(rnd, s):
            return 16 * (rnd + 1 + (ESLOTS // MSLOTS if rnd >= ROUNDS[0] and s < MSLOTS else 0))

        def block_of(layer, e, q):
            return e * (2 * USES) + (EQ * layer + 16 + q + 1)

        def steps(eng, body):
            with eng.Fori(0, NE // 2 - 1) as i:
                for par in range(2):
                    body(i * 2 + par, i, par, True, True)
            body(NE - 2, NE // 2 - 1, 0, True, False)
            body(NE - 1, NE // 2 - 1, 1, False, False)

        x_tiles = x_all.rearrange("(t p) d -> p t d", p=P)
        XF = KB * NTOK
        NORMS = ((r2, w_xhat, r1), (r1, r2, xn2), (r2, w_xhat, r1), (r2, r1, xn2))

        block = ctx.enter_context(nc.Block())

        @block.sync
        def _(sp):
            def load(rnd, s, dst, src):
                if rnd == ROUNDS[0] and s < MSLOTS:
                    sp.wait_ge(wlo_ok, 2 * (ESLOTS - MSLOTS + s + 1))
                elif rnd == ROUNDS[0]:
                    sp.wait_ge(whl_used, EQ)
                elif rnd:
                    sp.wait_ge(ring_used, used(rnd - 1, s))
                sp.dma_start(dst, src).then_inc(slot_ready[s], 16)

            def pair(s):
                return ring[:, s, :].rearrange("p (k n) -> p k n", k=2)

            def rows2(w, k2, c0=0):
                return w[k2 * 2 * P:(k2 + 1) * 2 * P, c0:c0 + D].rearrange("(k p) n -> p k n", p=P)

            def load_mod(*vectors):
                for vec_no in vectors:
                    for s in range(4):
                        slot = 4 * (vec_no % 3) + s
                        load(MOD_ROUNDS[vec_no // 3], slot, pair(slot), rows2(mod_w[vec_no // NMOD], s, vec_no % NMOD * D))

            def load_moe(layer):
                w3 = [w[layer].rearrange("e (k p) n -> p (e k) n", p=P) for w in (moe_w_gate, moe_w_up, moe_w_down)]

                def put(slot, w, e, s):
                    sp.dma_start(pair(slot), w3[w][:, bass.ds(e * KB + 2 * s, 2), :]).then_inc(slot_ready[slot], 16)

                for n in range(MSLOTS):
                    sp.wait_ge(ring_used, used(ROUNDS[layer] - 1, n))
                    put(n, n // 4, 0, n % 4)

                def step_loads(e, i, par, more, _):
                    for n in range(USES):
                        if not more and not 4 <= n < 8:
                            continue
                        m = n if more else n - 4
                        sp.wait_ge(wlo_ok, e * (2 * USES) + (EQ * layer + 2 * (m + 1)))
                        put((4 * par + m) % MSLOTS, (0, 2, 1)[n // 4], e + int(n // 4 != 1), n % 4)
                steps(sp, step_loads)

            def store_x(layer, x1):
                sp.wait_ge(x1_ok, 2 * NT * (layer + 1))
                sp.dma_start(x_res[layer].rearrange("(t p) d -> p t d", p=P), tok(x1)).then_inc(x1_stored, 16)

            sp.wait_ge(rows_in, 16 * 11)
            load_mod(0, 1, 2)
            for s in range(KB):
                load(ROUND_RG, s, ring[:, s, :], rg_w_in[s * P:(s + 1) * P, :])
            for s in range(4):
                load(ROUND_RG, KB + s, pair(KB + s), rows2(rg_w_out, s))
            load_mod(3, 4)
            sp.wait_ge(g_mm, KB)
            sp.dma_start(tok(r1)[:, 0:3, :], x_tiles[:, 0:3, :]).then_inc(x_in, 16)
            sp.wait_ge(mod_tr, 5)
            sp.dma_start(tok(r1)[:, 3:NT, :], x_tiles[:, 3:NT, :]).then_inc(x_in, 16)
            load_mod(6, 7, 5)
            store_x(0, r1)
            load_mod(8)
            load_moe(0)
            load_mod(9, 10, 11)
            for s in range(KB):
                load(ROUND_AT, s, ring[:, s, 0:QKV], at_w_qkv[s * P:(s + 1) * P, :])
            for s in range(4):
                load(ROUND_AT, KB + s, pair(KB + s), rows2(at_w_o, s))
            sp.wait_ge(qn_ok, NT)
            sp.dma_start(new_k, qn[:, NH * HD:NQK * HD]).then_inc(kv_stored, 16)
            sp.wait_ge(v_ok, NT)
            sp.dma_start(new_v, v_s[:, TL, :]).then_inc(kv_stored, 16)
            store_x(1, r2)
            load_moe(1)
            sp.wait_ge(st_row_ok, 1)
            sp.dma_start(new_state.rearrange("s (b p) -> (s b) p", p=P), st_row[:, :]).then_inc(stored, 16)
            sp.wait_ge(stored, 16)
            sp.wait_ge(kv_stored, 32)
            sp.wait_ge(x1_stored, 32)
            sp.wait_ge(xh_stored, 32)
            sp.wait_ge(scattered, 16 * 2 * NE)

        @block.gpsimd
        def _(pool):
            n = [0]

            def step(ins):
                n[0] += 1
                ins.then_inc(pool_s, 1)
                pool.wait_ge(pool_s, n[0])

            step(nc.gpsimd.memset(ident[:, :], 0.0))
            nc.gpsimd.affine_select(out=ident[:, :], in_=ident[:, :], compare_op=ALU.not_equal, fill=1.0,
                                    base=0, pattern=[[-1, P]], channel_multiplier=1).then_inc(consts, 1)
            nc.gpsimd.memset(bd, 0.0).then_inc(consts, 1)
            nc.gpsimd.memset(ones, 1.0).then_inc(consts, 1)

            def mod_bias(v):
                pool.wait_ge(mod_read, v + 1)
                nc.gpsimd.tensor_tensor(mod[:, v // NMOD, v % NMOD], modraw[:, v % 2],
                                        vec[:, :, R_MODB + v:R_MODB + v + 1].to_broadcast([P, KB, 2]),
                                        ALU.add).then_inc(mod_ok, 1)

            pool.wait_ge(vec_ok, 1)
            for v in range(3):
                mod_bias(v)
            pool.wait_ge(tr_mm, 2 * KB)
            nc.gpsimd.memset(upad, 0.0).then_inc(consts, 1)
            for b in range(KB):
                uc = ucs[b % 2]
                pool.wait_ge(sig_ok, 8 * (b + 1))
                pool.wait_ge(conv_ok, b + 1)
                nc.gpsimd.tensor_tensor(ig[:, :, 0:NLAT], ig[:, :, 0:NLAT],
                                        uc[:, 0:NLAT].unsqueeze(1).to_broadcast([P, 2, NLAT]), ALU.mult).then_inc(iu_ok, 1)
                nc.gpsimd.tensor_tensor(ig[:, :, NLAT:], ig[:, :, NLAT:],
                                        uc[:, C0:].unsqueeze(1).to_broadcast([P, 2, NCTX]), ALU.mult).then_inc(iu_ok, 1)
                pool.wait_ge(scan_ok, 4 * (b + 1))
                nc.gpsimd.tensor_copy(stv[:, 0, b:b + 1], hh[:, 0, NTOK - 1:NTOK]).then_inc(st_ok, 1)
                nc.gpsimd.tensor_copy(stv[:, 1, b:b + 1], hh[:, 1, NLAT:NLAT + 1]).then_inc(st_ok, 1)
            for v in range(3, 5):
                mod_bias(v)

            def experts(layer):
                base = layer * NE
                pool.wait_ge(x1_ok, 2 * NT * (layer + 1))
                nc.gpsimd.memset(tk[0:48, :], -1.0).then_inc(tk_set, 1)
                pool.wait_ge(amod_ok, 2 * layer + 2)
                if layer == 0:
                    mod_bias(5)
                pool.wait_ge(mod_ok, NMOD * (layer + 1))
                for s, (lo, hi) in enumerate(((0, CL), (CL, CE))):
                    nc.gpsimd.memset(sel[:, s, lo:hi], 1.0).then_inc(sel_ok, 1)
                    nc.gpsimd.memset(sel[:, 1 - s, lo:hi], 0.0).then_inc(sel_ok, 1)
                for m, src in enumerate((amod[:, 2 * layer + 1], mod[:, layer, 3])):
                    nc.gpsimd.tensor_copy(ex[m].rearrange("p (k n) -> p k n", k=KB)[:, :, 0:CL], src[:, :, 0:1].to_broadcast([P, KB, CL])).then_inc(ex_ok, 1)
                    nc.gpsimd.tensor_copy(ex[m].rearrange("p (k n) -> p k n", k=KB)[:, :, CL:CE], src[:, :, 1:2].to_broadcast([P, KB, CC])).then_inc(ex_ok, 1)
                pool.wait_ge(lg_mm, layer + 1)
                for s in range(2):
                    nc.gpsimd.tensor_tensor(diag2[:, s], ident[:, :].unsqueeze(1).to_broadcast([P, KB, P]),
                                            mod[:, layer, 5, :, s:s + 1].to_broadcast([P, KB, P]), ALU.mult).then_inc(diag2_ok, 1)
                if layer == 0:
                    for v in range(6, 9):
                        mod_bias(v)
                pool.wait_ge(route_ok, 2 * (layer + 1))
                pool.wait_ge(xh_stored, 16 * (layer + 1))
                pool.wait_ge(x1_stored, 16 * (layer + 1))

                def gather():
                    nc.gpsimd.indirect_dma_start(xg[0:CE, :], None, x_hat[layer],
                                                 bass.IndirectOffsetOnAxis(ap=gi[:, 0:1], axis=0)).then_inc(gathered, 16)

                def passed():
                    pool.sem_inc(waits_passed, 1)

                def scatter():
                    nc.gpsimd.indirect_dma_start(x_res[layer], bass.IndirectOffsetOnAxis(ap=si[:, 0:1], axis=0), ob[0:CE, :],
                                                 None, compute_op=ALU.add).then_inc(scattered, 16)

                def next_rows(e):
                    if not isinstance(e, int) or e:
                        pool.wait_ge(gathered, e * 16 + 16 * base)
                        pool.wait_ge(xtr_mm, e + base)
                    nc.gpsimd.tensor_copy(gi[:, :], idx_t[:, bass.ds(e, 1)]).then_inc(gi_ok, 1)
                    pool.wait_ge(gi_ok, e + (base + 1))
                    passed()
                    gather()

                def body(e, i, par, more, rows_left):
                    nc.gpsimd.tensor_copy(sg[:, :], g_t[:, bass.ds(e, 1)]).then_inc(sg_ok, 1)
                    nc.gpsimd.tensor_copy(si[:, :], idx_t[:, bass.ds(e, 1)]).then_inc(si_ok, 1)
                    if rows_left:
                        next_rows(e + 2)
                    pool.wait_ge(y_act, e + (base + 1))
                    nc.gpsimd.tensor_tensor(ob[0:CE, :], ob[0:CE, :], gg[0:CE, :], ALU.mult).then_inc(ob_ok, 1)
                    pool.wait_ge(ob_ok, e + (base + 1))
                    pool.wait_ge(si_ok, e + (base + 1))
                    passed()
                    scatter()
                    pool.wait_ge(scattered, e * 16 + 16 * (base + 1))

                next_rows(0)
                next_rows(1)
                pool.wait_ge(gg_ok, layer + 1)
                steps(pool, body)

            experts(0)
            for v in range(9, 12):
                mod_bias(v)
            pool.wait_ge(small_in, 16 * 7)
            for a in range(2):
                nc.gpsimd.tensor_copy(kdup[:, :, a, :], kc.rearrange("p (g n) -> p g n", g=NKV)).then_inc(kdup_ok, 1)
            nc.gpsimd.tensor_scalar(gains[:, 0:NH * HD], gains[:, 0:NH * HD], float(HD) ** -0.5, None, ALU.mult).then_inc(gains_ok, 1)
            nc.gpsimd.tensor_scalar(sinks[:, 1, :], sinks[:, 0, :], -1.0, None, ALU.mult).then_inc(sink_ok, 1)
            for t in range(NT):
                pool.wait_ge(qn_ok, t + 1)
                pool.wait_ge(k_mm, t + 1)
                for a in range(2):
                    nc.gpsimd.tensor_copy(kdup[:, :, a, :], qn[:, NH * HD:].rearrange("p (g n) -> p g n", g=NKV)).then_inc(kdup_ok, 1)
            pool.wait_ge(k_mm, NT + 1)
            pool.wait_ge(q_mm, NT)
            step(nc.gpsimd.memset(mask, 0.0))
            nc.gpsimd.affine_select(out=mask[:, P:2 * P], in_=mask[:, P:2 * P], compare_op=ALU.is_ge, fill=NEG,
                                    base=0, pattern=[[1, P]], channel_multiplier=-1).then_inc(consts, 1)
            nc.gpsimd.affine_select(out=mask[:, 3 * P:4 * P], in_=mask[:, 3 * P:4 * P], compare_op=ALU.is_ge, fill=NEG,
                                    base=0, pattern=[[-1, P]], channel_multiplier=1).then_inc(consts, 1)
            pool.wait_ge(s_mm, NU)
            nc.gpsimd.memset(ones1, 1.0).then_inc(consts, 1)
            experts(1)

        @block.tensor
        def _(pe):
            def wait_slot(rnd, s):
                pe.wait_ge(slot_ready[s], ready(rnd, s))

            def modulation(*vectors):
                def turn_row(v):
                    pe.wait_ge(mod_row, v + 1)
                    if v:
                        pe.wait_ge(mod_read, v)
                    for b in range(KB):
                        mm = nc.tensor.transpose(ps[:, 2, 2 * b:2 * b + 2], mod_rows(v)[0:2, b * P:(b + 1) * P], ident[0:2, 0:2])
                    mm.then_inc(mod_tr, 1)

                for v in vectors:
                    if v:
                        pe.wait_ge(mod_row, v)
                    for s in range(4):
                        slot = 4 * (v % 3) + s
                        wait_slot(MOD_ROUNDS[v // 3], slot)
                        for k in range(2):
                            for h in range(2):
                                mm = nc.tensor.matmul(ps[0:2, 6 + h, :], cond[:, 2 * s + k, :],
                                                      ring[:, slot, k * D + h * 512:k * D + (h + 1) * 512],
                                                      start=(s + k == 0), stop=(s == 3 and k == 1))
                        mm.then_inc(ring_used, 1)
                    if v > vectors[0]:
                        turn_row(v - 1)
                turn_row(vectors[-1])

            def gate_rows(layer, src_ones, src_diag):
                for s in range(2):
                    pe.wait_ge(diag_ok, 2 * layer + s + 1)
                    for n in range(2):
                        mm = nc.tensor.matmul(ps[:, 4 + 2 * s + n, :], src_ones, src_diag[:, s, 4 * n:4 * n + 4, :],
                                              start=True, stop=True)
                    mm.then_inc(gate_mm, 1)

            def turn(phase, route=None):
                xh, n0 = tok(NORMS[phase][1]), KB * phase
                pe.wait_ge(xhat_ok, NT * (phase + 1))
                pe.wait_ge(router_in, 32)
                for b in range(KB + 1):
                    if b < KB:
                        if b >= 2:
                            pe.wait_ge(tr_act, n0 + b - 1)
                            pe.wait_ge(tr_dve, n0 + b - 1)
                        for t in range(TL):
                            mm = nc.tensor.transpose(ps[:, b % 2, t * P:(t + 1) * P], xh[:, t, b * P:(b + 1) * P], ident[:, :])
                        mm.then_inc(tr_mm, 1)
                        nc.tensor.transpose(ps[:, 2 + b % 2, 0:P], xh[:, TL, b * P:(b + 1) * P], ident[:, :]).then_inc(tr_mm, 1)
                    if route is not None and b >= 1:
                        k = b - 1
                        pe.wait_ge(tr_act, n0 + k + 1)
                        pe.wait_ge(tr_dve, n0 + k + 1)
                        for t in range(NT):
                            mm = nc.tensor.matmul(ps[:, 4, t * NE:(t + 1) * NE], feat(xn2)[:, k, t * P:(t + 1) * P],
                                                  router[:, route, k, :], start=(k == 0 and t == 0),
                                                  stop=(k == KB - 1), skip_group_check=True)
                if route is not None:
                    mm.then_inc(lg_mm, 1)

            def mixer_out(layer, rnd, src):
                for t in range(NT):
                    if t >= 2:
                        pe.wait_ge(out_mul, 2 * (NT * layer + t - 1))
                    for n in range(2):
                        for k in range(KB):
                            if t == 0 and n == 0 and k % 2 == 0:
                                wait_slot(rnd, KB + k // 2)
                            mm = nc.tensor.matmul(ps[:, 2 * (t % 2) + n, :], feat(src)[:, k, t * P:(t + 1) * P],
                                                  ring[:, KB + k // 2, (k % 2) * D + n * 512:(k % 2) * D + (n + 1) * 512],
                                                  start=(k == 0), stop=(k == KB - 1))
                        if t == NT - 1 and n == 1:
                            mm.then_inc(ring_used, 4)
                        else:
                            mm.then_inc(out_mm, 1)

            def routes(layer):
                pe.wait_ge(aff_ok, layer + 1)
                for t in range(TL):
                    nc.tensor.transpose(ps[0:NE, 5, t * P:(t + 1) * P], lg[:, t, :], ident[:, :])
                nc.tensor.transpose(ps[0:NE, 3, 0:P], lg[:, TL, :], ident[:, :]).then_inc(aff_mm, 1)

            def chosen(layer):
                pe.wait_ge(comb_ok, 4 * (layer + 1))
                nc.tensor.transpose(ps[0:CE, 4, 0:NE], comb[0:NE, 0, :], ident[0:NE, 0:NE])
                nc.tensor.transpose(ps[0:CE, 4, NE:2 * NE], comb[0:NE, 1, :], ident[0:NE, 0:NE]).then_inc(comb_mm, 1)

            def gate_columns(layer):
                pe.wait_ge(diag2_ok, 2 * (layer + 1))
                pe.wait_ge(sel_ok, 4 * (layer + 1))
                for n in range(2):
                    for s in range(2):
                        mm = nc.tensor.matmul(ps[0:CE, n, :], sel[:, s, :], diag2[:, s, 4 * n:4 * n + 4, :],
                                              start=(s == 0), stop=(s == 1))
                mm.then_inc(gg_mm, 1)

            def experts(layer):
                base = layer * NE

                def product(e, q0, bank, xhl):
                    for k in range(KB):
                        w = whl[:, (q0 + k) % HL]
                        pe.wait_ge(whi_ok, block_of(layer, e, q0 + k))
                        for part in range(2):
                            for n in range(2):
                                nc.tensor.matmul(ps[0:CE, bank + n, :], xhl[:, part, k, :], w[:, 0, n * 512:(n + 1) * 512],
                                                 start=(k == 0 and part == 0), stop=False)
                        pe.wait_ge(wlo_ok, block_of(layer, e, q0 + k))
                        for n in range(2):
                            mm = nc.tensor.matmul(ps[0:CE, bank + n, :], xhl[:, 0, k, :], w[:, 1, n * 512:(n + 1) * 512],
                                                  start=False, stop=(k == KB - 1))
                        mm.then_inc(whl_used, 1)
                        yield k

                def run(blocks):
                    for _ in blocks:
                        pass

                def x_turn(e):
                    pe.wait_ge(gathered, e * 16 + 16 * (base + 1))
                    if not isinstance(e, int) or e >= 2:
                        pe.wait_ge(hh_ok, e + (base - 1))
                        pe.wait_ge(hl_ok, e + (base - 1))
                    elif e:
                        pe.wait_ge(xt_mul, base + 1)
                    for b in range(KB):
                        mm = nc.tensor.transpose(ps[:, 6 + b // 4, (b % 4) * CE:(b % 4 + 1) * CE], xg[0:CE, b * P:(b + 1) * P],
                                                 ident[0:CE, 0:CE])
                    mm.then_inc(xtr_mm, 1)

                def h_turn(e, read):
                    pe.wait_ge(h_ok, e + (base + 1))
                    pe.wait_ge(xt_mul, read)
                    for b in range(KB):
                        mm = nc.tensor.transpose(ps[:, 6 + b // 4, (b % 4) * CE:(b % 4 + 1) * CE], hid[0:CE, b * P:(b + 1) * P],
                                                 ident[0:CE, 0:CE])
                    mm.then_inc(htr_mm, 1)

                def gate_up(e, q0, bank, par):
                    return product(e, q0, bank, xs_hl[:, 1 - par])

                def body(e, i, par, more, rows_left):
                    if more:
                        pe.wait_ge(xh_ok, e + (base + 2))
                        pe.wait_ge(xl_ok, e + (base + 2))
                        pe.wait_ge(sil_ok, e + (base + 1))
                        for k in gate_up(e, 0, 0, par):
                            if k == 2:
                                h_turn(e, e + (base + 2))
                    else:
                        h_turn(e, base + NE)
                    pe.wait_ge(hh_ok, e + (base + 1))
                    pe.wait_ge(hl_ok, e + (base + 1))
                    run(product(e, 8 if more else 0, 4, hs_hl))
                    if rows_left:
                        x_turn(e + 2)
                    if more:
                        pe.wait_ge(h_ok, e + (base + 1))
                        run(gate_up(e, 16, 2, par))

                pe.wait_ge(gate_ok, 4 * (layer + 1))
                x_turn(0)
                pe.wait_ge(xh_ok, base + 1)
                pe.wait_ge(xl_ok, base + 1)
                pe.wait_ge(gg_ok, layer + 1)
                run(gate_up(-1, 8, 0, 1))
                x_turn(1)
                run(gate_up(-1, 16, 2, 1))
                steps(pe, body)

            pe.wait_ge(consts, 1)
            pe.wait_ge(rows_in, 16 * 11)
            for b in range(KB):
                mm = nc.tensor.transpose(ps[:, 0, b * 32:b * 32 + NROWS], rows[0:NROWS, b * P:(b + 1) * P],
                                         ident[0:NROWS, 0:NROWS])
            mm.then_inc(rows_t, 1)
            pe.wait_ge(cond_ok, 1)
            modulation(0, 1, 2)
            pe.wait_ge(mod_read, 3)
            turn(0)
            pe.wait_ge(consts, 3)
            pe.wait_ge(mod_read, 3)
            gate_rows(0, ones, diag)
            pe.wait_ge(tr_act, KB)
            pe.wait_ge(tr_dve, KB)
            pe.wait_ge(gate_ok, 4)
            xf = feat(r1)

            def project(cols, lat, con, gates_read, done, last=False):
                for k in range(KB):
                    nc.tensor.matmul(ps[:, lat, :], ring[:, k, cols:cols + P], xf[:, k, 0:NLAT], start=(k == 0), stop=(k == KB - 1))
                if gates_read:
                    pe.wait_ge(sig_ok, gates_read)
                for k in range(KB):
                    mm = nc.tensor.matmul(ps[:, con, 0:P], ring[:, k, cols:cols + P], xf[:, k, NLAT:], start=(k == 0), stop=(k == KB - 1))
                    if last and k < KB - 1:
                        mm.then_inc(ring_used, 1)
                mm.then_inc(done, 1)

            for b in range(KB + 1):
                if b < KB:
                    if b == 0:
                        for s in range(KB):
                            wait_slot(ROUND_RG, s)
                    if b >= 1:
                        pe.wait_ge(u_ok, 2 * b)
                    project(D + b * P, 0, 1, 0, u_mm)
                if b >= 1:
                    pe.wait_ge(conv_ok, b)
                    pe.wait_ge(bd_in, 16 * 8)
                    pe.wait_ge(gel_ok, 2 * b)
                    if b >= 2:
                        pe.wait_ge(sig_ok, 8 * (b - 1))
                    for m in range(4):
                        nc.tensor.matmul(ps[:, 4 + m, :], bd[:, m, b - 1, :], ucs[(b - 1) % 2][:, 0:NLAT], start=True, stop=True)
                        mm = nc.tensor.matmul(ps[:, 3, m * P:(m + 1) * P], bd[:, m, b - 1, :], ucs[(b - 1) % 2][:, C0:],
                                              start=True, stop=True)
                        if b == KB and m == 0:
                            mm.then_inc(ring_used, 1)
                    mm.then_inc(z_mm, 1)
                if b < KB:
                    if b >= 1:
                        pe.wait_ge(gel_ok, 2 * b)
                    project(b * P, 2, 3, 8 * b - 4 if b else 0, g_mm, b == KB - 1)
            pe.wait_ge(sig_ok, 8 * KB)
            pe.wait_ge(gel_ok, 2 * KB)
            modulation(3, 4)
            pe.wait_ge(mod_read, 5)
            pe.wait_ge(hg_ok, KB)
            mixer_out(0, ROUND_RG, r2)
            pe.wait_ge(st_ok, 2 * KB)
            nc.tensor.transpose(ps[0:16, 4, 0:P], stv[:, :, :].rearrange("p s b -> p (s b)"), ident[:, :]).then_inc(st_mm, 1)
            pe.wait_ge(st_row_ok, 1)
            turn(1, 0)
            routes(0)
            modulation(5)
            gate_columns(0)
            modulation(6, 7, 8)
            chosen(0)
            experts(0)

            def turn_k(n, bank):
                pe.wait_ge(kdup_ok, 2 * (n + 1))
                for g in range(NKV):
                    mm = nc.tensor.transpose(ps[:, bank, g * P:(g + 1) * P], kdup[:, g].rearrange("p a n -> p (a n)"), ident[:, :])
                mm.then_inc(k_mm, 1)

            modulation(9, 10)
            pe.wait_ge(mod_read, 11)
            turn(2)
            pe.wait_ge(tr_act, 3 * KB)
            pe.wait_ge(tr_dve, 3 * KB)
            modulation(11)
            pe.wait_ge(tr_act, 3 * KB)
            pe.wait_ge(tr_dve, 3 * KB)
            pe.wait_ge(mod_row, 2 * NMOD)
            pe.wait_ge(mod_read, 2 * NMOD)
            turn_k(0, 6)

            def turn_q(t):
                pe.wait_ge(qn_ok, t + 1)
                pe.wait_ge(k_ok, t + 1)
                if t >= 1:
                    pe.wait_ge(q_dve, t)
                for h in range(KB):
                    mm = nc.tensor.transpose(ps[:, 6 + h // 4, (h % 4) * P:(h % 4 + 1) * P], qn[:, h * P:(h + 1) * P], ident[:, :])
                mm.then_inc(q_mm, 1)
                pe.wait_ge(q_act, t + 1)
                turn_k(t + 1, 6)

            for t in range(NT):
                if t >= 2:
                    pe.wait_ge(qn_read, t - 1)
                    pe.wait_ge(v_ok, t - 1)
                for k in range(KB):
                    if t == 0:
                        wait_slot(ROUND_AT, k)
                    for n in range(3):
                        mm = nc.tensor.matmul(ps[:, 3 * (t % 2) + n, :], xf[:, k, t * P:(t + 1) * P],
                                              ring[:, k, n * 512:(n + 1) * 512], start=(k == 0), stop=(k == KB - 1))
                if t == NT - 1:
                    mm.then_inc(ring_used, KB)
                else:
                    mm.then_inc(qkv_mm, 1)
                if t >= 1:
                    turn_q(t - 1)
            turn_q(NT - 1)
            pe.wait_ge(k_ok, NT + 1)
            pe.wait_ge(q_dve, NT)
            pe.wait_ge(qn_read, NT)
            pe.wait_ge(v_ok, NT)
            for i in range(NU + 3):
                if i < NU:
                    j, hp = units[i]
                    if i >= 2:
                        pe.wait_ge(s_max, 2 * (i - 1))
                    for a in range(2):
                        for n, b0, m in runs(KEYB[j][0]):
                            mm = nc.tensor.matmul(ps[:, 2 * (i % 2) + a, n * P:(n + m) * P],
                                                  q_t[a * HD:(a + 1) * HD, hp, j * P:(j + 1) * P],
                                                  k_t[a * HD:(a + 1) * HD, hp // 2, b0 * P:(b0 + m) * P], start=True, stop=True)
                    mm.then_inc(s_mm, 1)
                if 1 <= i <= NU:
                    j, hp = units[i - 1]
                    pe.wait_ge(p_ok, 3 * i)
                    if i >= 2:
                        pe.wait_ge(pt_act, i - 1)
                        pe.wait_ge(pt_dve, i - 1)
                    if last_of_tile(i - 4):
                        pe.wait_ge(ot_act, (i - 4) // KB + 1)
                        pe.wait_ge(ot_dve, (i - 4) // KB + 1)
                    for a in range(2):
                        for n in range(len(KEYB[j][0])):
                            mm = nc.tensor.transpose(ps[:, 4 + a, n * P:(n + 1) * P], pm[:, (i - 1) % 2, a, n * P:(n + 1) * P], ident[:, :])
                    mm.then_inc(pt_mm, 1)
                if 2 <= i < NU + 2:
                    j, hp = units[i - 2]
                    pe.wait_ge(pt_act, i - 1)
                    pe.wait_ge(pt_dve, i - 1)
                    if i >= 4:
                        pe.wait_ge(o_ok, i - 3)
                    for a in range(2):
                        for n, b in enumerate(KEYB[j][0]):
                            mm = nc.tensor.matmul(ps[:, 6 + i % 2, a * HD:(a + 1) * HD], pt[:, i % 2, a, n * P:(n + 1) * P],
                                                  v_s[:, b, (hp // 2) * HD:(hp // 2 + 1) * HD], start=(n == 0),
                                                  stop=(n == len(KEYB[j][0]) - 1))
                    mm.then_inc(pv_mm, 1)
                if last_of_tile(i - 3):
                    j = (i - 3) // KB
                    pe.wait_ge(o_ok, KB * (j + 1))
                    if i <= NU:
                        pe.wait_ge(pt_act, i)
                        pe.wait_ge(pt_dve, i)
                    for b in range(KB):
                        mm = nc.tensor.transpose(ps[:, 4 + b // 4, (b % 4) * P:(b % 4 + 1) * P], gb[:, j % 2, b * P:(b + 1) * P], ident[:, :])
                    mm.then_inc(ot_mm, 1)
            pe.wait_ge(ot_act, NT)
            pe.wait_ge(ot_dve, NT)
            pe.wait_ge(consts, 7)
            gate_rows(1, ones1, diag1)
            mixer_out(1, ROUND_AT, r1)
            turn(3, 1)
            routes(1)
            gate_columns(1)
            chosen(1)
            experts(1)

        @block.scalar
        def _(act):
            def copy(out, in_, done, n=1):
                nc.scalar.activation(out, in_, ACT.Copy).then_inc(done, n)

            def squares(phase, x_ready):
                for t in range(3):
                    if x_ready is not None:
                        act.wait_ge(x1_ok, x_ready + 2 * (t + 1))
                    nc.scalar.activation(w_junk, tok(NORMS[phase][0])[:, t, :], ACT.Square,
                                         accum_out=sm[:, phase, 0, t:t + 1]).then_inc(ssq_act, 1)
                    act.wait_ge(ssq_act, 3 * phase + t + 1)
                act.wait_ge(var_ok, phase + 1)
                nc.scalar.activation(sm[:, phase, 1, 0:NT], sm[:, phase, 0, 0:NT], ACT.Sqrt).then_inc(std_ok, 1)

            def turned(phase, layer):
                out = feat(NORMS[phase][2])
                act.wait_ge(amod_ok, phase + 1)
                for b in range(KB):
                    act.wait_ge(tr_mm, 2 * (KB * phase + b) + 2 - (b + 1) % 2)
                    src, cols, st = ((ps[:, b % 2, :], slice(0, NLAT), 0) if b % 2 == 0
                                     else (ps[:, 2 + b % 2, 0:P], slice(NLAT, NTOK), 1))
                    nc.scalar.activation(out[:, b, cols], src, ACT.Identity, scale=amod[:, phase, b, st:st + 1],
                                         bias=mod[:, layer, 3 * (phase % 2), b, st:st + 1]).then_inc(tr_act, 1)

            def mod_reads(vs, between=None):
                def turned_row(v):
                    act.wait_ge(mod_tr, v + 1)
                    if v >= 2:
                        act.wait_ge(mod_ok, v - 1)
                    copy(modraw[:, v % 2].rearrange("p b s -> p (b s)"), ps[:, 2, 0:2 * KB], mod_read)

                for v in vs:
                    act.wait_ge(ring_used, used(MOD_ROUNDS[v // 3], 4 * (v % 3) + 3))
                    copy(mod_rows(v)[0:2, :].rearrange("p (h n) -> p h n", h=2), ps[0:2, 6:8, :], mod_row)
                    if between is not None and v == vs[0]:
                        between()
                    if v > vs[0]:
                        turned_row(v - 1)
                turned_row(vs[-1])

            def gate_copy(layer, out):
                for s in range(2):
                    act.wait_ge(gate_mm, 2 * layer + s + 1)
                    for n in range(2):
                        copy(out[:, s, n * 512:(n + 1) * 512], ps[:, 4 + 2 * s + n, :], gate_ok)

            def softmax(layer):
                act.wait_ge(lg_sub, layer + 1)
                nc.scalar.activation(lg, lg, ACT.Exp).then_inc(lg_exp, 1)

            def store_xhat(layer):
                act.wait_ge(xhat_ok, NT * (2 * layer + 2))
                act.dma_start(x_hat[layer].rearrange("(t p) d -> p t d", p=P), tok(NORMS[2 * layer + 1][1])).then_inc(xh_stored, 16)

            def gate_columns(layer):
                act.wait_ge(gg_mm, layer + 1)
                copy(gg[0:CE, :].rearrange("p (h n) -> p h n", h=2), ps[0:CE, 0:2, :], gg_ok)

            def experts(layer):
                base = layer * NE
                act.wait_ge(ring_used, used(ROUNDS[layer] - 1, SLOTS - 1))

                def high(e, i, par, q):
                    n = 8 + USES * par + q // 2 if e is not None else q // 2 - 4
                    slot = n % MSLOTS
                    if q % 2 == 0:
                        act.wait_ge(slot_ready[slot], i * (16 * 2 * USES // MSLOTS)
                                    + 16 * (ROUNDS[layer] + ESLOTS // MSLOTS * layer + n // MSLOTS + 1))
                    if n >= HL // 2:
                        act.wait_ge(whl_used, block_of(layer, -1 if e is None else e, q) - HL)
                    nc.scalar.activation(whl[:, q % HL, 0, :], ring[:, slot, (q % 2) * D:(q % 2 + 1) * D], ACT.Copy).then_inc(whi_ok, 1)

                def x_high(e, buf):
                    act.wait_ge(xt_ok, e + (base + 1))
                    copy(xs_hl[:, buf, 0].rearrange("p k n -> p (k n)"), xt, xh_ok)

                def silu(e):
                    if base or not isinstance(e, int) or e:
                        act.wait_ge(h_ok, e + base)
                    nc.scalar.activation(sil[0:CE, :].rearrange("p (h n) -> p h n", h=2), ps[0:CE, 0:2, :], ACT.Silu).then_inc(sil_ok, 1)

                def h_high(e):
                    act.wait_ge(htr_mm, e + (base + 1))
                    copy(hs_hl[:, 0].rearrange("p (h m) n -> p h (m n)", h=2), ps[:, 6:8, 0:4 * CE], hh_ok)

                def output(e):
                    act.wait_ge(sg_ok, e + (base + 1))
                    nc.scalar.activation(ob[0:CE, :].rearrange("p (h n) -> p h n", h=2), ps[0:CE, 4:6, :], ACT.Copy,
                                         scale=sg[:, 0:1]).then_inc(y_act, 1)

                def body(e, i, par, more, rows_left):
                    if not more:
                        for q in range(8):
                            high(e, i, par, q)
                            if q == 3:
                                h_high(e)
                        act.wait_ge(whl_used, block_of(layer, e, 7))
                        output(e)
                        return
                    for q in range(2 * USES):
                        high(e, i, par, q)
                        if q == 6:
                            h_high(e)
                        if q == 12:
                            silu(e + 1)
                        if q == 20:
                            output(e)
                        if q == 21 and rows_left:
                            x_high(e + 2, par)

                for q in range(8, 2 * USES):
                    high(None, 0, 1, q)
                    if q == 11:
                        x_high(0, 0)
                    if q == 20:
                        silu(0)
                    if q == 21:
                        x_high(1, 1)
                steps(act, body)

            vecs = ((R_C, c), (R_CCTX, c_ctx), (R_G1, norm1_g), (R_G2, norm2_g), (R_CW, rg_conv_w), (R_CB, rg_conv_b),
                    (R_BA, rg_b_a), (R_BX, rg_b_x), (R_LAM, rg_lambda), (R_H0, state), (R_MODB, mod_b))
            for r, v in vecs:
                act.dma_start(rows[r:r + v.shape[0], :], v).then_inc(rows_in, 16)
            act.dma_start(tok(r2), x_tiles).then_inc(x_in, 16)
            for l in range(2):
                act.dma_start(router[:, l], moe_router[l].rearrange("(k p) e -> p k e", p=P)).then_inc(router_in, 16)
            act.wait_ge(consts, 2)
            for m, w in enumerate((rg_w_a[0], rg_w_a[1], rg_w_x[0], rg_w_x[1])):
                for h in range(2):
                    act.dma_start(bd[h * RB:(h + 1) * RB, m, :, h * RB:(h + 1) * RB],
                                  w.rearrange("(c h) i j -> h i c j", h=2)[h]).then_inc(bd_in, 16)
            act.wait_ge(vec_ok, 1)
            nc.scalar.activation(cond[:, :, :], vec[:, :, R_C:R_C + 2], ACT.Sigmoid).then_inc(sig_c, 1)
            act.wait_ge(lam_abs, 1)
            nc.scalar.activation(spt[:, 3], spt[:, 1], ACT.Exp, scale=-1.0).then_inc(lam_exp, 1)
            act.wait_ge(x_in, 16)
            squares(0, None)
            mod_reads(range(3))
            turned(0, 0)
            gate_copy(0, gb)

            act.wait_ge(consts, 4)
            for b in range(KB + 1):
                if b < KB:
                    act.wait_ge(u_mm, b + 1)
                    if b >= 1:
                        act.wait_ge(conv_ok, b)
                    copy(upad[:, 2:2 + NLAT], ps[:, 0, :], u_ok)
                    copy(upad[:, 4 + NLAT:4 + NLAT + NCTX], ps[:, 1, 0:P], u_ok)
                if b >= 1:
                    c1 = b - 1
                    act.wait_ge(z_mm, b)
                    if b >= 2:
                        act.wait_ge(q_read, c1)
                        act.wait_ge(ig_used, c1)
                    for cols in (slice(NLAT, NTOK), slice(0, NLAT)):
                        for m, row in enumerate((R_BA, R_BA + 1, R_BX, R_BX + 1)):
                            nc.scalar.activation((rt, ig)[m // 2][:, m % 2, cols],
                                                 ps[:, 3, m * P:(m + 1) * P] if cols.start else ps[:, 4 + m, :],
                                                 ACT.Sigmoid, bias=vec[:, c1, row:row + 1]).then_inc(sig_ok, 1)
                    act.wait_ge(sig_ok, 8 * b)
                    act.wait_ge(sp_ok, 1)
                    for s in range(2):
                        nc.scalar.activation(rt[:, s], rt[:, s], ACT.Tanh, scale=sp4[:, c1, s:s + 1]).then_inc(tanh_ok, 1)
                    act.wait_ge(tanh_ok, 2 * b)
                    if b >= 2:
                        act.wait_ge(scan_ok, 4 * c1)
                    nc.scalar.activation(sq, rt, ACT.Sqrt, scale=4.0).then_inc(sqrt_ok, 1)
                if b < KB:
                    act.wait_ge(g_mm, b + 1)
                    if b >= 1:
                        act.wait_ge(hg_ok, b)
                    nc.scalar.activation(gel[:, 0:NLAT], ps[:, 2, :], ACT.Gelu_apprx_tanh).then_inc(gel_ok, 1)
                    nc.scalar.activation(gel[:, NLAT:], ps[:, 3, 0:P], ACT.Gelu_apprx_tanh).then_inc(gel_ok, 1)
            mod_reads(range(3, 5))
            squares(1, 0)
            store_xhat(0)
            turned(1, 0)
            softmax(0)
            mod_reads(range(5, 6))
            gate_columns(0)
            mod_reads(range(6, 9))
            experts(0)

            act.wait_ge(scattered, 16 * NE)
            act.dma_start(tok(r2), x_mid.rearrange("(t p) d -> p t d", p=P)).then_inc(x_in, 16)
            act.dma_start(kc, cache_k).then_inc(small_in, 16)
            act.dma_start(v_s[:, 5, :], cache_v).then_inc(small_in, 16)
            act.dma_start(gains[:, 0:NH * HD].rearrange("p (h n) -> p h n", n=HD),
                          at_q_norm.unsqueeze(1).to_broadcast([P, NH, HD])).then_inc(small_in, 16)
            act.dma_start(gains[:, NH * HD:].rearrange("p (h n) -> p h n", n=HD),
                          at_k_norm.unsqueeze(1).to_broadcast([P, NKV, HD])).then_inc(small_in, 16)
            for s in range(2):
                act.dma_start(tab[:, s], rope[s].rearrange("(t p) n -> p t n", p=P)).then_inc(small_in, 16)
            act.dma_start(sinks[:, 0, :], at_sink.to_broadcast([P, NH])).then_inc(small_in, 16)

            def x_squares():
                act.wait_ge(x_in, 64)
                squares(2, None)

            mod_reads(range(9, 11), x_squares)
            turned(2, 1)
            mod_reads(range(11, 12))
            act.wait_ge(k_mm, 1)
            copy(k_t[:, :, NTOK:KEYS], ps[:, 6, :], k_ok)

            def turned_q(t):
                act.wait_ge(q_mm, t + 1)
                copy(q_t[:, 0:4, t * P:(t + 1) * P], ps[:, 6, :], q_act)
                act.wait_ge(k_mm, t + 2)
                copy(k_t[:, :, t * P:(t + 1) * P], ps[:, 6, :], k_ok)

            for t in range(NT):
                if t < NT - 1:
                    act.wait_ge(qkv_mm, t + 1)
                else:
                    act.wait_ge(ring_used, used(ROUND_AT, KB - 1))
                z = 3 * (t % 2)
                if t >= 1:
                    act.wait_ge(qn_ok, t)
                for n, w in ((0, 512), (1, 512), (2, 256)):
                    nc.scalar.activation(qs[:, n * 512:n * 512 + w], ps[:, z + n, 0:w], ACT.Square).then_inc(qsq_ok, 1)
                copy(v_s[:, t, :], ps[:, z + 2, 256:512], v_ok)
                act.wait_ge(qvar_ok, t + 1)
                nc.scalar.activation(ss20[:, 1], ss20[:, 0], ACT.Sqrt).then_inc(qstd_ok, 1)
                if t >= 1:
                    turned_q(t - 1)
            turned_q(NT - 1)
            for i in range(NU + 3):
                if i < NU:
                    j, hp = units[i]
                    act.wait_ge(nm_ok, i + 1)
                    w = len(KEYB[j][0]) * P
                    for a in range(2):
                        nc.scalar.activation(pm[:, i % 2, a, 0:w], pm[:, i % 2, a, 0:w], ACT.Exp, bias=stat[:, i % 4, 1, a:a + 1],
                                             accum_out=stat[:, i % 4, 3, a:a + 1]).then_inc(p_ok, 1)
                    nc.scalar.activation(stat[:, i % 4, 4, :], stat[:, i % 4, 2, :], ACT.Exp).then_inc(p_ok, 1)
                if 1 <= i <= NU:
                    w = len(KEYB[units[i - 1][0]][0]) * P
                    act.wait_ge(pt_mm, i)
                    if i >= 3:
                        act.wait_ge(pv_mm, i - 2)
                    copy(pt[:, (i - 1) % 2, 0, 0:w], ps[:, 4, 0:w], pt_act)
                if last_of_tile(i - 3):
                    j = (i - 3) // KB
                    act.wait_ge(ot_mm, j + 1)
                    copy(feat(r1)[:, 0:4, j * P:(j + 1) * P], ps[:, 4, :], ot_act)
            gate_copy(1, gb1)
            squares(3, 2 * NT)
            store_xhat(1)
            turned(3, 1)
            softmax(1)
            gate_columns(1)
            experts(1)

        @block.vector
        def _(eng):
            n = [0]

            def step(ins):
                n[0] += 1
                ins.then_inc(dve, 1)
                eng.wait_ge(dve, n[0])

            v = nc.vector

            def norm(phase, x_ready):
                x, xh = tok(NORMS[phase][0]), tok(NORMS[phase][1])
                for t in range(3, NT):
                    if x_ready is not None:
                        eng.wait_ge(x1_ok, x_ready + 2 * (t + 1))
                    v.tensor_tensor_reduce(out=w_junk2, in0=x[:, t, :], in1=x[:, t, :], scale=1.0, scalar=0.0,
                                           op0=ALU.mult, op1=ALU.add, accum_out=sm[:, phase, 0, t:t + 1]).then_inc(ssq_ok, 1)
                    eng.wait_ge(ssq_ok, 2 * phase + t - 2)
                eng.wait_ge(ssq_act, 3 * (phase + 1))
                eng.wait_ge(ssq_ok, 2 * (phase + 1))
                v.tensor_scalar(sm[:, phase, 0, 0:NT], sm[:, phase, 0, 0:NT], 1.0 / D, EPS, ALU.mult, ALU.add).then_inc(var_ok, 1)
                eng.wait_ge(std_ok, phase + 1)
                step(v.reciprocal(sm[:, phase, 2, 0:NT], sm[:, phase, 1, 0:NT]))
                for t in range(NT):
                    v.tensor_scalar(xh[:, t, :], x[:, t, :], sm[:, phase, 2, t:t + 1], None, ALU.mult).then_inc(xhat_ok, 1)

            def turned(phase, layer):
                eng.wait_ge(mod_ok, NMOD * layer + 3 * (phase % 2) + 2)
                row = (R_G1, R_G2)[phase % 2] + layer
                v.scalar_tensor_tensor(out=amod[:, phase], in0=mod[:, layer, 3 * (phase % 2) + 1], scalar=1.0,
                                       in1=vec[:, :, row:row + 1].to_broadcast([P, KB, 2]), op0=ALU.add,
                                       op1=ALU.mult).then_inc(amod_ok, 1)
                eng.wait_ge(amod_ok, phase + 1)
                out = feat(NORMS[phase][2])
                for b in range(KB):
                    eng.wait_ge(tr_mm, 2 * (KB * phase + b) + 1 + (b + 1) % 2)
                    src, cols, st = ((ps[:, b % 2, :], slice(0, NLAT), 0) if b % 2 == 1
                                     else (ps[:, 2 + b % 2, 0:P], slice(NLAT, NTOK), 1))
                    v.tensor_scalar(out[:, b, cols], src, amod[:, phase, b, st:st + 1],
                                    mod[:, layer, 3 * (phase % 2), b, st:st + 1], ALU.mult, ALU.add).then_inc(tr_dve, 1)

            def diagonals(layer, out):
                eng.wait_ge(mod_ok, NMOD * layer + 3)
                for s in range(2):
                    v.tensor_tensor(out[:, s], ident[:, :].unsqueeze(1).to_broadcast([P, KB, P]),
                                    mod[:, layer, 2, :, s:s + 1].to_broadcast([P, KB, P]), ALU.mult).then_inc(diag_ok, 1)

            def residual(layer, x1, g, rnd):
                x = tok(x1)
                eng.wait_ge(gate_ok, 4 * (layer + 1))
                for t in range(NT):
                    for h in range(2):
                        m = 2 * t + h
                        if m < 2 * NT - 1:
                            eng.wait_ge(out_mm, (2 * NT - 1) * layer + m + 1)
                        else:
                            eng.wait_ge(ring_used, used(rnd, SLOTS - 1))
                        v.tensor_tensor(w_tmp[:, m % 2], ps[:, 2 * (t % 2) + h, :], g[:, t // TL, h * 512:(h + 1) * 512],
                                        ALU.mult).then_inc(out_mul, 1)
                        eng.wait_ge(out_mul, 2 * NT * layer + m + 1)
                        xs = x[:, t, h * 512:(h + 1) * 512]
                        v.tensor_tensor(xs, xs, w_tmp[:, m % 2], ALU.add).then_inc(x1_ok, 1)

            def route(layer):
                lgp = ps[:, 4, 0:NT * NE].rearrange("p (t n) -> p t n", t=NT)
                eng.wait_ge(lg_mm, layer + 1)
                step(v.tensor_reduce(mx5[:, 0, 0:NT], lgp, AX.X, ALU.max))
                v.tensor_tensor(lg, lgp, mx5[:, 0, 0:NT].unsqueeze(2).to_broadcast([P, NT, NE]), ALU.subtract).then_inc(lg_sub, 1)
                eng.wait_ge(lg_exp, layer + 1)
                step(v.tensor_reduce(mx5[:, 1, 0:NT], lg, AX.X, ALU.add))
                step(v.reciprocal(mx5[:, 1, 0:NT], mx5[:, 1, 0:NT]))
                v.tensor_tensor(lg, lg, mx5[:, 1, 0:NT].unsqueeze(2).to_broadcast([P, NT, NE]), ALU.mult).then_inc(aff_ok, 1)
                eng.wait_ge(tk_set, layer + 1)
                eng.wait_ge(aff_mm, layer + 1)
                step(v.tensor_copy(tk[0:NE, :], ps[0:NE, 5, :]))
                step(v.tensor_copy(tk[32:32 + NE, 0:NCTX], ps[0:NE, 3, 0:P]))
                for r in range(CL // 8):
                    k8 = slice(8 * r, 8 * r + 8)
                    step(v.max(tv[0:48, k8], tk[0:48, :]))
                    step(v.max_index(ti[0:48, k8], tv[0:48, k8], tk[0:48, :]))
                    if r < CL // 8 - 1:
                        step(v.match_replace(tk[0:48, :], tv[0:48, k8], tk[0:48, :], -1.0))
                v.tensor_copy(comb[0:NE, 0, 0:CL], tv[0:NE, :]).then_inc(comb_ok, 1)
                v.tensor_copy(comb[0:NE, 0, CL:CE], tv[32:32 + NE, 0:CC]).then_inc(comb_ok, 1)
                v.tensor_copy(comb[0:NE, 1, 0:CL], ti[0:NE, :]).then_inc(comb_ok, 1)
                v.tensor_scalar(comb[0:NE, 1, CL:CE], ti[32:32 + NE, 0:CC], float(NLAT), None, ALU.add).then_inc(comb_ok, 1)
                eng.wait_ge(comb_mm, layer + 1)
                v.tensor_copy(g_t[:, :], ps[0:CE, 4, 0:NE]).then_inc(route_ok, 1)
                v.tensor_copy(idx_t[:, :], ps[0:CE, 4, NE:2 * NE]).then_inc(route_ok, 1)

            def experts(layer):
                base = layer * NE
                eng.wait_ge(ex_ok, 4 * (layer + 1))

                def rest(e, par, q):
                    n = 8 + USES * par + q // 2 if e is not None else q // 2 - 4
                    eng.wait_ge(whi_ok, block_of(layer, -1 if e is None else e, q))
                    v.tensor_tensor(whl[:, q % HL, 1, :], ring[:, n % MSLOTS, (q % 2) * D:(q % 2 + 1) * D],
                                    whl[:, q % HL, 0, :].bitcast(F32), ALU.subtract).then_inc(wlo_ok, 1)

                def halves(t):
                    return t.rearrange("p (h n) -> p h n", h=2)

                def x_mod(e):
                    eng.wait_ge(xtr_mm, e + (base + 1))
                    v.tensor_tensor(halves(xt), ps[:, 6:8, 0:4 * CE], halves(ex[0]), ALU.mult).then_inc(xt_mul, 1)
                    eng.wait_ge(xt_mul, e + (base + 1))
                    v.tensor_tensor(xt, xt, ex[1], ALU.add).then_inc(xt_ok, 1)

                def x_rest(e, buf):
                    eng.wait_ge(xh_ok, e + (base + 1))
                    v.tensor_tensor(xs_hl[:, buf, 1].rearrange("p k n -> p (k n)"), xt,
                                    xs_hl[:, buf, 0].rearrange("p k n -> p (k n)").bitcast(F32), ALU.subtract).then_inc(xl_ok, 1)

                def hidden(e):
                    eng.wait_ge(sil_ok, e + (base + 1))
                    v.tensor_tensor(halves(hid[0:CE, :]), ps[0:CE, 2:4, :], halves(sil[0:CE, :]), ALU.mult).then_inc(h_ok, 1)

                def h_rest(e):
                    eng.wait_ge(hh_ok, e + (base + 1))
                    v.tensor_tensor(hs_hl[:, 1].rearrange("p (h m) n -> p h (m n)", h=2), ps[:, 6:8, 0:4 * CE],
                                    hs_hl[:, 0].rearrange("p (h m) n -> p h (m n)", h=2).bitcast(F32), ALU.subtract).then_inc(hl_ok, 1)

                def body(e, i, par, more, rows_left):
                    for q in range(2 * USES if more else 8):
                        rest(e, par, q)
                        if q == 3:
                            hidden(e)
                        if q == (6 if more else 3):
                            h_rest(e)
                        if q == 19 and rows_left:
                            x_mod(e + 2)
                        if q == 21 and rows_left:
                            x_rest(e + 2, par)

                for q in range(8, 2 * USES):
                    rest(None, 1, q)
                    if q == 11:
                        x_mod(0)
                        x_rest(0, 0)
                    if q == 19:
                        x_mod(1)
                    if q == 21:
                        x_rest(1, 1)
                steps(eng, body)

            eng.wait_ge(rows_t, 1)
            v.tensor_copy(vec[:, :, 0:NROWS], ps[:, 0, 0:KB * 32].rearrange("p (b r) -> p b r", b=KB)[:, :, 0:NROWS]).then_inc(vec_ok, 1)
            eng.wait_ge(vec_ok, 1)
            eng.wait_ge(sig_c, 1)
            v.tensor_tensor(cond[:, :, :], cond[:, :, :], vec[:, :, R_C:R_C + 2], ALU.mult).then_inc(cond_ok, 1)
            lam = vec[:, :, R_LAM:R_LAM + 2]
            step(v.tensor_scalar(spt[:, 0], lam, -1.0, None, ALU.mult))
            v.tensor_tensor(spt[:, 1], spt[:, 0], lam, ALU.max).then_inc(lam_abs, 1)
            step(v.tensor_scalar(spt[:, 2], spt[:, 0], 0.0, 4.0, ALU.max, ALU.mult))
            eng.wait_ge(lam_exp, 1)
            step(v.tensor_scalar(spt[:, 4], spt[:, 3], 2.0, None, ALU.add))
            step(v.reciprocal(spt[:, 4], spt[:, 4]))
            step(v.tensor_tensor(spt[:, 3], spt[:, 3], spt[:, 4], ALU.mult))
            step(v.tensor_tensor(spt[:, 4], spt[:, 3], spt[:, 3], ALU.mult))
            step(v.tensor_scalar(spt[:, 5], spt[:, 4], 1.0 / 17, None, ALU.mult))
            for m in (15, 13, 11, 9, 7, 5, 3):
                step(v.scalar_tensor_tensor(out=spt[:, 5], in0=spt[:, 5], scalar=1.0 / m, in1=spt[:, 4], op0=ALU.add, op1=ALU.mult))
            step(v.scalar_tensor_tensor(out=spt[:, 5], in0=spt[:, 5], scalar=1.0, in1=spt[:, 3], op0=ALU.add, op1=ALU.mult))
            v.scalar_tensor_tensor(out=sp4[:, :, :], in0=spt[:, 5], scalar=8.0, in1=spt[:, 2], op0=ALU.mult, op1=ALU.add).then_inc(sp_ok, 1)
            eng.wait_ge(x_in, 16)
            norm(0, None)
            turned(0, 0)
            diagonals(0, diag)

            hg = feat(r2)
            eng.wait_ge(consts, 4)
            for b in range(KB + 1):
                if b < KB:
                    uc = ucs[b % 2]
                    eng.wait_ge(u_ok, 2 * (b + 1))
                    if b >= 2:
                        eng.wait_ge(z_mm, b - 1)
                        eng.wait_ge(iu_ok, 2 * (b - 1))
                    step(v.tensor_scalar(uc, upad[:, 0:UC], vec[:, b, R_CW:R_CW + 1], vec[:, b, R_CB:R_CB + 1], ALU.mult, ALU.add))
                    for k in range(1, 4):
                        ins = v.scalar_tensor_tensor(out=uc, in0=upad[:, k:k + UC], scalar=vec[:, b, R_CW + k:R_CW + k + 1],
                                                     in1=uc, op0=ALU.mult, op1=ALU.add)
                        if k < 3:
                            step(ins)
                    ins.then_inc(conv_ok, 1)
                if b >= 1:
                    c1 = b - 1
                    eng.wait_ge(tanh_ok, 2 * b)
                    v.tensor_scalar(qq, rt, 1.0, None, ALU.add).then_inc(q_read, 1)
                    eng.wait_ge(q_read, b)
                    step(v.reciprocal(qq, qq))
                    v.tensor_scalar(aa, qq, 2.0, -1.0, ALU.mult, ALU.add)
                    eng.wait_ge(sqrt_ok, b)
                    step(v.tensor_tensor(sq, sq, qq, ALU.mult))
                    eng.wait_ge(iu_ok, 2 * b)
                    v.tensor_tensor(sq, sq, ig, ALU.mult).then_inc(ig_used, 1)
                    eng.wait_ge(ig_used, b)
                    if b >= 2:
                        eng.wait_ge(st_ok, 2 * c1)
                    v.tensor_tensor_scan(hh[:, 0, 0:NLAT], aa[:, 0, 0:NLAT], sq[:, 0, 0:NLAT],
                                         vec[:, c1, R_H0:R_H0 + 1], ALU.mult, ALU.add).then_inc(scan_ok, 1)
                    v.tensor_tensor_scan(hh[:, 0, NLAT:], aa[:, 0, NLAT:], sq[:, 0, NLAT:], 0.0, ALU.mult, ALU.add).then_inc(scan_ok, 1)
                    v.tensor_tensor_scan(hh[:, 1, 0:NLAT][:, ::-1], aa[:, 1, 0:NLAT][:, ::-1], sq[:, 1, 0:NLAT][:, ::-1],
                                         vec[:, c1, R_H0 + 1:R_H0 + 2], ALU.mult, ALU.add).then_inc(scan_ok, 1)
                    v.tensor_tensor_scan(hh[:, 1, NLAT:][:, ::-1], aa[:, 1, NLAT:][:, ::-1], sq[:, 1, NLAT:][:, ::-1],
                                         0.0, ALU.mult, ALU.add).then_inc(scan_ok, 1)
                    eng.wait_ge(scan_ok, 4 * b)
                    step(v.tensor_tensor(aa[:, 0], hh[:, 0], hh[:, 1], ALU.add))
                    eng.wait_ge(gel_ok, 2 * b)
                    v.tensor_tensor(hg[:, c1, :], aa[:, 0], gel, ALU.mult).then_inc(hg_ok, 1)
            eng.wait_ge(x_in, 48)
            residual(0, r1, gb, ROUND_RG)
            eng.wait_ge(st_mm, 1)
            v.tensor_copy(st_row[:, :], ps[0:16, 4, 0:P]).then_inc(st_row_ok, 1)
            norm(1, 0)
            turned(1, 0)
            route(0)
            experts(0)

            eng.wait_ge(x_in, 64)
            norm(2, None)
            turned(2, 1)

            def turned_q(t):
                eng.wait_ge(q_mm, t + 1)
                v.tensor_copy(q_t[:, 4:8, t * P:(t + 1) * P], ps[:, 7, :].rearrange("p (h n) -> p h n", h=4)).then_inc(q_dve, 1)

            qn3, qs3, gn3 = (a.rearrange("p (h n) -> p h n", h=NQK) for a in (qn, qs, gains))
            qn4, qs4 = (a.rearrange("p (h f q n) -> p h f q n", h=NQK, f=2, q=2) for a in (qn, qs))
            eng.wait_ge(gains_ok, 1)
            eng.wait_ge(small_in, 16 * 7)
            for t in range(NT):
                z = 3 * (t % 2)
                eng.wait_ge(qsq_ok, 3 * (t + 1))
                step(v.tensor_reduce(ss20[:, 0], qs3, AX.X, ALU.add))
                v.tensor_scalar(ss20[:, 0], ss20[:, 0], 1.0 / HD, EPS, ALU.mult, ALU.add).then_inc(qvar_ok, 1)
                eng.wait_ge(qstd_ok, t + 1)
                step(v.reciprocal(ss20[:, 1], ss20[:, 1]))
                eng.wait_ge(kdup_ok, 2 * (t + 1))
                if t >= 1:
                    turned_q(t - 1)
                for lo, hi, src in ((0, 8, ps[:, z, :]), (8, 16, ps[:, z + 1, :]), (16, 20, ps[:, z + 2, 0:256])):
                    ins = v.tensor_tensor(qn3[:, lo:hi], src.rearrange("p (h n) -> p h n", n=HD),
                                          ss20[:, 1, lo:hi].unsqueeze(2).to_broadcast([P, hi - lo, HD]), ALU.mult)
                    if hi < NQK:
                        step(ins)
                ins.then_inc(qn_read, 1)
                eng.wait_ge(qn_read, t + 1)
                ins = v.tensor_tensor(qn, qn, gains, ALU.mult)
                if t < TL:
                    step(ins)
                    for q in range(2):
                        v.tensor_tensor(qs4[:, :, :, q, :], qn4[:, :, :, 1 - q, :],
                                        tab[:, 1, t].rearrange("p (f q n) -> p f q n", f=2, q=2)[:, :, q, :].unsqueeze(1)
                                        .to_broadcast([P, NQK, 2, HD // 4]), ALU.mult).then_inc(rot_ok, 1)
                    eng.wait_ge(rot_ok, 2 * (t + 1))
                    step(v.tensor_tensor(qn3, qn3, tab[:, 0, t].unsqueeze(1).to_broadcast([P, NQK, HD]), ALU.mult))
                    ins = v.tensor_tensor(qn, qn, qs, ALU.add)
                ins.then_inc(qn_ok, 1)
            turned_q(NT - 1)
            eng.wait_ge(consts, 6)
            eng.wait_ge(sink_ok, 1)
            eng.wait_ge(kv_stored, 32)
            for i in range(NU + 3):
                if i < NU:
                    j, hp = units[i]
                    w, m0 = len(KEYB[j][0]) * P, KEYB[j][1]
                    st = stat[:, i % 4]
                    eng.wait_ge(s_mm, i + 1)
                    if i >= 2:
                        eng.wait_ge(pt_mm, i - 1)
                    for a in range(2):
                        v.tensor_tensor_reduce(out=pm[:, i % 2, a, 0:w], in0=ps[:, 2 * (i % 2) + a, 0:w],
                                               in1=mask[:, m0:m0 + w], scale=1.0, scalar=NEG, op0=ALU.add, op1=ALU.max,
                                               accum_out=st[:, 0, a:a + 1]).then_inc(s_max, 1)
                    eng.wait_ge(s_max, 2 * (i + 1))
                    step(v.scalar_tensor_tensor(out=st[:, 1, :], in0=st[:, 0, :], scalar=-1.0, in1=sinks[:, 1, 2 * hp:2 * hp + 2],
                                                op0=ALU.mult, op1=ALU.min))
                    v.tensor_tensor(st[:, 2, :], sinks[:, 0, 2 * hp:2 * hp + 2], st[:, 1, :], ALU.add).then_inc(nm_ok, 1)
                if 1 <= i <= NU:
                    w = len(KEYB[units[i - 1][0]][0]) * P
                    eng.wait_ge(pt_mm, i)
                    if i >= 3:
                        eng.wait_ge(pv_mm, i - 2)
                    v.tensor_copy(pt[:, (i - 1) % 2, 1, 0:w], ps[:, 5, 0:w]).then_inc(pt_dve, 1)
                if 2 <= i < NU + 2:
                    j, hp = units[i - 2]
                    st = stat[:, (i - 2) % 4]
                    eng.wait_ge(p_ok, 3 * (i - 1))
                    step(v.tensor_tensor(st[:, 5, :], st[:, 3, :], st[:, 4, :], ALU.add))
                    step(v.reciprocal(st[:, 6, :], st[:, 5, :]))
                    eng.wait_ge(pv_mm, i - 1)
                    if j >= 2:
                        eng.wait_ge(ot_mm, j - 1)
                    v.tensor_tensor(gb[:, j % 2, hp * P:(hp + 1) * P].rearrange("p (a n) -> p a n", a=2),
                                    ps[:, 6 + i % 2, 0:P].rearrange("p (a n) -> p a n", a=2),
                                    st[:, 6, :].unsqueeze(2).to_broadcast([P, 2, HD]), ALU.mult).then_inc(o_ok, 1)
                if last_of_tile(i - 3):
                    j = (i - 3) // KB
                    eng.wait_ge(ot_mm, j + 1)
                    v.tensor_copy(feat(r1)[:, 4:8, j * P:(j + 1) * P], ps[:, 5, :].rearrange("p (h n) -> p h n", h=4)).then_inc(ot_dve, 1)
            diagonals(1, diag1)
            residual(1, r2, gb1, ROUND_AT)
            norm(3, 2 * NT)
            turned(3, 1)
            route(1)
            experts(1)


def rope_table():
    t = np.arange(NLAT)
    inv = (np.float32(10000.0) ** (-np.arange(HD // 4, dtype=np.float32) / (HD // 4))).astype(np.float32)
    ar = (t // 64).astype(np.float32)[:, None] * inv
    ac = (t % 64).astype(np.float32)[:, None] * inv
    ang = np.concatenate([ar, ar, ac, ac], axis=1)
    sign = np.repeat(np.array([-1, 1, -1, 1], np.float32), HD // 4)
    return np.stack([np.cos(ang), np.sin(ang) * sign]).astype(np.float32)


def kernel(x_prompt, x_sample, state_rglru, cache_k, cache_v, c, c_ctx, mod_w, mod_b, norm1_g, norm2_g,
           rg_w_in, rg_conv_w, rg_conv_b, rg_w_a, rg_b_a, rg_w_x, rg_b_x, rg_lambda, rg_w_out,
           at_w_qkv, at_q_norm, at_k_norm, at_sink, at_w_o, ft_w, moe_router, moe_w_gate, moe_w_up, moe_w_down):
    import concourse.bacc as bacc
    from concourse.bass_utils import run_bass_kernel_spmd

    ins = {
        "x_all": np.concatenate([np.asarray(x_sample)[0], np.asarray(x_prompt)[0]]),
        "state": np.asarray(state_rglru).reshape(2, D),
        "cache_k": np.asarray(cache_k).reshape(P, NKV * HD), "cache_v": np.asarray(cache_v).reshape(P, NKV * HD),
        "c": np.asarray(c).reshape(1, D), "c_ctx": np.asarray(c_ctx).reshape(1, D),
        "mod_w": np.asarray(mod_w), "mod_b": np.asarray(mod_b).reshape(2 * NMOD, D),
        "norm1_g": np.asarray(norm1_g), "norm2_g": np.asarray(norm2_g),
        "rg_w_in": np.asarray(rg_w_in)[0], "rg_conv_w": np.asarray(rg_conv_w)[0], "rg_conv_b": np.asarray(rg_conv_b),
        "rg_w_a": np.asarray(rg_w_a)[0], "rg_b_a": np.asarray(rg_b_a)[0],
        "rg_w_x": np.asarray(rg_w_x)[0], "rg_b_x": np.asarray(rg_b_x)[0],
        "rg_lambda": np.asarray(rg_lambda)[0], "rg_w_out": np.asarray(rg_w_out)[0],
        "at_w_qkv": np.asarray(at_w_qkv)[0], "at_q_norm": np.asarray(at_q_norm), "at_k_norm": np.asarray(at_k_norm),
        "at_sink": np.asarray(at_sink), "at_w_o": np.asarray(at_w_o)[0], "moe_router": np.asarray(moe_router),
        "moe_w_gate": np.asarray(moe_w_gate), "moe_w_up": np.asarray(moe_w_up), "moe_w_down": np.asarray(moe_w_down),
        "rope": rope_table(),
    }
    outs = {"y_all": (NTOK, D), "new_state": (2, D), "new_k": (NCTX, NKV * HD), "new_v": (NCTX, NKV * HD)}
    nc = bacc.Bacc("TRN2", target_bir_lowering=False, num_devices=1)
    aps = {k: nc.dram_tensor(f"in_{k}", a.shape, F32, kind="ExternalInput").ap() for k, a in ins.items()}
    aps.update({k: nc.dram_tensor(f"out_{k}", s, F32, kind="ExternalOutput").ap() for k, s in outs.items()})
    build(nc, **aps)
    r = run_bass_kernel_spmd(nc, [{f"in_{k}": np.ascontiguousarray(a) for k, a in ins.items()}], core_ids=[0]).results[0]
    y = r["out_y_all"]
    return (y[NLAT:].reshape(1, NCTX, D), y[:NLAT].reshape(1, NLAT, D), r["out_new_state"].reshape(1, 1, 2, D),
            r["out_new_k"].reshape(1, 1, NCTX, NKV, HD), r["out_new_v"].reshape(1, 1, NCTX, NKV, HD))
```

```python
from contextlib import ExitStack

import numpy as np

import concourse.bass as bass
from concourse import mybir

F32 = mybir.dt.float32
F32R = mybir.dt.float32r
U32 = mybir.dt.uint32
ALU = mybir.AluOpType
ACT = mybir.ActivationFunctionType
AX = mybir.AxisListType

P = 128
D = 1024
KB = D // P
NLAT, NCTX = 512, 128
NTOK = NLAT + NCTX
TL = NLAT // P
NT = NTOK // P
NMOD = 6
EPS = 1e-6
NB = 16
RB = D // NB
NH, NKV, HD = 16, 4, 64
NQK = NH + NKV
QKV = (NH + 2 * NKV) * HD
NE = 16
CL, CC = 2 * NLAT // NE, 2 * NCTX // NE
CE = CL + CC
NEG = -1e30

SLOTS, MSLOTS = 12, 8
ROUND_RG, ROUND_AT = 1, 5
MOD_ROUNDS = (0, 2, 3, 4)
MOD_ORDER = (0, 1, 2, 3, 4, 5, 6, 7, 9, 10, 8, 11)
ROUNDS = (4, 6)
USES = 12
ESLOTS = NE * USES
HL = 4
EQ = 2 * ESLOTS

R_C, R_CCTX, R_G1, R_G2, R_CW, R_CB, R_BA, R_BX, R_LAM, R_H0, R_MODB = 0, 1, 2, 4, 6, 10, 11, 13, 15, 17, 19
NROWS = R_MODB + 2 * NMOD
UPAD = 2 + NLAT + 2 + NCTX + 1
UC = NLAT + 2 + NCTX
C0 = NLAT + 2


def build(nc, x_all, state, cache_k, cache_v, c, c_ctx, mod_w, mod_b, norm1_g, norm2_g,
          rg_w_in, rg_conv_w, rg_conv_b, rg_w_a, rg_b_a, rg_w_x, rg_b_x, rg_lambda, rg_w_out,
          at_w_qkv, at_q_norm, at_k_norm, at_sink, at_w_o, moe_router, moe_w_gate, moe_w_up,
          moe_w_down, rope, y_all, new_state, new_k, new_v):
    with ExitStack() as ctx:
        def sb(name, shape, dt=F32):
            return ctx.enter_context(nc.sbuf_tensor(name, shape, dt))

        def sem(name):
            return ctx.enter_context(nc.semaphore(name))

        x_mid = nc.dram_tensor("x_mid", (NTOK, D), F32, kind="Internal").ap()
        x_hat = [nc.dram_tensor(f"x_hat{l}", (NTOK, D), F32, kind="Internal").ap() for l in range(2)]
        x_res = (x_mid, y_all)

        ps = ctx.enter_context(nc.psum_tensor("ps", [P, 8, 512], F32))
        ring_at = -(-nc.sbuf_base // 32) * 32
        ring = sb("ring", [P, SLOTS, 2 * D])
        whl = nc.alloc_sbuf_tensor_at("whl", [P, HL, 2, D], F32R, offset=ring_at + 4 * MSLOTS * 2 * D)
        r1_at = ring_at + 4 * SLOTS * 2 * D
        assert nc.sbuf_base == r1_at
        r1 = sb("r1", [P, 5 * D])
        r2 = sb("r2", [P, 5 * D])
        xs_hl = nc.alloc_sbuf_tensor_at("xs_hl", [P, 2, 2, KB, CE], F32R, offset=r1_at)
        hs_hl = nc.alloc_sbuf_tensor_at("hs_hl", [P, 2, KB, CE], F32R, offset=r1_at + 4 * 4 * KB * CE)
        mx_hi = nc.alloc_sbuf_tensor_at("mx_hi", [P, KB, NTOK], F32R, offset=r1_at)
        mx_lo = nc.alloc_sbuf_tensor_at("mx_lo", [P, KB, NTOK], F32R, offset=ring_at + 4 * MSLOTS * 2 * D)
        gb_at = r1_at + 4 * 2 * 5 * D
        assert nc.sbuf_base == gb_at
        wcol = [nc.alloc_sbuf_tensor_at("wcol_u", [P, 2, KB, P], F32R, offset=ring_at + 4 * (MSLOTS * 2 * D + KB * NTOK)),
                nc.alloc_sbuf_tensor_at("wcol_g", [P, 2, KB, P], F32R, offset=gb_at)]
        gb = sb("gb", [P, 2, D])
        W_at = gb_at + 4 * 2 * D
        assert nc.sbuf_base == W_at
        xq_hi = nc.alloc_sbuf_tensor_at("xq_hi", [P, 2, KB, P], F32R, offset=gb_at)
        wq_hi = nc.alloc_sbuf_tensor_at("wq_hi", [P, KB, D], F32R, offset=ring_at + 4 * MSLOTS * 2 * D)
        wq = nc.alloc_sbuf_tensor_at("wq", [P, KB, 2 * D], F32R, offset=ring_at)
        wo_hl = nc.alloc_sbuf_tensor_at("wo_hl", [P, KB, 2, D], F32R, offset=ring_at)
        mo_hi = nc.alloc_sbuf_tensor_at("mo_hi", [P, KB, NTOK], F32R, offset=W_at)
        mo_lo = [nc.alloc_sbuf_tensor_at("mo_lo0", [P, KB, NTOK], F32R, offset=r1_at + 4 * 5 * D),
                 nc.alloc_sbuf_tensor_at("mo_lo1", [P, KB, NTOK], F32R, offset=r1_at)]
        W = sb("W", [P, 14592])
        ident = sb("ident", [P, P])
        ones = sb("ones", [P, P])
        vec = sb("vec", [P, KB, 32])
        mod = sb("mod", [P, 2, NMOD, KB, 2])
        cond = sb("cond", [P, KB, 2])
        amod = sb("amod", [P, 4, KB, 2])
        router = sb("router", [P, 2, KB, NE])
        sp4 = sb("sp4", [P, KB, 2])
        spn = sb("spn", [P, KB, 2])
        stv = sb("stv", [P, 2, KB])
        st_row = sb("st_row", [16, P])
        sm = sb("sm", [P, 4, 3, 8])
        modraw = sb("modraw", [P, 2, KB, 2])
        mx5 = sb("mx5", [P, 2, 8])
        spt = sb("spt", [P, 6, KB, 2])
        sinks = sb("sinks", [P, 2, NH])
        stat = sb("stat", [P, 4, 8, 2])
        ss20 = sb("ss20", [P, 2, NQK])
        idx_t = sb("idx_t", [CE, NE], U32)
        g_t = sb("g_t", [CE, NE])
        gi = sb("gi", [CE, 1], U32)
        si = sb("si", [CE, 1], U32)
        sg = sb("sg", [CE, 1])

        def tok(t):
            return t[:, :].rearrange("p (t d) -> p t d", t=NT)

        w_tmp = W[:, 6144:7168].rearrange("p (a n) -> p a n", a=2)

        def mod_bank(n):
            return 0 if n in (3, 4) else 6

        def mod_rows(n):
            if n == 10:
                return gb[:, 1, :]
            src = r1[:, 3 * D:] if n < 5 else W[:, 6144:]
            return src[:, (n % 2) * D:(n % 2 + 1) * D]

        def feat(t):
            return t[:, 0:KB * NTOK].rearrange("p (k n) -> p k n", k=KB)

        off = [0]

        def work(n, at=None):
            if at is not None:
                off[0] = at
            off[0] += n
            assert off[0] <= 14592
            return W[:, off[0] - n:off[0]]

        w_xhat = work(5 * D, 0)
        w_junk = work(D)
        rows = work(D)
        mx_raw = W[:, 5 * D:5 * D + 2 * NTOK].rearrange("p (u n) -> p u n", u=2)
        w_junk2 = W[:, 8320:8320 + D]
        upad = work(UPAD + 3, 0)
        ucs = [work(UC) for _ in range(2)]
        rt = work(2 * NTOK).rearrange("p (a n) -> p a n", a=2)
        ig = work(2 * NTOK).rearrange("p (a n) -> p a n", a=2)
        sq = work(2 * NTOK).rearrange("p (a n) -> p a n", a=2)
        aas = [work(2 * NTOK).rearrange("p (a n) -> p a n", a=2) for _ in range(2)]
        hh = work(2 * NTOK).rearrange("p (a n) -> p a n", a=2)
        gels = (ring[:, SLOTS - 1, D:D + NTOK], work(NTOK))
        diag = W[:, off[0]:off[0] + 2 * D].rearrange("p (s b d) -> p s b d", s=2, b=KB)
        bd = work(4 * KB * P).rearrange("p (m c j) -> p m c j", m=4, c=KB)
        q_t = work(KB * NTOK, 0).rearrange("p (h n) -> p h n", h=KB)
        KEYS = NTOK + P
        k_t = work(NKV * KEYS).rearrange("p (g n) -> p g n", g=NKV)
        v_s = work(6 * NKV * HD).rearrange("p (t n) -> p t n", t=6)
        T1 = off[0]
        qn = work(NQK * HD)
        qs = work(NQK * HD)
        gains = work(NQK * HD)
        tab = work(2 * TL * HD).rearrange("p (s t n) -> p s t n", s=2, t=TL)
        kdup = work(NKV * P).rearrange("p (g a n) -> p g a n", g=NKV, a=2)
        pm = work(2 * 2 * 512, T1).rearrange("p (u i n) -> p u i n", u=2, i=2)
        pt = work(2 * 2 * 512).rearrange("p (u i n) -> p u i n", u=2, i=2)
        mask = work(5 * P)
        kc = qn[:, 0:NKV * HD]
        gb1 = work(2 * D, T1).rearrange("p (s d) -> p s d", s=2)
        diag1 = work(2 * D).rearrange("p (s b d) -> p s b d", s=2, b=KB)
        xn2 = work(5 * D, 0)
        xg = work(D)
        sil = work(D)
        hid = work(D)
        ob = work(D)
        gg = work(D)
        ex = [work(KB * CE) for _ in range(2)]
        xt = work(KB * CE)
        tk = work(512)
        tv = work(CL)
        ti = W[:, off[0]:off[0] + CL].bitcast(U32)
        work(CL)
        sel = work(2 * CE).rearrange("p (s n) -> p s n", s=2)
        diag2 = gb[:, :, :].rearrange("p s (b d) -> p s b d", b=KB)
        comb = work(2 * CE).rearrange("p (a n) -> p a n", a=2)
        lg = work(NT * NE).rearrange("p (t n) -> p t n", t=NT)
        assert off[0] <= 14592

        waits_passed = sem("waits_passed")
        slot_ready = [sem(f"slot_ready{s}") for s in range(SLOTS)]
        ring_used, rows_in, x_in, bd_in = sem("ring_used"), sem("rows_in"), sem("x_in"), sem("bd_in")
        small_in, router_in, consts, dve = sem("small_in"), sem("router_in"), sem("consts"), sem("dve")
        pool_s, rows_t, vec_ok, sig_c = sem("pool_s"), sem("rows_t"), sem("vec_ok"), sem("sig_c")
        cond_ok, lam_abs, lam_exp, sp_ok = sem("cond_ok"), sem("lam_abs"), sem("lam_exp"), sem("sp_ok")
        mod_row, mod_tr = sem("mod_row"), sem("mod_tr")
        x_mid_in = sem("x_mid_in")
        xq_hi_ok, xq_lo_ok, wq_hi_ok, wq_lo_ok = sem("xq_hi_ok"), sem("xq_lo_ok"), sem("wq_hi_ok"), sem("wq_lo_ok")
        ig_used, mx_hi_ok, mx_lo_ok = sem("ig_used"), sem("mx_hi_ok"), sem("mx_lo_ok")
        wo_hi_ok, wo_lo_ok, mo_hi_ok, mo_lo_ok = sem("wo_hi_ok"), sem("wo_lo_ok"), sem("mo_hi_ok"), sem("mo_lo_ok")
        wcol_hi_ok, wcol_lo_ok = sem("wcol_hi_ok"), sem("wcol_lo_ok")
        mod_read, mod_ok, diag_ok, gate_mm = sem("mod_read"), sem("mod_ok"), sem("diag_ok"), sem("gate_mm")
        gate_ok, ssq_act, ssq_ok, var_ok = sem("gate_ok"), sem("ssq_act"), sem("ssq_ok"), sem("var_ok")
        std_ok, xhat_ok, tr_mm, tr_act = sem("std_ok"), sem("xhat_ok"), sem("tr_mm"), sem("tr_act")
        tr_dve, amod_ok, u_mm, u_ok = sem("tr_dve"), sem("amod_ok"), sem("u_mm"), sem("u_ok")
        conv_ok, g_mm, z_mm, sig_ok = sem("conv_ok"), sem("g_mm"), sem("z_mm"), sem("sig_ok")
        tanh_ok, sqrt_ok, gel_ok, iu_ok = sem("tanh_ok"), sem("sqrt_ok"), sem("gel_ok"), sem("iu_ok")
        a_ok, scan_ok, hg_ok, st_ok = sem("a_ok"), sem("scan_ok"), sem("hg_ok"), sem("st_ok")
        st_mm, st_row_ok, out_mm, out_mul = sem("st_mm"), sem("st_row_ok"), sem("out_mm"), sem("out_mul")
        x1_ok, x1_stored, xh_stored, stored = sem("x1_ok"), sem("x1_stored"), sem("xh_stored"), sem("stored")
        kv_stored, lg_mm, lg_sub, lg_exp = sem("kv_stored"), sem("lg_mm"), sem("lg_sub"), sem("lg_exp")
        aff_ok, aff_mm, tk_set, comb_ok = sem("aff_ok"), sem("aff_mm"), sem("tk_set"), sem("comb_ok")
        comb_mm, route_ok, ex_ok = sem("comb_mm"), sem("route_ok"), sem("ex_ok")
        gathered, scattered, xtr_mm, xt_mul = sem("gathered"), sem("scattered"), sem("xtr_mm"), sem("xt_mul")
        xt_ok, xh_ok, xl_ok, sil_ok = sem("xt_ok"), sem("xh_ok"), sem("xl_ok"), sem("sil_ok")
        h_ok, htr_mm, hh_ok, hl_ok = sem("h_ok"), sem("htr_mm"), sem("hh_ok"), sem("hl_ok")
        whi_ok, wlo_ok, whl_used, y_act = sem("whi_ok"), sem("wlo_ok"), sem("whl_used"), sem("y_act")
        ob_ok, sg_ok, gi_ok, si_ok = sem("ob_ok"), sem("sg_ok"), sem("gi_ok"), sem("si_ok")
        sel_ok, diag2_ok, gg_mm, gg_ok = sem("sel_ok"), sem("diag2_ok"), sem("gg_mm"), sem("gg_ok")
        kdup_ok, rot_ok = sem("kdup_ok"), sem("rot_ok")
        qkv_mm, qsq_ok, qvar_ok, qstd_ok = sem("qkv_mm"), sem("qsq_ok"), sem("qvar_ok"), sem("qstd_ok")
        v_ok, qn_read, qn_ok, q_mm = sem("v_ok"), sem("qn_read"), sem("qn_ok"), sem("q_mm")
        q_act, q_dve, k_mm, k_ok = sem("q_act"), sem("q_dve"), sem("k_mm"), sem("k_ok")
        sink_ok, s_mm, s_max, nm_ok = sem("sink_ok"), sem("s_mm"), sem("s_max"), sem("nm_ok")
        p_ok, pt_mm, pt_act, pt_dve = sem("p_ok"), sem("pt_mm"), sem("pt_act"), sem("pt_dve")
        pv_mm, o_ok, ot_mm, ot_act = sem("pv_mm"), sem("o_ok"), sem("ot_mm"), sem("ot_act")
        ot_dve, gains_ok = sem("ot_dve"), sem("gains_ok")

        KEYB = {0: ([0, 1, 5], 2 * P), 1: ([0, 1, 2, 5], P), 2: ([1, 2, 3, 5], P), 3: ([5, 2, 3], 0), 4: ([4], 0)}
        units = [(j, hp) for j in range(NT) for hp in range(KB)]
        NU = len(units)

        def last_of_tile(i):
            return 0 <= i < NU and i % KB == KB - 1

        def runs(blocks):
            out = []
            for n, b in enumerate(blocks):
                if out and b == out[-1][1] + out[-1][2]:
                    out[-1][2] += 1
                else:
                    out.append([n, b, 1])
            return out

        last_mod = [(MOD_ROUNDS[3], s) for s in range(MSLOTS, SLOTS)]
        gate_mod = [(MOD_ROUNDS[2], s) for s in range(MSLOTS, SLOTS)]
        order = [(rnd, s) for rnd in range(ROUNDS[1]) for s in range(SLOTS)
                 if rnd not in (ROUND_RG, ROUND_AT) and not (rnd >= MOD_ROUNDS[2] and s >= MSLOTS)] + gate_mod + last_mod

        def used(rnd, s):
            return order.index((rnd, s)) + 1

        def ready(rnd, s):
            if (rnd, s) in last_mod:
                rnd += 1
            elif rnd == ROUND_AT and s >= MSLOTS:
                rnd -= 1
            return 16 * (rnd + 1 + (ESLOTS // MSLOTS if rnd >= ROUNDS[0] and s < MSLOTS else 0))

        def block_of(layer, e, q):
            return e * (2 * USES) + (EQ * layer + 16 + q + 1)

        def steps(eng, body):
            with eng.Fori(0, NE // 2 - 1) as i:
                for par in range(2):
                    body(i * 2 + par, i, par, True, True)
            body(NE - 2, NE // 2 - 1, 0, True, False)
            body(NE - 1, NE // 2 - 1, 1, False, False)

        x_tiles = x_all.rearrange("(t p) d -> p t d", p=P)
        XF = KB * NTOK
        NORM_TILES = (slice(0, NT - 1), slice(NT - 1, NT))
        NORMS = ((r2, w_xhat, r1), (r1, r2, xn2), (r2, w_xhat, r1), (r2, r1, xn2))

        block = ctx.enter_context(nc.Block())

        @block.sync
        def _(sp):
            def load(rnd, s, dst, src):
                if rnd == ROUNDS[0] and s < MSLOTS:
                    sp.wait_ge(wlo_ok, 2 * (ESLOTS - MSLOTS + s + 1))
                elif (rnd, s) in last_mod:
                    sp.wait_ge(wo_lo_ok, KB + 2 * (s - MSLOTS + 1))
                elif (rnd, s) in gate_mod:
                    sp.wait_ge(qkv_mm, NT)
                elif rnd == ROUND_AT and s >= MSLOTS:
                    sp.wait_ge(ring_used, used(MOD_ROUNDS[2], s))
                elif rnd == MOD_ROUNDS[1] and s < MSLOTS:
                    sp.wait_ge(wcol_lo_ok, 2 * KB)
                elif rnd == MOD_ROUNDS[1]:
                    sp.wait_ge(wo_lo_ok, 2 * (s - MSLOTS + 1))
                elif rnd == MOD_ROUNDS[2] and s < MSLOTS:
                    sp.wait_ge(out_mm, NT)
                elif rnd == ROUND_RG and s >= MSLOTS:
                    sp.wait_ge(g_mm, KB)
                    sp.wait_ge(hg_ok, KB - 1)
                elif rnd:
                    sp.wait_ge(ring_used, used(rnd - 1, s))
                sp.dma_start(dst, src).then_inc(slot_ready[s], 16)

            def pair(s):
                return ring[:, s, :].rearrange("p (k n) -> p k n", k=2)

            def rows2(w, k2, c0=0):
                return w[k2 * 2 * P:(k2 + 1) * 2 * P, c0:c0 + D].rearrange("(k p) n -> p k n", p=P)

            def load_mod(*vectors):
                for vec_no in vectors:
                    for s in range(4):
                        slot = 4 * (vec_no % 3) + s
                        load(MOD_ROUNDS[vec_no // 3], slot, pair(slot), rows2(mod_w[vec_no // NMOD], s, vec_no % NMOD * D))

            def load_moe(layer):
                w3 = [w[layer].rearrange("e (k p) n -> p (e k) n", p=P) for w in (moe_w_gate, moe_w_up, moe_w_down)]

                def put(slot, w, e, s):
                    sp.dma_start(pair(slot), w3[w][:, bass.ds(e * KB + 2 * s, 2), :]).then_inc(slot_ready[slot], 16)

                for n in range(MSLOTS):
                    if layer == 0:
                        sp.wait_ge(ring_used, used(ROUNDS[layer] - 1, n))
                    else:
                        sp.wait_ge(out_mm, 2 * NT)
                    put(n, n // 4, 0, n % 4)

                def step_loads(e, i, par, more, _):
                    for n in range(USES):
                        if not more and not 4 <= n < 8:
                            continue
                        m = n if more else n - 4
                        sp.wait_ge(wlo_ok, e * (2 * USES) + (EQ * layer + 2 * (m + 1)))
                        put((4 * par + m) % MSLOTS, (0, 2, 1)[n // 4], e + int(n // 4 != 1), n % 4)
                steps(sp, step_loads)

            def store_x(layer, x1):
                sp.wait_ge(x1_ok, 2 * NT * (layer + 1))
                sp.dma_start(x_res[layer].rearrange("(t p) d -> p t d", p=P), tok(x1)).then_inc(x1_stored, 16)

            sp.wait_ge(rows_in, 16 * 11)
            load_mod(0, 1, 2)
            for s in range(KB):
                load(ROUND_RG, s, ring[:, s, :], rg_w_in[s * P:(s + 1) * P, :])
            load_mod(3, 4)
            for s in range(4):
                load(ROUND_RG, KB + s, pair(KB + s), rows2(rg_w_out, s))
            sp.wait_ge(g_mm, KB)
            sp.dma_start(tok(r1)[:, 0:3, :], x_tiles[:, 0:3, :]).then_inc(x_in, 16)
            sp.wait_ge(mod_tr, 5)
            sp.dma_start(tok(r1)[:, 3:NT, :], x_tiles[:, 3:NT, :]).then_inc(x_in, 16)
            load_mod(5, 6, 7)
            store_x(0, r1)
            load_moe(0)
            load_mod(9, 10)
            sp.wait_ge(x_mid_in, 16)
            for s in range(KB):
                load(ROUND_AT, s, ring[:, s, 0:QKV], at_w_qkv[s * P:(s + 1) * P, :])
            load_mod(8)
            sp.wait_ge(qn_ok, NT)
            sp.dma_start(new_k, qn[:, NH * HD:NQK * HD]).then_inc(kv_stored, 16)
            sp.wait_ge(v_ok, NT)
            sp.dma_start(new_v, v_s[:, TL, :]).then_inc(kv_stored, 16)
            for s in range(4):
                load(ROUND_AT, KB + s, pair(KB + s), rows2(at_w_o, s))
            load_mod(11)
            store_x(1, r2)
            load_moe(1)
            sp.wait_ge(st_row_ok, 1)
            sp.dma_start(new_state.rearrange("s (b p) -> (s b) p", p=P), st_row[:, :]).then_inc(stored, 16)
            sp.wait_ge(stored, 16)
            sp.wait_ge(kv_stored, 32)
            sp.wait_ge(x1_stored, 32)
            sp.wait_ge(xh_stored, 32)
            sp.wait_ge(scattered, 16 * 2 * NE)

        @block.gpsimd
        def _(pool):
            n = [0]

            def step(ins):
                n[0] += 1
                ins.then_inc(pool_s, 1)
                pool.wait_ge(pool_s, n[0])

            step(nc.gpsimd.memset(ident[:, :], 0.0))
            nc.gpsimd.affine_select(out=ident[:, :], in_=ident[:, :], compare_op=ALU.not_equal, fill=1.0,
                                    base=0, pattern=[[-1, P]], channel_multiplier=1).then_inc(consts, 1)
            nc.gpsimd.memset(bd, 0.0).then_inc(consts, 1)
            nc.gpsimd.memset(ones[:, :], 1.0).then_inc(consts, 1)

            def mod_bias(n):
                v = MOD_ORDER[n]
                pool.wait_ge(mod_read, n + 1)
                nc.gpsimd.tensor_tensor(mod[:, v // NMOD, v % NMOD], modraw[:, n % 2],
                                        vec[:, :, R_MODB + v:R_MODB + v + 1].to_broadcast([P, KB, 2]),
                                        ALU.add).then_inc(mod_ok, 1)

            pool.wait_ge(vec_ok, 1)
            for v in range(3):
                mod_bias(v)
            pool.wait_ge(tr_mm, 2 * KB)
            nc.gpsimd.memset(upad, 0.0).then_inc(consts, 1)

            def column_high(n):
                cols = (D if n % 2 == 0 else 0) + n // 2 * P
                if n >= 2:
                    pool.wait_ge((u_mm, g_mm)[n % 2], n // 2)
                nc.gpsimd.tensor_copy(wcol[n % 2][:, 0], ring[:, 0:KB, cols:cols + P]).then_inc(wcol_hi_ok, 1)

            pool.wait_ge(ring_used, used(0, SLOTS - 1))
            for s in range(KB):
                pool.wait_ge(slot_ready[s], ready(ROUND_RG, s))
                ins = nc.gpsimd.tensor_copy(wcol[0][:, 0, s], ring[:, s, D:D + P])
            ins.then_inc(wcol_hi_ok, 1)
            for b in range(KB + 1):
                if b < KB:
                    column_high(2 * b + 1)
                if b < KB - 1:
                    column_high(2 * b + 2)
                if b >= 1:
                    uc = ucs[(b - 1) % 2]
                    pool.wait_ge(sig_ok, 8 * b)
                    pool.wait_ge(conv_ok, b)
                    nc.gpsimd.tensor_tensor(ig[:, :, 0:NLAT], ig[:, :, 0:NLAT],
                                            uc[:, 0:NLAT].unsqueeze(1).to_broadcast([P, 2, NLAT]), ALU.mult).then_inc(iu_ok, 1)
                    nc.gpsimd.tensor_tensor(ig[:, :, NLAT:], ig[:, :, NLAT:],
                                            uc[:, C0:].unsqueeze(1).to_broadcast([P, 2, NCTX]), ALU.mult).then_inc(iu_ok, 1)
            for k in range(KB // 2):
                pool.wait_ge(wo_hi_ok, k + 1)
                nc.gpsimd.tensor_tensor(wo_hl[:, k, 1, :], ring[:, KB + k // 2, (k % 2) * D:(k % 2 + 1) * D],
                                        wo_hl[:, k, 0, :].bitcast(F32), ALU.subtract).then_inc(wo_lo_ok, 1)
            for v in range(3, 5):
                mod_bias(v)

            def experts(layer):
                base = layer * NE
                pool.wait_ge(x1_ok, 2 * NT * (layer + 1))
                nc.gpsimd.memset(tk[0:48, :], -1.0).then_inc(tk_set, 1)
                mod_bias(5 + NMOD * layer)
                pool.wait_ge(mod_ok, NMOD * (layer + 1))
                for s in range(2):
                    nc.gpsimd.memset(sel[:, s, :], 0.0).then_inc(sel_ok, 1)
                    pool.wait_ge(sel_ok, 4 * layer + 2 * s + 1)
                    nc.gpsimd.memset(sel[:, s, slice(0, CL) if s == 0 else slice(CL, CE)], 1.0).then_inc(sel_ok, 1)
                for s in range(2):
                    nc.gpsimd.tensor_tensor(diag2[:, s], ident[:, :].unsqueeze(1).to_broadcast([P, KB, P]),
                                            mod[:, layer, 5, :, s:s + 1].to_broadcast([P, KB, P]), ALU.mult).then_inc(diag2_ok, 1)
                for m, src in enumerate((amod[:, 2 * layer + 1], mod[:, layer, 3])):
                    if m == 0:
                        pool.wait_ge(amod_ok, 2 * layer + 2)
                    exm = ex[m].rearrange("p (k n) -> p k n", k=KB)
                    nc.gpsimd.tensor_copy(exm[:, :, 0:CL], src[:, :, 0:1].to_broadcast([P, KB, CL])).then_inc(ex_ok, 1)
                    nc.gpsimd.tensor_copy(exm[:, :, CL:CE], src[:, :, 1:2].to_broadcast([P, KB, CC])).then_inc(ex_ok, 1)
                pool.wait_ge(route_ok, 2 * (layer + 1))
                pool.wait_ge(xh_stored, 16 * (layer + 1))
                pool.wait_ge(x1_stored, 16 * (layer + 1))

                def gather():
                    nc.gpsimd.indirect_dma_start(xg[0:CE, :], None, x_hat[layer],
                                                 bass.IndirectOffsetOnAxis(ap=gi[:, 0:1], axis=0)).then_inc(gathered, 16)

                def passed():
                    pool.sem_inc(waits_passed, 1)

                def scatter():
                    nc.gpsimd.indirect_dma_start(x_res[layer], bass.IndirectOffsetOnAxis(ap=si[:, 0:1], axis=0), ob[0:CE, :],
                                                 None, compute_op=ALU.add).then_inc(scattered, 16)

                def next_rows(e):
                    if not isinstance(e, int) or e:
                        pool.wait_ge(gathered, e * 16 + 16 * base)
                        pool.wait_ge(xtr_mm, e + base)
                    nc.gpsimd.tensor_copy(gi[:, :], idx_t[:, bass.ds(e, 1)]).then_inc(gi_ok, 1)
                    pool.wait_ge(gi_ok, e + (base + 1))
                    passed()
                    gather()

                def body(e, i, par, more, rows_left):
                    nc.gpsimd.tensor_copy(sg[:, :], g_t[:, bass.ds(e, 1)]).then_inc(sg_ok, 1)
                    nc.gpsimd.tensor_copy(si[:, :], idx_t[:, bass.ds(e, 1)]).then_inc(si_ok, 1)
                    if rows_left:
                        next_rows(e + 2)
                    pool.wait_ge(y_act, e + (base + 1))
                    nc.gpsimd.tensor_tensor(ob[0:CE, :], ob[0:CE, :], gg[0:CE, :], ALU.mult).then_inc(ob_ok, 1)
                    pool.wait_ge(ob_ok, e + (base + 1))
                    pool.wait_ge(si_ok, e + (base + 1))
                    passed()
                    scatter()
                    pool.wait_ge(scattered, e * 16 + 16 * (base + 1))

                next_rows(0)
                if layer == 0:
                    for v in range(6, 8):
                        mod_bias(v)
                next_rows(1)
                pool.wait_ge(gg_ok, layer + 1)
                steps(pool, body)

            experts(0)
            pool.dma_start(tok(r2), x_mid.rearrange("(t p) d -> p t d", p=P)).then_inc(x_mid_in, 16)
            pool.dma_start(kc, cache_k).then_inc(small_in, 16)
            pool.dma_start(v_s[:, 5, :], cache_v).then_inc(small_in, 16)
            pool.dma_start(gains[:, 0:NH * HD].rearrange("p (h n) -> p h n", n=HD),
                              at_q_norm.unsqueeze(1).to_broadcast([P, NH, HD])).then_inc(small_in, 16)
            pool.dma_start(gains[:, NH * HD:].rearrange("p (h n) -> p h n", n=HD),
                              at_k_norm.unsqueeze(1).to_broadcast([P, NKV, HD])).then_inc(small_in, 16)
            for s in range(2):
                pool.dma_start(tab[:, s], rope[s].rearrange("(t p) n -> p t n", p=P)).then_inc(small_in, 16)
            pool.dma_start(sinks[:, 0, :], at_sink.to_broadcast([P, NH])).then_inc(small_in, 16)
            for v in range(8, 10):
                mod_bias(v)
            pool.wait_ge(small_in, 16 * 7)
            for a in range(2):
                nc.gpsimd.tensor_copy(kdup[:, :, a, :], kc.rearrange("p (g n) -> p g n", g=NKV)).then_inc(kdup_ok, 1)
            nc.gpsimd.tensor_scalar(gains[:, 0:NH * HD], gains[:, 0:NH * HD], float(HD) ** -0.5, None, ALU.mult).then_inc(gains_ok, 1)
            nc.gpsimd.tensor_scalar(sinks[:, 1, :], sinks[:, 0, :], -1.0, None, ALU.mult).then_inc(sink_ok, 1)
            for t in range(NT):
                pool.wait_ge(qn_ok, t + 1)
                pool.wait_ge(k_mm, t + 1)
                for a in range(2):
                    nc.gpsimd.tensor_copy(kdup[:, :, a, :], qn[:, NH * HD:].rearrange("p (g n) -> p g n", g=NKV)).then_inc(kdup_ok, 1)
            pool.wait_ge(k_mm, NT + 1)
            pool.wait_ge(q_mm, NT)
            step(nc.gpsimd.memset(mask, 0.0))
            nc.gpsimd.affine_select(out=mask[:, P:2 * P], in_=mask[:, P:2 * P], compare_op=ALU.is_ge, fill=NEG,
                                    base=0, pattern=[[1, P]], channel_multiplier=-1).then_inc(consts, 1)
            nc.gpsimd.affine_select(out=mask[:, 3 * P:4 * P], in_=mask[:, 3 * P:4 * P], compare_op=ALU.is_ge, fill=NEG,
                                    base=0, pattern=[[-1, P]], channel_multiplier=1).then_inc(consts, 1)
            mod_bias(10)
            for k in range(KB):
                pool.wait_ge(slot_ready[KB + k // 2], ready(ROUND_AT, KB + k // 2))
                pool.wait_ge(qkv_mm, NT)
                w = ring[:, KB + k // 2, (k % 2) * D:(k % 2 + 1) * D]
                nc.gpsimd.tensor_copy(wo_hl[:, k, 0, :], w).then_inc(wo_hi_ok, 1)
                pool.wait_ge(wo_hi_ok, KB + k + 1)
                nc.gpsimd.tensor_tensor(wo_hl[:, k, 1, :], w, wo_hl[:, k, 0, :].bitcast(F32), ALU.subtract).then_inc(wo_lo_ok, 1)
            experts(1)

        @block.tensor
        def _(pe):
            def wait_slot(rnd, s):
                pe.wait_ge(slot_ready[s], ready(rnd, s))

            behind = []

            def modulation(*vectors, turn_last=True):
                def turn_row(v):
                    pe.wait_ge(mod_row, v + 1)
                    if v:
                        pe.wait_ge(mod_read, v)
                    for b in range(KB):
                        mm = nc.tensor.transpose(ps[:, 2, 2 * b:2 * b + 2], mod_rows(v)[0:2, b * P:(b + 1) * P], ident[0:2, 0:2])
                    mm.then_inc(mod_tr, 1)

                for n in vectors:
                    v = MOD_ORDER[n]
                    if n:
                        pe.wait_ge(mod_row, n)
                    for s in range(4):
                        slot = 4 * (v % 3) + s
                        wait_slot(MOD_ROUNDS[v // 3], slot)
                        for k in range(2):
                            for h in range(2):
                                mm = nc.tensor.matmul(ps[0:2, mod_bank(n) + h, :], cond[:, 2 * s + k, :],
                                                      ring[:, slot, k * D + h * 512:k * D + (h + 1) * 512],
                                                      start=(s + k == 0), stop=(s == 3 and k == 1))
                        mm.then_inc(ring_used, 1)
                    if behind:
                        turn_row(behind.pop())
                    behind.append(n)
                if turn_last:
                    turn_row(behind.pop())

            def gate_rows(layer, src_diag):
                for s in range(2):
                    pe.wait_ge(diag_ok, 2 * layer + s + 1)
                    for n in range(2):
                        mm = nc.tensor.matmul(ps[:, 4 + 2 * s + n, :], ones[:, :], src_diag[:, s, 4 * n:4 * n + 4, :],
                                              start=True, stop=True)
                    mm.then_inc(gate_mm, 1)

            def turn(phase, route=None):
                xh, n0 = tok(NORMS[phase][1]), KB * phase
                pe.wait_ge(xhat_ok, NT * (phase + 1))
                pe.wait_ge(router_in, 32)
                for b in range(KB + 1):
                    if b < KB:
                        if b >= 2:
                            pe.wait_ge(tr_act, n0 + b - 1)
                            pe.wait_ge(tr_dve, n0 + b - 1)
                        for t in range(TL):
                            mm = nc.tensor.transpose(ps[:, b % 2, t * P:(t + 1) * P], xh[:, t, b * P:(b + 1) * P], ident[:, :])
                        mm.then_inc(tr_mm, 1)
                        nc.tensor.transpose(ps[:, 2 + b % 2, 0:P], xh[:, TL, b * P:(b + 1) * P], ident[:, :]).then_inc(tr_mm, 1)
                    if route is not None and b >= 1:
                        k = b - 1
                        pe.wait_ge(tr_act, n0 + k + 1)
                        pe.wait_ge(tr_dve, n0 + k + 1)
                        for t in range(NT):
                            mm = nc.tensor.matmul(ps[:, 4, t * NE:(t + 1) * NE], feat(xn2)[:, k, t * P:(t + 1) * P],
                                                  router[:, route, k, :], start=(k == 0 and t == 0),
                                                  stop=(k == KB - 1), skip_group_check=True)
                if route is not None:
                    mm.then_inc(lg_mm, 1)

            def mixer_out(layer, after_first=None):
                for t in range(NT):
                    if t >= 2:
                        pe.wait_ge(out_mul, 2 * (NT * layer + t - 1))
                    toks = slice(t * P, (t + 1) * P)
                    for k in range(KB):
                        if t == 0:
                            for ok in (wo_hi_ok, wo_lo_ok, mo_hi_ok, mo_lo_ok):
                                pe.wait_ge(ok, KB * layer + k + 1)
                        for x, part in ((mo_hi, 0), (mo_hi, 1), (mo_lo[layer], 0)):
                            for n in range(2):
                                mm = nc.tensor.matmul(ps[:, 2 * (t % 2) + n, :], x[:, k, toks], wo_hl[:, k, part, n * 512:(n + 1) * 512],
                                                      start=(k == 0 and x is mo_hi and part == 0),
                                                      stop=(k == KB - 1 and x is not mo_hi))
                    mm.then_inc(out_mm, 1)
                    if t == 0 and after_first is not None:
                        after_first()

            def routes(layer):
                pe.wait_ge(aff_ok, layer + 1)
                for t in range(TL):
                    nc.tensor.transpose(ps[0:NE, 5, t * P:(t + 1) * P], lg[:, t, :], ident[:, :])
                nc.tensor.transpose(ps[0:NE, 3, 0:P], lg[:, TL, :], ident[:, :]).then_inc(aff_mm, 1)

            def chosen(layer):
                pe.wait_ge(comb_ok, 4 * (layer + 1))
                nc.tensor.transpose(ps[0:CE, 4, 0:NE], comb[0:NE, 0, :], ident[0:NE, 0:NE])
                nc.tensor.transpose(ps[0:CE, 4, NE:2 * NE], comb[0:NE, 1, :], ident[0:NE, 0:NE]).then_inc(comb_mm, 1)

            def gate_columns(layer):
                pe.wait_ge(diag2_ok, 2 * (layer + 1))
                pe.wait_ge(sel_ok, 4 * (layer + 1))
                for n in range(2):
                    for s in range(2):
                        mm = nc.tensor.matmul(ps[0:CE, n, :], sel[:, s, :], diag2[:, s, 4 * n:4 * n + 4, :],
                                              start=(s == 0), stop=(s == 1))
                mm.then_inc(gg_mm, 1)

            def experts(layer):
                base = layer * NE

                def product(e, q0, bank, xhl):
                    for k in range(KB):
                        w = whl[:, (q0 + k) % HL]
                        pe.wait_ge(whi_ok, block_of(layer, e, q0 + k))
                        for part in range(2):
                            for n in range(2):
                                nc.tensor.matmul(ps[0:CE, bank + n, :], xhl[:, part, k, :], w[:, 0, n * 512:(n + 1) * 512],
                                                 start=(k == 0 and part == 0), stop=False)
                        pe.wait_ge(wlo_ok, block_of(layer, e, q0 + k))
                        for n in range(2):
                            mm = nc.tensor.matmul(ps[0:CE, bank + n, :], xhl[:, 0, k, :], w[:, 1, n * 512:(n + 1) * 512],
                                                  start=False, stop=(k == KB - 1))
                        mm.then_inc(whl_used, 1)
                        yield k

                def run(blocks):
                    for _ in blocks:
                        pass

                def x_turn(e):
                    pe.wait_ge(gathered, e * 16 + 16 * (base + 1))
                    if not isinstance(e, int) or e >= 2:
                        pe.wait_ge(hh_ok, e + (base - 1))
                        pe.wait_ge(hl_ok, e + (base - 1))
                    elif e:
                        pe.wait_ge(xt_mul, base + 1)
                    for b in range(KB):
                        mm = nc.tensor.transpose(ps[:, 6 + b // 4, (b % 4) * CE:(b % 4 + 1) * CE], xg[0:CE, b * P:(b + 1) * P],
                                                 ident[0:CE, 0:CE])
                    mm.then_inc(xtr_mm, 1)

                def h_turn(e, read):
                    pe.wait_ge(h_ok, e + (base + 1))
                    pe.wait_ge(xt_mul, read)
                    for b in range(KB):
                        mm = nc.tensor.transpose(ps[:, 6 + b // 4, (b % 4) * CE:(b % 4 + 1) * CE], hid[0:CE, b * P:(b + 1) * P],
                                                 ident[0:CE, 0:CE])
                    mm.then_inc(htr_mm, 1)

                def gate_up(e, q0, bank, par):
                    return product(e, q0, bank, xs_hl[:, 1 - par])

                def body(e, i, par, more, rows_left):
                    if more:
                        pe.wait_ge(xh_ok, e + (base + 2))
                        pe.wait_ge(xl_ok, e + (base + 2))
                        pe.wait_ge(sil_ok, e + (base + 1))
                        for k in gate_up(e, 0, 0, par):
                            if k == 2:
                                h_turn(e, e + (base + 2))
                    else:
                        h_turn(e, base + NE)
                    pe.wait_ge(hh_ok, e + (base + 1))
                    pe.wait_ge(hl_ok, e + (base + 1))
                    run(product(e, 8 if more else 0, 4, hs_hl))
                    if rows_left:
                        x_turn(e + 2)
                    if more:
                        pe.wait_ge(h_ok, e + (base + 1))
                        run(gate_up(e, 16, 2, par))

                pe.wait_ge(gate_ok, 4 * (layer + 1))
                x_turn(0)
                pe.wait_ge(xh_ok, base + 1)
                pe.wait_ge(xl_ok, base + 1)
                pe.wait_ge(gg_ok, layer + 1)
                run(gate_up(-1, 8, 0, 1))
                x_turn(1)
                run(gate_up(-1, 16, 2, 1))
                steps(pe, body)

            pe.wait_ge(consts, 1)
            pe.wait_ge(rows_in, 16 * 11)
            for b in range(KB):
                mm = nc.tensor.transpose(ps[:, 0, b * 32:b * 32 + NROWS], rows[0:NROWS, b * P:(b + 1) * P],
                                         ident[0:NROWS, 0:NROWS])
            mm.then_inc(rows_t, 1)
            pe.wait_ge(cond_ok, 1)
            modulation(0, 1, 2)
            pe.wait_ge(mod_read, 3)
            turn(0)
            pe.wait_ge(tr_act, KB)
            pe.wait_ge(tr_dve, KB)
            pe.wait_ge(mx_hi_ok, KB)
            pe.wait_ge(mx_lo_ok, KB)
            xf = feat(r1)
            HT = NTOK // 2

            def project(n, banks, gates_read, done):
                pe.wait_ge(wcol_hi_ok, n + 1)
                pe.wait_ge(wcol_lo_ok, n + 1)
                w = wcol[n % 2]
                for h, bank in enumerate(banks):
                    toks = slice(h * HT, (h + 1) * HT)
                    if h == 1 and gates_read:
                        pe.wait_ge(sig_ok, gates_read)
                    for k in range(KB):
                        nc.tensor.matmul(ps[:, bank, 0:HT], w[:, 0, k, :], mx_hi[:, k, toks], start=(k == 0), stop=False)
                        nc.tensor.matmul(ps[:, bank, 0:HT], w[:, 0, k, :], mx_lo[:, k, toks], start=False, stop=False)
                        mm = nc.tensor.matmul(ps[:, bank, 0:HT], w[:, 1, k, :], mx_hi[:, k, toks], start=False, stop=(k == KB - 1))
                mm.then_inc(done, 1)

            for b in range(KB + 1):
                if b < KB:
                    if b >= 1:
                        pe.wait_ge(u_ok, 3 * b)
                    project(2 * b, (0, 1), 0, u_mm)
                if b == KB:
                    pe.wait_ge(u_ok, 3 * KB)
                    modulation(3, turn_last=False)
                if b >= 1:
                    pe.wait_ge(conv_ok, b)
                    pe.wait_ge(bd_in, 16 * 8)
                    pe.wait_ge(gel_ok, 2 * b)
                    if b >= 2:
                        pe.wait_ge(sig_ok, 8 * (b - 1))
                    for m in range(4):
                        nc.tensor.matmul(ps[:, 4 + m, :], bd[:, m, b - 1, :], ucs[(b - 1) % 2][:, 0:NLAT], start=True, stop=True)
                        mm = nc.tensor.matmul(ps[:, 3, m * P:(m + 1) * P], bd[:, m, b - 1, :], ucs[(b - 1) % 2][:, C0:],
                                              start=True, stop=True)
                    mm.then_inc(z_mm, 1)
                if b < KB:
                    if b >= 1:
                        pe.wait_ge(gel_ok, 2 * b)
                    project(2 * b + 1, (2, 3), 8 * b - 4 if b else 0, g_mm)
            pe.wait_ge(gel_ok, 2 * KB)
            modulation(4)
            pe.wait_ge(mod_read, 5)
            pe.wait_ge(consts, 3)
            pe.wait_ge(sig_ok, 8 * KB)
            mixer_out(0, lambda: gate_rows(0, diag))
            pe.wait_ge(st_ok, 2 * KB)
            nc.tensor.transpose(ps[0:16, 4, 0:P], stv[:, :, :].rearrange("p s b -> p (s b)"), ident[:, :]).then_inc(st_mm, 1)
            pe.wait_ge(gate_ok, 4)
            modulation(5, turn_last=False)
            pe.wait_ge(st_row_ok, 1)
            turn(1, 0)
            routes(0)
            modulation()
            modulation(6)
            chosen(0)
            gate_columns(0)
            modulation(7)
            experts(0)

            def turn_k(n, bank):
                pe.wait_ge(kdup_ok, 2 * (n + 1))
                for g in range(NKV):
                    mm = nc.tensor.transpose(ps[:, bank, g * P:(g + 1) * P], kdup[:, g].rearrange("p a n -> p (a n)"), ident[:, :])
                mm.then_inc(k_mm, 1)

            modulation(8, 9)
            pe.wait_ge(mod_read, 10)
            turn(2)
            pe.wait_ge(tr_act, 3 * KB)
            pe.wait_ge(tr_dve, 3 * KB)
            pe.wait_ge(mod_row, 10)
            turn_k(0, 6)

            def turn_q(t):
                pe.wait_ge(qn_ok, t + 1)
                pe.wait_ge(k_ok, t + 1)
                if t >= 1:
                    pe.wait_ge(q_dve, t)
                for h in range(KB):
                    mm = nc.tensor.transpose(ps[:, 6 + h // 4, (h % 4) * P:(h % 4 + 1) * P], qn[:, h * P:(h + 1) * P], ident[:, :])
                mm.then_inc(q_mm, 1)
                pe.wait_ge(q_act, t + 1)
                turn_k(t + 1, 6)

            for t in range(NT):
                if t >= 2:
                    pe.wait_ge(qn_read, t - 1)
                    pe.wait_ge(v_ok, t - 1)
                pe.wait_ge(xq_hi_ok, t + 1)
                pe.wait_ge(xq_lo_ok, t + 1)
                for k in range(KB):
                    if t == 0:
                        pe.wait_ge(wq_hi_ok, 2 * (k + 1))
                        pe.wait_ge(wq_lo_ok, 2 * (k + 1))
                    high = [wq_hi[:, k, 0:512], wq_hi[:, k, 512:D], wq[:, k, QKV:QKV + 512]]
                    rest = [wq[:, k, n * 512:(n + 1) * 512] for n in range(3)]
                    x_hi, x_lo = xq_hi[:, t % 2, k, :], mo_lo[1][:, k, t * P:(t + 1) * P]
                    for m, (x, w) in enumerate(((x_hi, high), (x_hi, rest), (x_lo, high))):
                        for n in range(3):
                            mm = nc.tensor.matmul(ps[:, 3 * (t % 2) + n, :], x, w[n], start=(k == 0 and m == 0),
                                                  stop=(k == KB - 1 and m == 2))
                mm.then_inc(qkv_mm, 1)
                if t >= 1:
                    turn_q(t - 1)
            turn_q(NT - 1)
            pe.wait_ge(k_ok, NT + 1)
            pe.wait_ge(q_dve, NT)
            pe.wait_ge(qn_read, NT)
            pe.wait_ge(v_ok, NT)
            modulation(10)
            pe.wait_ge(mod_read, 11)
            for i in range(NU + 3):
                if i < NU:
                    j, hp = units[i]
                    if i >= 2:
                        pe.wait_ge(s_max, 2 * (i - 1))
                    for a in range(2):
                        for n, b0, m in runs(KEYB[j][0]):
                            mm = nc.tensor.matmul(ps[:, 2 * (i % 2) + a, n * P:(n + m) * P],
                                                  q_t[a * HD:(a + 1) * HD, hp, j * P:(j + 1) * P],
                                                  k_t[a * HD:(a + 1) * HD, hp // 2, b0 * P:(b0 + m) * P], start=True, stop=True)
                    mm.then_inc(s_mm, 1)
                if 1 <= i <= NU:
                    j, hp = units[i - 1]
                    pe.wait_ge(p_ok, 3 * i)
                    if i >= 2:
                        pe.wait_ge(pt_act, i - 1)
                        pe.wait_ge(pt_dve, i - 1)
                    if last_of_tile(i - 4):
                        pe.wait_ge(ot_act, (i - 4) // KB + 1)
                        pe.wait_ge(ot_dve, (i - 4) // KB + 1)
                    for a in range(2):
                        for n in range(len(KEYB[j][0])):
                            mm = nc.tensor.transpose(ps[:, 4 + a, n * P:(n + 1) * P], pm[:, (i - 1) % 2, a, n * P:(n + 1) * P], ident[:, :])
                    mm.then_inc(pt_mm, 1)
                if 2 <= i < NU + 2:
                    j, hp = units[i - 2]
                    pe.wait_ge(pt_act, i - 1)
                    pe.wait_ge(pt_dve, i - 1)
                    if i >= 4:
                        pe.wait_ge(o_ok, i - 3)
                    for a in range(2):
                        for n, b in enumerate(KEYB[j][0]):
                            mm = nc.tensor.matmul(ps[:, 6 + i % 2, a * HD:(a + 1) * HD], pt[:, i % 2, a, n * P:(n + 1) * P],
                                                  v_s[:, b, (hp // 2) * HD:(hp // 2 + 1) * HD], start=(n == 0),
                                                  stop=(n == len(KEYB[j][0]) - 1))
                    mm.then_inc(pv_mm, 1)
                if last_of_tile(i - 3):
                    j = (i - 3) // KB
                    pe.wait_ge(o_ok, KB * (j + 1))
                    if i <= NU:
                        pe.wait_ge(pt_act, i)
                        pe.wait_ge(pt_dve, i)
                    for b in range(KB):
                        mm = nc.tensor.transpose(ps[:, 4 + b // 4, (b % 4) * P:(b % 4 + 1) * P], gb[:, j % 2, b * P:(b + 1) * P], ident[:, :])
                    mm.then_inc(ot_mm, 1)
            pe.wait_ge(ot_act, NT)
            pe.wait_ge(ot_dve, NT)
            mixer_out(1, lambda: gate_rows(1, diag1))
            pe.wait_ge(gate_ok, 8)
            modulation(11, turn_last=False)
            turn(3, 1)
            routes(1)
            modulation()
            gate_columns(1)
            chosen(1)
            experts(1)

        @block.scalar
        def _(act):
            def copy(out, in_, done, n=1):
                nc.scalar.activation(out, in_, ACT.Copy).then_inc(done, n)

            def squares(phase, x_ready):
                for t in range(3):
                    if x_ready is not None:
                        act.wait_ge(x1_ok, x_ready + 2 * (t + 1))
                    nc.scalar.activation(w_junk, tok(NORMS[phase][0])[:, t, :], ACT.Square,
                                         accum_out=sm[:, phase, 0, t:t + 1]).then_inc(ssq_act, 1)
                    act.wait_ge(ssq_act, 3 * phase + t + 1)
                for g, ts in enumerate(NORM_TILES):
                    act.wait_ge(var_ok, 2 * phase + g + 1)
                    nc.scalar.activation(sm[:, phase, 1, ts], sm[:, phase, 0, ts], ACT.Sqrt).then_inc(std_ok, 1)

            def turned(phase, layer, between=None):
                out = feat(NORMS[phase][2])
                act.wait_ge(amod_ok, phase + 1)
                for b in range(KB):
                    act.wait_ge(tr_mm, 2 * (KB * phase + b) + 2 - (b + 1) % 2)
                    src, cols, st = ((ps[:, b % 2, :], slice(0, NLAT), 0) if b % 2 == 0
                                     else (ps[:, 2 + b % 2, 0:P], slice(NLAT, NTOK), 1))
                    nc.scalar.activation(out[:, b, cols], src, ACT.Identity, scale=amod[:, phase, b, st:st + 1],
                                         bias=mod[:, layer, 3 * (phase % 2), b, st:st + 1]).then_inc(tr_act, 1)
                    if between is not None:
                        between(b)

            behind = []

            def mod_reads(vs, between=None, turn_last=True):
                def turned_row(v):
                    act.wait_ge(mod_tr, v + 1)
                    if v >= 2:
                        act.wait_ge(mod_ok, v - 1)
                    copy(modraw[:, v % 2].rearrange("p b s -> p (b s)"), ps[:, 2, 0:2 * KB], mod_read)

                for n in vs:
                    v = MOD_ORDER[n]
                    act.wait_ge(ring_used, used(MOD_ROUNDS[v // 3], 4 * (v % 3) + 3))
                    copy(mod_rows(n)[0:2, :].rearrange("p (h n) -> p h n", h=2), ps[0:2, mod_bank(n):mod_bank(n) + 2, :], mod_row)
                    if between is not None and n == vs[0]:
                        between()
                    if behind:
                        turned_row(behind.pop())
                    behind.append(n)
                if turn_last:
                    turned_row(behind.pop())

            def out_weights_high(ks):
                for k in ks:
                    act.wait_ge(slot_ready[KB + k // 2], ready(ROUND_RG, KB + k // 2))
                    act.wait_ge(ring_used, used(MOD_ROUNDS[1], k))
                    copy(wo_hl[:, k, 0, :], ring[:, KB + k // 2, (k % 2) * D:(k % 2 + 1) * D], wo_hi_ok)

            def mixed_high(layer):
                if layer == 0:
                    act.wait_ge(hg_ok, KB)
                else:
                    act.wait_ge(ot_act, NT)
                    act.wait_ge(ot_dve, NT)
                for k in range(KB):
                    copy(mo_hi[:, k, :], feat((r2, r1)[layer])[:, k, :], mo_hi_ok)

            def gate_copy(layer, out):
                for s in range(2):
                    act.wait_ge(gate_mm, 2 * layer + s + 1)
                    for n in range(2):
                        copy(out[:, s, n * 512:(n + 1) * 512], ps[:, 4 + 2 * s + n, :], gate_ok)

            def softmax(layer):
                act.wait_ge(lg_sub, layer + 1)
                nc.scalar.activation(lg, lg, ACT.Exp).then_inc(lg_exp, 1)

            def store_xhat(layer):
                act.wait_ge(xhat_ok, NT * (2 * layer + 2))
                act.dma_start(x_hat[layer].rearrange("(t p) d -> p t d", p=P), tok(NORMS[2 * layer + 1][1])).then_inc(xh_stored, 16)

            def high(layer, e, i, par, q):
                n = 8 + USES * par + q // 2 if e is not None else q // 2 - 4
                slot = n % MSLOTS
                if q % 2 == 0:
                    act.wait_ge(slot_ready[slot], i * (16 * 2 * USES // MSLOTS)
                                + 16 * (ROUNDS[layer] + ESLOTS // MSLOTS * layer + n // MSLOTS + 1))
                if n >= HL // 2:
                    act.wait_ge(whl_used, block_of(layer, -1 if e is None else e, q) - HL)
                nc.scalar.activation(whl[:, q % HL, 0, :], ring[:, slot, (q % 2) * D:(q % 2 + 1) * D], ACT.Copy).then_inc(whi_ok, 1)

            def split_place(layer):
                act.wait_ge(ring_used, used((MOD_ROUNDS[1], MOD_ROUNDS[3])[layer], SLOTS - 1))

            def first_high(b):
                if b == 1:
                    split_place(1)
                if b % 2:
                    high(1, None, 0, 1, 8 + b // 2)

            def gate_columns(layer):
                act.wait_ge(gg_mm, layer + 1)
                copy(gg[0:CE, :].rearrange("p (h n) -> p h n", h=2), ps[0:CE, 0:2, :], gg_ok)

            def experts(layer):
                base = layer * NE
                def x_high(e, buf):
                    act.wait_ge(xt_ok, e + (base + 1))
                    copy(xs_hl[:, buf, 0].rearrange("p k n -> p (k n)"), xt, xh_ok)

                def silu(e):
                    if base or not isinstance(e, int) or e:
                        act.wait_ge(h_ok, e + base)
                    nc.scalar.activation(sil[0:CE, :].rearrange("p (h n) -> p h n", h=2), ps[0:CE, 0:2, :], ACT.Silu).then_inc(sil_ok, 1)

                def h_high(e):
                    act.wait_ge(htr_mm, e + (base + 1))
                    copy(hs_hl[:, 0].rearrange("p (h m) n -> p h (m n)", h=2), ps[:, 6:8, 0:4 * CE], hh_ok)

                def output(e):
                    act.wait_ge(sg_ok, e + (base + 1))
                    nc.scalar.activation(ob[0:CE, :].rearrange("p (h n) -> p h n", h=2), ps[0:CE, 4:6, :], ACT.Copy,
                                         scale=sg[:, 0:1]).then_inc(y_act, 1)

                def body(e, i, par, more, rows_left):
                    if not more:
                        for q in range(8):
                            high(layer, e, i, par, q)
                            if q == 3:
                                h_high(e)
                        act.wait_ge(whl_used, block_of(layer, e, 7))
                        output(e)
                        return
                    for q in range(2 * USES):
                        high(layer, e, i, par, q)
                        if q == 6:
                            h_high(e)
                        if q == 12:
                            silu(e + 1)
                        if q == 20:
                            output(e)
                        if q == 21 and rows_left:
                            x_high(e + 2, par)

                if layer == 0:
                    split_place(0)
                    high(0, None, 0, 1, 8)
                x_high(0, 0)
                for q in range((9, 12)[layer], 2 * USES):
                    high(layer, None, 0, 1, q)
                    if q == 20:
                        silu(0)
                    if q == 21:
                        x_high(1, 1)
                steps(act, body)

            vecs = ((R_C, c), (R_CCTX, c_ctx), (R_G1, norm1_g), (R_G2, norm2_g), (R_CW, rg_conv_w), (R_CB, rg_conv_b),
                    (R_BA, rg_b_a), (R_BX, rg_b_x), (R_LAM, rg_lambda), (R_H0, state), (R_MODB, mod_b))
            for r, v in vecs:
                act.dma_start(rows[r:r + v.shape[0], :], v).then_inc(rows_in, 16)
            act.dma_start(tok(r2), x_tiles).then_inc(x_in, 16)
            for l in range(2):
                act.dma_start(router[:, l], moe_router[l].rearrange("(k p) e -> p k e", p=P)).then_inc(router_in, 16)
            act.wait_ge(vec_ok, 1)
            nc.scalar.activation(cond[:, :, :], vec[:, :, R_C:R_C + 2], ACT.Sigmoid).then_inc(sig_c, 1)
            act.wait_ge(consts, 2)
            for m, w in enumerate((rg_w_a[0], rg_w_a[1], rg_w_x[0], rg_w_x[1])):
                for h in range(2):
                    act.dma_start(bd[h * RB:(h + 1) * RB, m, :, h * RB:(h + 1) * RB],
                                  w.rearrange("(c h) i j -> h i c j", h=2)[h]).then_inc(bd_in, 16)
            act.wait_ge(lam_abs, 1)
            nc.scalar.activation(spt[:, 3], spt[:, 1], ACT.Exp, scale=-1.0).then_inc(lam_exp, 1)
            act.wait_ge(x_in, 16)
            squares(0, None)
            mod_reads(range(3))
            act.wait_ge(amod_ok, 1)
            for b in range(KB):
                act.wait_ge(tr_mm, 2 * b + 2 - (b + 1) % 2)
                if b >= 2:
                    act.wait_ge(mx_lo_ok, b - 1)
                src, cols, st = ((ps[:, b % 2, :], slice(0, NLAT), 0) if b % 2 == 0
                                 else (ps[:, 2 + b % 2, 0:P], slice(NLAT, NTOK), 1))
                nc.scalar.activation(mx_raw[:, b % 2, cols], src, ACT.Identity, scale=amod[:, 0, b, st:st + 1],
                                     bias=mod[:, 0, 0, b, st:st + 1]).then_inc(tr_act, 1)
                act.wait_ge(tr_act, b + 1)
                act.wait_ge(tr_dve, b + 1)
                copy(mx_hi[:, b, :], mx_raw[:, b % 2, :], mx_hi_ok)

            HT = NTOK // 2
            act.wait_ge(consts, 4)
            for b in range(KB + 1):
                if b < KB:
                    act.wait_ge(u_mm, b + 1)
                    if b >= 1:
                        act.wait_ge(conv_ok, b)
                    copy(upad[:, 2:2 + HT], ps[:, 0, 0:HT], u_ok)
                    copy(upad[:, 2 + HT:2 + NLAT], ps[:, 1, 0:NLAT - HT], u_ok)
                    copy(upad[:, 4 + NLAT:4 + NLAT + NCTX], ps[:, 1, NLAT - HT:HT], u_ok)
                if b == KB:
                    mod_reads([3], turn_last=False)
                if b >= 1:
                    c1 = b - 1
                    act.wait_ge(z_mm, b)
                    if b >= 2:
                        act.wait_ge(ig_used, c1)
                    for cols in (slice(NLAT, NTOK), slice(0, NLAT)):
                        for m, row in enumerate((R_BA, R_BA + 1, R_BX, R_BX + 1)):
                            nc.scalar.activation((rt, ig)[m // 2][:, m % 2, cols],
                                                 ps[:, 3, m * P:(m + 1) * P] if cols.start else ps[:, 4 + m, :],
                                                 ACT.Sigmoid, bias=vec[:, c1, row:row + 1]).then_inc(sig_ok, 1)
                    act.wait_ge(sig_ok, 8 * b)
                    act.wait_ge(sp_ok, 2)
                    if b >= 3:
                        act.wait_ge(hg_ok, c1 - 1)
                    for s in range(2):
                        nc.scalar.activation(aas[c1 % 2][:, s], rt[:, s], ACT.Exp, scale=spn[:, c1, s:s + 1]).then_inc(a_ok, 1)
                    for s in range(2):
                        nc.scalar.activation(rt[:, s], rt[:, s], ACT.Tanh, scale=sp4[:, c1, s:s + 1]).then_inc(tanh_ok, 1)
                    act.wait_ge(tanh_ok, 2 * b)
                    if b >= 2:
                        act.wait_ge(scan_ok, 4 * c1)
                    nc.scalar.activation(sq, rt, ACT.Sqrt).then_inc(sqrt_ok, 1)
                if b < KB:
                    act.wait_ge(g_mm, b + 1)
                    if b >= 2:
                        act.wait_ge(hg_ok, b - 1)
                    gel = gels[b % 2]
                    nc.scalar.activation(gel[:, 0:HT], ps[:, 2, 0:HT], ACT.Gelu_apprx_tanh).then_inc(gel_ok, 1)
                    nc.scalar.activation(gel[:, HT:], ps[:, 3, 0:HT], ACT.Gelu_apprx_tanh).then_inc(gel_ok, 1)
            out_weights_high(range(KB // 2))
            mod_reads([4])
            mixed_high(0)
            out_weights_high(range(KB // 2, KB))
            gate_copy(0, gb)
            squares(1, 0)
            mod_reads([5], turn_last=False)
            store_xhat(0)
            turned(1, 0)
            softmax(0)
            mod_reads([])
            mod_reads([6])
            gate_columns(0)
            mod_reads([7])
            experts(0)

            def x_squares():
                act.wait_ge(x_mid_in, 16)
                squares(2, None)

            mod_reads([8, 9], x_squares)
            turned(2, 1)

            def input_high(t):
                if t >= 2:
                    act.wait_ge(qkv_mm, t - 1)
                if t == 0:
                    act.wait_ge(tr_act, 3 * KB)
                    act.wait_ge(tr_dve, 3 * KB)
                copy(xq_hi[:, t % 2], feat(r1)[:, :, t * P:(t + 1) * P], xq_hi_ok)

            input_high(0)
            act.wait_ge(whl_used, EQ)
            for k in range(KB):
                act.wait_ge(slot_ready[k], ready(ROUND_AT, k))
                copy(wq_hi[:, k, :], ring[:, k, 0:D], wq_hi_ok)
                copy(wq[:, k, QKV:QKV + 512], ring[:, k, D:QKV], wq_hi_ok)
            act.wait_ge(k_mm, 1)
            copy(k_t[:, :, NTOK:KEYS], ps[:, 6, :], k_ok)

            def turned_q(t):
                act.wait_ge(q_mm, t + 1)
                copy(q_t[:, 0:4, t * P:(t + 1) * P], ps[:, 6, :], q_act)
                act.wait_ge(k_mm, t + 2)
                copy(k_t[:, :, t * P:(t + 1) * P], ps[:, 6, :], k_ok)

            for t in range(NT):
                if t < NT - 1:
                    input_high(t + 1)
                act.wait_ge(qkv_mm, t + 1)
                z = 3 * (t % 2)
                if t >= 1:
                    act.wait_ge(qn_ok, t)
                for n, w in ((0, 512), (1, 512), (2, 256)):
                    nc.scalar.activation(qs[:, n * 512:n * 512 + w], ps[:, z + n, 0:w], ACT.Square).then_inc(qsq_ok, 1)
                copy(v_s[:, t, :], ps[:, z + 2, 256:512], v_ok)
                act.wait_ge(qvar_ok, t + 1)
                nc.scalar.activation(ss20[:, 1], ss20[:, 0], ACT.Sqrt).then_inc(qstd_ok, 1)
                if t >= 1:
                    turned_q(t - 1)
            turned_q(NT - 1)
            mod_reads([10])
            for i in range(NU + 3):
                if i < NU:
                    j, hp = units[i]
                    act.wait_ge(nm_ok, i + 1)
                    w = len(KEYB[j][0]) * P
                    for a in range(2):
                        nc.scalar.activation(pm[:, i % 2, a, 0:w], pm[:, i % 2, a, 0:w], ACT.Exp, bias=stat[:, i % 4, 1, a:a + 1],
                                             accum_out=stat[:, i % 4, 3, a:a + 1]).then_inc(p_ok, 1)
                    nc.scalar.activation(stat[:, i % 4, 4, :], stat[:, i % 4, 2, :], ACT.Exp).then_inc(p_ok, 1)
                if 1 <= i <= NU:
                    w = len(KEYB[units[i - 1][0]][0]) * P
                    act.wait_ge(pt_mm, i)
                    if i >= 3:
                        act.wait_ge(pv_mm, i - 2)
                    copy(pt[:, (i - 1) % 2, 0, 0:w], ps[:, 4, 0:w], pt_act)
                if last_of_tile(i - 3):
                    j = (i - 3) // KB
                    act.wait_ge(ot_mm, j + 1)
                    copy(feat(r1)[:, 0:4, j * P:(j + 1) * P], ps[:, 4, :], ot_act)
            mixed_high(1)
            gate_copy(1, gb1)
            squares(3, 2 * NT)
            mod_reads([11], turn_last=False)
            store_xhat(1)
            turned(3, 1, first_high)
            softmax(1)
            mod_reads([])
            gate_columns(1)
            experts(1)

        @block.vector
        def _(eng):
            n = [0]

            def step(ins):
                n[0] += 1
                ins.then_inc(dve, 1)
                eng.wait_ge(dve, n[0])

            v = nc.vector

            def norm_sums(phase, g):
                x, ts = tok(NORMS[phase][0]), NORM_TILES[g]
                t = ts.stop - 1
                v.tensor_tensor_reduce(out=w_junk2, in0=x[:, t, :], in1=x[:, t, :], scale=1.0, scalar=0.0,
                                       op0=ALU.mult, op1=ALU.add, accum_out=sm[:, phase, 0, t:t + 1]).then_inc(ssq_ok, 1)
                eng.wait_ge(ssq_ok, 2 * phase + g + 1)
                eng.wait_ge(ssq_act, 3 * (phase + 1))
                v.tensor_scalar(sm[:, phase, 0, ts], sm[:, phase, 0, ts], 1.0 / D, EPS, ALU.mult, ALU.add).then_inc(var_ok, 1)

            def norm_scale(phase, g):
                x, xh, ts = tok(NORMS[phase][0]), tok(NORMS[phase][1]), NORM_TILES[g]
                eng.wait_ge(std_ok, 2 * phase + g + 1)
                step(v.reciprocal(sm[:, phase, 2, ts], sm[:, phase, 1, ts]))
                for t in range(ts.start, ts.stop):
                    v.tensor_scalar(xh[:, t, :], x[:, t, :], sm[:, phase, 2, t:t + 1], None, ALU.mult).then_inc(xhat_ok, 1)

            def norm_end(phase):
                norm_sums(phase, 1)
                norm_scale(phase, 0)
                norm_scale(phase, 1)

            def turned(phase, layer, between=None):
                eng.wait_ge(mod_ok, NMOD * layer + 3 * (phase % 2) + 2)
                row = (R_G1, R_G2)[phase % 2] + layer
                v.scalar_tensor_tensor(out=amod[:, phase], in0=mod[:, layer, 3 * (phase % 2) + 1], scalar=1.0,
                                       in1=vec[:, :, row:row + 1].to_broadcast([P, KB, 2]), op0=ALU.add,
                                       op1=ALU.mult).then_inc(amod_ok, 1)
                eng.wait_ge(amod_ok, phase + 1)
                out = feat(NORMS[phase][2])
                for b in range(KB):
                    eng.wait_ge(tr_mm, 2 * (KB * phase + b) + 1 + (b + 1) % 2)
                    src, cols, st = ((ps[:, b % 2, :], slice(0, NLAT), 0) if b % 2 == 1
                                     else (ps[:, 2 + b % 2, 0:P], slice(NLAT, NTOK), 1))
                    v.tensor_scalar(out[:, b, cols], src, amod[:, phase, b, st:st + 1],
                                    mod[:, layer, 3 * (phase % 2), b, st:st + 1], ALU.mult, ALU.add).then_inc(tr_dve, 1)
                    if between is not None:
                        between(b)

            def diagonals(layer, out):
                eng.wait_ge(mod_ok, (3, 11)[layer])
                for s in range(2):
                    v.tensor_tensor(out[:, s], ident[:, :].unsqueeze(1).to_broadcast([P, KB, P]),
                                    mod[:, layer, 2, :, s:s + 1].to_broadcast([P, KB, P]), ALU.mult).then_inc(diag_ok, 1)

            def out_weights_rest():
                eng.wait_ge(wo_lo_ok, KB // 2)
                for k in range(KB // 2, KB):
                    eng.wait_ge(wo_hi_ok, k + 1)
                    v.tensor_tensor(wo_hl[:, k, 1, :], ring[:, KB + k // 2, (k % 2) * D:(k % 2 + 1) * D],
                                    wo_hl[:, k, 0, :].bitcast(F32), ALU.subtract).then_inc(wo_lo_ok, 1)

            def mixed_rest(layer):
                for k in range(KB):
                    eng.wait_ge(mo_hi_ok, KB * layer + k + 1)
                    v.tensor_tensor(mo_lo[layer][:, k, :], feat((r2, r1)[layer])[:, k, :], mo_hi[:, k, :].bitcast(F32),
                                    ALU.subtract).then_inc(mo_lo_ok, 1)

            def residual(layer, x1, g):
                x = tok(x1)
                eng.wait_ge(gate_ok, 4 * (layer + 1))
                for t in range(NT):
                    for h in range(2):
                        m = 2 * t + h
                        eng.wait_ge(out_mm, NT * layer + t + 1)
                        v.tensor_tensor(w_tmp[:, m % 2], ps[:, 2 * (t % 2) + h, :], g[:, t // TL, h * 512:(h + 1) * 512],
                                        ALU.mult).then_inc(out_mul, 1)
                        eng.wait_ge(out_mul, 2 * NT * layer + m + 1)
                        xs = x[:, t, h * 512:(h + 1) * 512]
                        v.tensor_tensor(xs, xs, w_tmp[:, m % 2], ALU.add).then_inc(x1_ok, 1)
                    if t >= NT - 2:
                        eng.wait_ge(x1_ok, 2 * NT * layer + 2 * (t + 1))
                        if t == NT - 2:
                            norm_sums(2 * layer + 1, 0)
                        else:
                            norm_end(2 * layer + 1)

            def route(layer):
                lgp = ps[:, 4, 0:NT * NE].rearrange("p (t n) -> p t n", t=NT)
                eng.wait_ge(lg_mm, layer + 1)
                step(v.tensor_reduce(mx5[:, 0, 0:NT], lgp, AX.X, ALU.max))
                v.tensor_tensor(lg, lgp, mx5[:, 0, 0:NT].unsqueeze(2).to_broadcast([P, NT, NE]), ALU.subtract).then_inc(lg_sub, 1)
                eng.wait_ge(lg_exp, layer + 1)
                step(v.tensor_reduce(mx5[:, 1, 0:NT], lg, AX.X, ALU.add))
                step(v.reciprocal(mx5[:, 1, 0:NT], mx5[:, 1, 0:NT]))
                v.tensor_tensor(lg, lg, mx5[:, 1, 0:NT].unsqueeze(2).to_broadcast([P, NT, NE]), ALU.mult).then_inc(aff_ok, 1)
                eng.wait_ge(tk_set, layer + 1)
                eng.wait_ge(aff_mm, layer + 1)
                step(v.tensor_copy(tk[0:NE, :], ps[0:NE, 5, :]))
                step(v.tensor_copy(tk[32:32 + NE, 0:NCTX], ps[0:NE, 3, 0:P]))
                for r in range(CL // 8):
                    k8 = slice(8 * r, 8 * r + 8)
                    step(v.max(tv[0:48, k8], tk[0:48, :]))
                    step(v.max_index(ti[0:48, k8], tv[0:48, k8], tk[0:48, :]))
                    if r < CL // 8 - 1:
                        step(v.match_replace(tk[0:48, :], tv[0:48, k8], tk[0:48, :], -1.0))
                v.tensor_copy(comb[0:NE, 0, 0:CL], tv[0:NE, :]).then_inc(comb_ok, 1)
                v.tensor_copy(comb[0:NE, 0, CL:CE], tv[32:32 + NE, 0:CC]).then_inc(comb_ok, 1)
                v.tensor_copy(comb[0:NE, 1, 0:CL], ti[0:NE, :]).then_inc(comb_ok, 1)
                v.tensor_scalar(comb[0:NE, 1, CL:CE], ti[32:32 + NE, 0:CC], float(NLAT), None, ALU.add).then_inc(comb_ok, 1)
                eng.wait_ge(comb_mm, layer + 1)
                v.tensor_copy(g_t[:, :], ps[0:CE, 4, 0:NE]).then_inc(route_ok, 1)
                v.tensor_copy(idx_t[:, :], ps[0:CE, 4, NE:2 * NE]).then_inc(route_ok, 1)

            def rest(layer, e, par, q):
                n = 8 + USES * par + q // 2 if e is not None else q // 2 - 4
                eng.wait_ge(whi_ok, block_of(layer, -1 if e is None else e, q))
                v.tensor_tensor(whl[:, q % HL, 1, :], ring[:, n % MSLOTS, (q % 2) * D:(q % 2 + 1) * D],
                                whl[:, q % HL, 0, :].bitcast(F32), ALU.subtract).then_inc(wlo_ok, 1)

            def first_rest(b):
                if b % 2:
                    rest(1, None, 1, 8 + b // 2)

            def experts(layer):
                base = layer * NE
                eng.wait_ge(ex_ok, 4 * (layer + 1))

                def halves(t):
                    return t.rearrange("p (h n) -> p h n", h=2)

                def x_mod(e):
                    eng.wait_ge(xtr_mm, e + (base + 1))
                    v.tensor_tensor(halves(xt), ps[:, 6:8, 0:4 * CE], halves(ex[0]), ALU.mult).then_inc(xt_mul, 1)
                    eng.wait_ge(xt_mul, e + (base + 1))
                    v.tensor_tensor(xt, xt, ex[1], ALU.add).then_inc(xt_ok, 1)

                def x_rest(e, buf):
                    eng.wait_ge(xh_ok, e + (base + 1))
                    v.tensor_tensor(xs_hl[:, buf, 1].rearrange("p k n -> p (k n)"), xt,
                                    xs_hl[:, buf, 0].rearrange("p k n -> p (k n)").bitcast(F32), ALU.subtract).then_inc(xl_ok, 1)

                def hidden(e):
                    eng.wait_ge(sil_ok, e + (base + 1))
                    v.tensor_tensor(halves(hid[0:CE, :]), ps[0:CE, 2:4, :], halves(sil[0:CE, :]), ALU.mult).then_inc(h_ok, 1)

                def h_rest(e):
                    eng.wait_ge(hh_ok, e + (base + 1))
                    v.tensor_tensor(hs_hl[:, 1].rearrange("p (h m) n -> p h (m n)", h=2), ps[:, 6:8, 0:4 * CE],
                                    hs_hl[:, 0].rearrange("p (h m) n -> p h (m n)", h=2).bitcast(F32), ALU.subtract).then_inc(hl_ok, 1)

                def body(e, i, par, more, rows_left):
                    for q in range(2 * USES if more else 8):
                        rest(layer, e, par, q)
                        if q == 3:
                            hidden(e)
                        if q == (6 if more else 3):
                            h_rest(e)
                        if q == 19 and rows_left:
                            x_mod(e + 2)
                        if q == 21 and rows_left:
                            x_rest(e + 2, par)

                x_mod(0)
                if layer == 0:
                    rest(0, None, 1, 8)
                x_rest(0, 0)
                for q in range((9, 12)[layer], 2 * USES):
                    rest(layer, None, 1, q)
                    if q == 19:
                        x_mod(1)
                    if q == 21:
                        x_rest(1, 1)
                steps(eng, body)

            eng.wait_ge(rows_t, 1)
            v.tensor_copy(vec[:, :, 0:NROWS], ps[:, 0, 0:KB * 32].rearrange("p (b r) -> p b r", b=KB)[:, :, 0:NROWS]).then_inc(vec_ok, 1)
            eng.wait_ge(vec_ok, 1)
            eng.wait_ge(sig_c, 1)
            v.tensor_tensor(cond[:, :, :], cond[:, :, :], vec[:, :, R_C:R_C + 2], ALU.mult).then_inc(cond_ok, 1)
            lam = vec[:, :, R_LAM:R_LAM + 2]
            step(v.tensor_scalar(spt[:, 0], lam, -1.0, None, ALU.mult))
            v.tensor_tensor(spt[:, 1], spt[:, 0], lam, ALU.max).then_inc(lam_abs, 1)
            step(v.tensor_scalar(spt[:, 2], spt[:, 0], 0.0, 4.0, ALU.max, ALU.mult))
            eng.wait_ge(lam_exp, 1)
            step(v.tensor_scalar(spt[:, 4], spt[:, 3], 2.0, None, ALU.add))
            step(v.reciprocal(spt[:, 4], spt[:, 4]))
            step(v.tensor_tensor(spt[:, 3], spt[:, 3], spt[:, 4], ALU.mult))
            step(v.tensor_tensor(spt[:, 4], spt[:, 3], spt[:, 3], ALU.mult))
            step(v.tensor_scalar(spt[:, 5], spt[:, 4], 1.0 / 17, None, ALU.mult))
            for m in (15, 13, 11, 9, 7, 5, 3):
                step(v.scalar_tensor_tensor(out=spt[:, 5], in0=spt[:, 5], scalar=1.0 / m, in1=spt[:, 4], op0=ALU.add, op1=ALU.mult))
            step(v.scalar_tensor_tensor(out=spt[:, 5], in0=spt[:, 5], scalar=1.0, in1=spt[:, 3], op0=ALU.add, op1=ALU.mult))
            v.scalar_tensor_tensor(out=sp4[:, :, :], in0=spt[:, 5], scalar=8.0, in1=spt[:, 2], op0=ALU.mult, op1=ALU.add).then_inc(sp_ok, 1)
            eng.wait_ge(sp_ok, 1)
            v.tensor_scalar(spn[:, :, :], sp4[:, :, :], -2.0, None, ALU.mult).then_inc(sp_ok, 1)
            eng.wait_ge(x_in, 16)
            norm_sums(0, 0)
            norm_end(0)
            eng.wait_ge(mod_ok, 2)
            v.scalar_tensor_tensor(out=amod[:, 0], in0=mod[:, 0, 1], scalar=1.0, in1=vec[:, :, R_G1:R_G1 + 1].to_broadcast([P, KB, 2]),
                                   op0=ALU.add, op1=ALU.mult).then_inc(amod_ok, 1)
            eng.wait_ge(amod_ok, 1)

            def mixer_rest(b):
                eng.wait_ge(mx_hi_ok, b + 1)
                v.tensor_tensor(mx_lo[:, b, :], mx_raw[:, b % 2, :], mx_hi[:, b, :].bitcast(F32), ALU.subtract).then_inc(mx_lo_ok, 1)

            for b in range(KB):
                eng.wait_ge(tr_mm, 2 * b + 1 + (b + 1) % 2)
                if b >= 2:
                    eng.wait_ge(mx_lo_ok, b - 1)
                src, cols, st = ((ps[:, b % 2, :], slice(0, NLAT), 0) if b % 2 == 1
                                 else (ps[:, 2 + b % 2, 0:P], slice(NLAT, NTOK), 1))
                v.tensor_scalar(mx_raw[:, b % 2, cols], src, amod[:, 0, b, st:st + 1], mod[:, 0, 0, b, st:st + 1],
                                ALU.mult, ALU.add).then_inc(tr_dve, 1)
                if b >= 1:
                    mixer_rest(b - 1)
            mixer_rest(KB - 1)

            def column_rest(n):
                cols = (D if n % 2 == 0 else 0) + n // 2 * P
                eng.wait_ge(wcol_hi_ok, n + 1)
                v.tensor_tensor(wcol[n % 2][:, 1], ring[:, 0:KB, cols:cols + P], wcol[n % 2][:, 0].bitcast(F32),
                                ALU.subtract).then_inc(wcol_lo_ok, 1)

            column_rest(0)

            hg = feat(r2)
            eng.wait_ge(consts, 4)
            for b in range(KB + 1):
                if b < KB:
                    column_rest(2 * b + 1)
                    uc = ucs[b % 2]
                    eng.wait_ge(u_ok, 3 * (b + 1))
                    if b >= 2:
                        eng.wait_ge(z_mm, b - 1)
                        eng.wait_ge(iu_ok, 2 * (b - 1))
                    step(v.tensor_scalar(uc, upad[:, 0:UC], vec[:, b, R_CW:R_CW + 1], vec[:, b, R_CB:R_CB + 1], ALU.mult, ALU.add))
                    for k in range(1, 4):
                        ins = v.scalar_tensor_tensor(out=uc, in0=upad[:, k:k + UC], scalar=vec[:, b, R_CW + k:R_CW + k + 1],
                                                     in1=uc, op0=ALU.mult, op1=ALU.add)
                        if k < 3:
                            step(ins)
                    ins.then_inc(conv_ok, 1)
                if b < KB - 1:
                    column_rest(2 * b + 2)
                if b >= 1:
                    c1 = b - 1
                    aa = aas[c1 % 2]
                    eng.wait_ge(a_ok, 2 * b)
                    eng.wait_ge(sqrt_ok, b)
                    step(v.scalar_tensor_tensor(out=sq, in0=aa, scalar=1.0, in1=sq, op0=ALU.add, op1=ALU.mult))
                    eng.wait_ge(iu_ok, 2 * b)
                    v.tensor_tensor(sq, sq, ig, ALU.mult).then_inc(ig_used, 1)
                    eng.wait_ge(ig_used, b)
                    if b >= 2:
                        eng.wait_ge(st_ok, 2 * c1)
                    v.tensor_tensor_scan(hh[:, 0, 0:NLAT], aa[:, 0, 0:NLAT], sq[:, 0, 0:NLAT],
                                         vec[:, c1, R_H0:R_H0 + 1], ALU.mult, ALU.add).then_inc(scan_ok, 1)
                    v.tensor_tensor_scan(hh[:, 0, NLAT:], aa[:, 0, NLAT:], sq[:, 0, NLAT:], 0.0, ALU.mult, ALU.add).then_inc(scan_ok, 1)
                    v.tensor_tensor_scan(hh[:, 1, 0:NLAT][:, ::-1], aa[:, 1, 0:NLAT][:, ::-1], sq[:, 1, 0:NLAT][:, ::-1],
                                         vec[:, c1, R_H0 + 1:R_H0 + 2], ALU.mult, ALU.add).then_inc(scan_ok, 1)
                    v.tensor_tensor_scan(hh[:, 1, NLAT:][:, ::-1], aa[:, 1, NLAT:][:, ::-1], sq[:, 1, NLAT:][:, ::-1],
                                         0.0, ALU.mult, ALU.add).then_inc(scan_ok, 1)
                    eng.wait_ge(scan_ok, 4 * b)
                    v.tensor_copy(stv[:, 0, c1:b], hh[:, 0, NTOK - 1:NTOK]).then_inc(st_ok, 1)
                    v.tensor_copy(stv[:, 1, c1:b], hh[:, 1, NLAT:NLAT + 1]).then_inc(st_ok, 1)
                    step(v.tensor_tensor(aa[:, 0], hh[:, 0], hh[:, 1], ALU.add))
                    eng.wait_ge(gel_ok, 2 * b)
                    v.tensor_tensor(hg[:, c1, :], aa[:, 0], gels[c1 % 2], ALU.mult).then_inc(hg_ok, 1)
            mixed_rest(0)
            out_weights_rest()
            diagonals(0, diag)
            eng.wait_ge(x_in, 48)
            residual(0, r1, gb)
            eng.wait_ge(st_mm, 1)
            v.tensor_copy(st_row[:, :], ps[0:16, 4, 0:P]).then_inc(st_row_ok, 1)
            turned(1, 0)
            route(0)
            experts(0)

            eng.wait_ge(x_mid_in, 16)
            norm_sums(2, 0)
            norm_end(2)
            turned(2, 1)

            def turned_q(t):
                eng.wait_ge(q_mm, t + 1)
                v.tensor_copy(q_t[:, 4:8, t * P:(t + 1) * P], ps[:, 7, :].rearrange("p (h n) -> p h n", h=4)).then_inc(q_dve, 1)

            qn3, qs3, gn3 = (a.rearrange("p (h n) -> p h n", h=NQK) for a in (qn, qs, gains))
            qn4, qs4 = (a.rearrange("p (h f q n) -> p h f q n", h=NQK, f=2, q=2) for a in (qn, qs))

            def input_rest(t):
                cols = slice(t * P, (t + 1) * P)
                eng.wait_ge(xq_hi_ok, t + 1)
                v.tensor_tensor(mo_lo[1][:, :, cols], feat(r1)[:, :, cols], xq_hi[:, t % 2].bitcast(F32), ALU.subtract).then_inc(xq_lo_ok, 1)

            input_rest(0)
            for k in range(KB):
                eng.wait_ge(wq_hi_ok, 2 * k + 1)
                v.tensor_tensor(wq[:, k, 0:D], ring[:, k, 0:D], wq_hi[:, k, :].bitcast(F32), ALU.subtract).then_inc(wq_lo_ok, 1)
                eng.wait_ge(wq_hi_ok, 2 * k + 2)
                v.tensor_tensor(wq[:, k, D:QKV], ring[:, k, D:QKV], wq[:, k, QKV:QKV + 512].bitcast(F32), ALU.subtract).then_inc(wq_lo_ok, 1)
            eng.wait_ge(gains_ok, 1)
            eng.wait_ge(small_in, 16 * 7)
            for t in range(NT):
                if t < NT - 1:
                    input_rest(t + 1)
                z = 3 * (t % 2)
                eng.wait_ge(qsq_ok, 3 * (t + 1))
                step(v.tensor_reduce(ss20[:, 0], qs3, AX.X, ALU.add))
                v.tensor_scalar(ss20[:, 0], ss20[:, 0], 1.0 / HD, EPS, ALU.mult, ALU.add).then_inc(qvar_ok, 1)
                eng.wait_ge(qstd_ok, t + 1)
                step(v.reciprocal(ss20[:, 1], ss20[:, 1]))
                eng.wait_ge(kdup_ok, 2 * (t + 1))
                if t >= 1:
                    turned_q(t - 1)
                for lo, hi, src in ((0, 8, ps[:, z, :]), (8, 16, ps[:, z + 1, :]), (16, 20, ps[:, z + 2, 0:256])):
                    ins = v.tensor_tensor(qn3[:, lo:hi], src.rearrange("p (h n) -> p h n", n=HD),
                                          ss20[:, 1, lo:hi].unsqueeze(2).to_broadcast([P, hi - lo, HD]), ALU.mult)
                    if hi < NQK:
                        step(ins)
                ins.then_inc(qn_read, 1)
                eng.wait_ge(qn_read, t + 1)
                ins = v.tensor_tensor(qn, qn, gains, ALU.mult)
                if t < TL:
                    step(ins)
                    for q in range(2):
                        v.tensor_tensor(qs4[:, :, :, q, :], qn4[:, :, :, 1 - q, :],
                                        tab[:, 1, t].rearrange("p (f q n) -> p f q n", f=2, q=2)[:, :, q, :].unsqueeze(1)
                                        .to_broadcast([P, NQK, 2, HD // 4]), ALU.mult).then_inc(rot_ok, 1)
                    eng.wait_ge(rot_ok, 2 * (t + 1))
                    step(v.tensor_tensor(qn3, qn3, tab[:, 0, t].unsqueeze(1).to_broadcast([P, NQK, HD]), ALU.mult))
                    ins = v.tensor_tensor(qn, qn, qs, ALU.add)
                ins.then_inc(qn_ok, 1)
            turned_q(NT - 1)
            eng.wait_ge(consts, 6)
            eng.wait_ge(sink_ok, 1)
            eng.wait_ge(kv_stored, 32)
            for i in range(NU + 3):
                if i < NU:
                    j, hp = units[i]
                    w, m0 = len(KEYB[j][0]) * P, KEYB[j][1]
                    st = stat[:, i % 4]
                    eng.wait_ge(s_mm, i + 1)
                    if i >= 2:
                        eng.wait_ge(pt_mm, i - 1)
                    for a in range(2):
                        v.tensor_tensor_reduce(out=pm[:, i % 2, a, 0:w], in0=ps[:, 2 * (i % 2) + a, 0:w],
                                               in1=mask[:, m0:m0 + w], scale=1.0, scalar=NEG, op0=ALU.add, op1=ALU.max,
                                               accum_out=st[:, 0, a:a + 1]).then_inc(s_max, 1)
                    eng.wait_ge(s_max, 2 * (i + 1))
                    step(v.scalar_tensor_tensor(out=st[:, 1, :], in0=st[:, 0, :], scalar=-1.0, in1=sinks[:, 1, 2 * hp:2 * hp + 2],
                                                op0=ALU.mult, op1=ALU.min))
                    v.tensor_tensor(st[:, 2, :], sinks[:, 0, 2 * hp:2 * hp + 2], st[:, 1, :], ALU.add).then_inc(nm_ok, 1)
                if 1 <= i <= NU:
                    w = len(KEYB[units[i - 1][0]][0]) * P
                    eng.wait_ge(pt_mm, i)
                    if i >= 3:
                        eng.wait_ge(pv_mm, i - 2)
                    v.tensor_copy(pt[:, (i - 1) % 2, 1, 0:w], ps[:, 5, 0:w]).then_inc(pt_dve, 1)
                if 2 <= i < NU + 2:
                    j, hp = units[i - 2]
                    st = stat[:, (i - 2) % 4]
                    eng.wait_ge(p_ok, 3 * (i - 1))
                    step(v.tensor_tensor(st[:, 5, :], st[:, 3, :], st[:, 4, :], ALU.add))
                    step(v.reciprocal(st[:, 6, :], st[:, 5, :]))
                    eng.wait_ge(pv_mm, i - 1)
                    if j >= 2:
                        eng.wait_ge(ot_mm, j - 1)
                    v.tensor_tensor(gb[:, j % 2, hp * P:(hp + 1) * P].rearrange("p (a n) -> p a n", a=2),
                                    ps[:, 6 + i % 2, 0:P].rearrange("p (a n) -> p a n", a=2),
                                    st[:, 6, :].unsqueeze(2).to_broadcast([P, 2, HD]), ALU.mult).then_inc(o_ok, 1)
                if last_of_tile(i - 3):
                    j = (i - 3) // KB
                    eng.wait_ge(ot_mm, j + 1)
                    v.tensor_copy(feat(r1)[:, 4:8, j * P:(j + 1) * P], ps[:, 5, :].rearrange("p (h n) -> p h n", h=4)).then_inc(ot_dve, 1)
            mixed_rest(1)
            diagonals(1, diag1)
            residual(1, r2, gb1)
            turned(3, 1, first_rest)
            route(1)
            experts(1)


def rope_table():
    t = np.arange(NLAT)
    inv = (np.float32(10000.0) ** (-np.arange(HD // 4, dtype=np.float32) / (HD // 4))).astype(np.float32)
    ar = (t // 64).astype(np.float32)[:, None] * inv
    ac = (t % 64).astype(np.float32)[:, None] * inv
    ang = np.concatenate([ar, ar, ac, ac], axis=1)
    sign = np.repeat(np.array([-1, 1, -1, 1], np.float32), HD // 4)
    return np.stack([np.cos(ang), np.sin(ang) * sign]).astype(np.float32)


def kernel(x_prompt, x_sample, state_rglru, cache_k, cache_v, c, c_ctx, mod_w, mod_b, norm1_g, norm2_g,
           rg_w_in, rg_conv_w, rg_conv_b, rg_w_a, rg_b_a, rg_w_x, rg_b_x, rg_lambda, rg_w_out,
           at_w_qkv, at_q_norm, at_k_norm, at_sink, at_w_o, ft_w, moe_router, moe_w_gate, moe_w_up, moe_w_down):
    import concourse.bacc as bacc
    from concourse.bass_utils import run_bass_kernel_spmd

    ins = {
        "x_all": np.concatenate([np.asarray(x_sample)[0], np.asarray(x_prompt)[0]]),
        "state": np.asarray(state_rglru).reshape(2, D),
        "cache_k": np.asarray(cache_k).reshape(P, NKV * HD), "cache_v": np.asarray(cache_v).reshape(P, NKV * HD),
        "c": np.asarray(c).reshape(1, D), "c_ctx": np.asarray(c_ctx).reshape(1, D),
        "mod_w": np.asarray(mod_w), "mod_b": np.asarray(mod_b).reshape(2 * NMOD, D),
        "norm1_g": np.asarray(norm1_g), "norm2_g": np.asarray(norm2_g),
        "rg_w_in": np.asarray(rg_w_in)[0], "rg_conv_w": np.asarray(rg_conv_w)[0], "rg_conv_b": np.asarray(rg_conv_b),
        "rg_w_a": np.asarray(rg_w_a)[0], "rg_b_a": np.asarray(rg_b_a)[0],
        "rg_w_x": np.asarray(rg_w_x)[0], "rg_b_x": np.asarray(rg_b_x)[0],
        "rg_lambda": np.asarray(rg_lambda)[0], "rg_w_out": np.asarray(rg_w_out)[0],
        "at_w_qkv": np.asarray(at_w_qkv)[0], "at_q_norm": np.asarray(at_q_norm), "at_k_norm": np.asarray(at_k_norm),
        "at_sink": np.asarray(at_sink), "at_w_o": np.asarray(at_w_o)[0], "moe_router": np.asarray(moe_router),
        "moe_w_gate": np.asarray(moe_w_gate), "moe_w_up": np.asarray(moe_w_up), "moe_w_down": np.asarray(moe_w_down),
        "rope": rope_table(),
    }
    outs = {"y_all": (NTOK, D), "new_state": (2, D), "new_k": (NCTX, NKV * HD), "new_v": (NCTX, NKV * HD)}
    nc = bacc.Bacc("TRN2", target_bir_lowering=False, num_devices=1)
    aps = {k: nc.dram_tensor(f"in_{k}", a.shape, F32, kind="ExternalInput").ap() for k, a in ins.items()}
    aps.update({k: nc.dram_tensor(f"out_{k}", s, F32, kind="ExternalOutput").ap() for k, s in outs.items()})
    build(nc, **aps)
    r = run_bass_kernel_spmd(nc, [{f"in_{k}": np.ascontiguousarray(a) for k, a in ins.items()}], core_ids=[0]).results[0]
    y = r["out_y_all"]
    return (y[NLAT:].reshape(1, NCTX, D), y[:NLAT].reshape(1, NLAT, D), r["out_new_state"].reshape(1, 1, 2, D),
            r["out_new_k"].reshape(1, 1, NCTX, NKV, HD), r["out_new_v"].reshape(1, 1, NCTX, NKV, HD))
```
